# Optimizing a Trainium2 kernel written in Bass

```python
import math
import jax
import jax.numpy as jnp
from jax import lax
import numpy as np

D_MODEL = 1024
BATCH = 1
SEQ = 1024
DEPTH = 2
DEC_BATCH = 8
DEC_SEQ = 1
PAST_LEN = 256
PAGE_SIZE = 128

N_A_LAYERS = DEPTH // 2
N_B_LAYERS = DEPTH - N_A_LAYERS
RWKV_HEAD = 64
RWKV_HEADS = D_MODEL // RWKV_HEAD
DECAY_LORA = 64
AAA_LORA = 64
GATE_LORA = 160
GN_EPS = 64e-5
HEAD_DIM = 64
Q_HEADS = 16
KV_HEADS = 4
REP = Q_HEADS // KV_HEADS
DILATED_GROUPS = ((128, 1), (512, 4), (2048, 16))
N_GROUPS_B = len(DILATED_GROUPS)
WINDOW_MAX = max(w for w, _ in DILATED_GROUPS)
ROT_DIM = HEAD_DIM // 4
ROPE_THETA = 500000.0
Q_BLOCK = 128
N_EXPERTS = 32
N_EXPERT_GROUPS = 4
EXPERTS_PER_GROUP = N_EXPERTS // N_EXPERT_GROUPS
TOP_K = 2
D_EXPERT = 512
DN_ALPHA = (2 * DEPTH) ** 0.25
DN_BETA = (8 * DEPTH) ** -0.25
LN_EPS = 1e-5

kernel_name = 'yoco_rwkv7_dilated_moe_step'

def layer_norm(x, g, b):
    xf = x.astype(jnp.float32)
    mu = xf.mean(-1, keepdims=True)
    var = jnp.square(xf - mu).mean(-1, keepdims=True)
    return ((xf - mu) * lax.rsqrt(var + LN_EPS) * g + b).astype(x.dtype)

def ada_mod(c, w, b, n):
    m = jax.nn.silu(c) @ w + b
    return [t[:, None, :] for t in jnp.split(m, n, axis=-1)]

def partial_rotary(x, pos):
    half = ROT_DIM // 2
    inv = ROPE_THETA ** (-jnp.arange(half, dtype=jnp.float32) * 2.0 / ROT_DIM)
    ang = pos.astype(jnp.float32)[:, None] * inv[None, :]
    shape = (1, ang.shape[0]) + (1,) * (x.ndim - 3) + (half,)
    cos = jnp.cos(ang).reshape(shape)
    sin = jnp.sin(ang).reshape(shape)
    x1 = x[..., :half].astype(jnp.float32)
    x2 = x[..., half:ROT_DIM].astype(jnp.float32)
    rot = jnp.concatenate([x1 * cos - x2 * sin, x2 * cos + x1 * sin], axis=-1).astype(x.dtype)
    return jnp.concatenate([rot, x[..., ROT_DIM:]], axis=-1)

def wkv7_step(S, inp):
    r, w, k, v, a, b = inp
    sa = jnp.einsum('bhij,bhj->bhi', S, a)
    S = S * w[:, :, None, :] + sa[..., None] * b[:, :, None, :] + v[..., None] * k[:, :, None, :]
    return S, jnp.einsum('bhij,bhj->bhi', S, r)

def rwkv7_time_mix(h, shift0, wkv0, mu, w_rkv, w0, w1, w2, a0, a1, a2, g1, g2,
                   k_k, k_a, r_k, lnx_g, lnx_b, w_o):
    B, T, D = h.shape
    H, N = RWKV_HEADS, RWKV_HEAD
    h_prev = jnp.concatenate([shift0[:, None, :].astype(h.dtype), h[:, :-1]], axis=1)
    xx = h_prev - h
    xr, xw, xk, xv, xa, xg = [h + xx * mu[i] for i in range(6)]
    r = xr @ w_rkv[0]
    k = xk @ w_rkv[1]
    v = xv @ w_rkv[2]
    w_log = -jax.nn.softplus(-(w0 + jnp.tanh(xw @ w1) @ w2).astype(jnp.float32)) - 0.5
    decay = jnp.exp(-jnp.exp(w_log))
    a_lr = jax.nn.sigmoid((a0 + (xa @ a1) @ a2).astype(jnp.float32))
    g = jax.nn.sigmoid(xg @ g1) @ g2

    def heads(t):
        return t.astype(jnp.float32).reshape(B, T, H, N)

    kk = heads(k * k_k)
    kk = kk / jnp.maximum(jnp.sqrt(jnp.sum(kk * kk, axis=-1, keepdims=True)), 1e-12)
    k_h = heads(k.astype(jnp.float32) * (1.0 + (a_lr - 1.0) * k_a))
    r_h, v_h, w_h, alr_h = heads(r), heads(v), heads(decay), heads(a_lr)
    seqs = tuple(jnp.moveaxis(t, 1, 0) for t in (r_h, w_h, k_h, v_h, -kk, kk * alr_h))
    S_T, y = lax.scan(wkv7_step, wkv0.astype(jnp.float32), seqs)
    y = jnp.moveaxis(y, 0, 1)
    ym = y.mean(-1, keepdims=True)
    yv = jnp.square(y - ym).mean(-1, keepdims=True)
    y = ((y - ym) * lax.rsqrt(yv + GN_EPS)).reshape(B, T, D) * lnx_g + lnx_b
    bonus = jnp.sum(r_h * k_h * r_k, axis=-1, keepdims=True) * v_h
    y = y + bonus.reshape(B, T, D)
    out = (y * g).astype(h.dtype) @ w_o
    return out, h[:, -1], S_T

def dilated_core(q, k_all, v_all, q_rows):
    scale = HEAD_DIM ** -0.5
    outs, lses = [], []
    for gi, (win, dil) in enumerate(DILATED_GROUPS):
        offs = jnp.arange(win // dil + 1, dtype=jnp.int32) * dil
        idx = q_rows[:, None] - offs[None, :]
        valid = idx >= 0
        idx = jnp.maximum(idx, 0)
        kg = k_all[:, idx].astype(jnp.float32)
        vg = v_all[:, idx].astype(jnp.float32)
        s = jnp.einsum('bqhrd,bqjhd->bqhrj', q[:, :, gi].astype(jnp.float32), kg) * scale
        s = jnp.where(valid[None, :, None, None, :], s, -jnp.inf)
        m = s.max(-1, keepdims=True)
        p = jnp.exp(s - m)
        l = p.sum(-1, keepdims=True)
        outs.append(jnp.einsum('bqhrj,bqjhd->bqhrd', p, vg) / l)
        lses.append(m[..., 0] + jnp.log(l[..., 0]))
    wgt = jax.nn.softmax(jnp.stack(lses), axis=0)
    return jnp.einsum('gbqhr,gbqhrd->bqhrd', wgt, jnp.stack(outs))

def dilated_attention(q, k_all, v_all, q_rows):
    B, T = q.shape[0], q.shape[1]
    if T % Q_BLOCK == 0 and T > Q_BLOCK:
        nb = T // Q_BLOCK
        qb = jnp.moveaxis(q.reshape((B, nb, Q_BLOCK) + q.shape[2:]), 1, 0)
        rows = q_rows.reshape(nb, Q_BLOCK)
        o = lax.map(lambda a: dilated_core(a[0], k_all, v_all, a[1]), (qb, rows))
        return jnp.moveaxis(o, 0, 1).reshape((B, T) + o.shape[3:])
    return dilated_core(q, k_all, v_all, q_rows)

def moe_ffn(h, router_w, router_b, w_in, w_out):
    B, T, D = h.shape
    n = B * T
    xf = h.reshape(n, D)
    aff = jax.nn.sigmoid((xf @ router_w).astype(jnp.float32))
    sel = (aff + router_b.astype(jnp.float32)).reshape(n, N_EXPERT_GROUPS, EXPERTS_PER_GROUP)
    grp = jnp.argmax(lax.top_k(sel, 2)[0].sum(-1), axis=-1)
    in_grp = jnp.take_along_axis(sel, grp[:, None, None], axis=1)[:, 0]
    loc = lax.top_k(in_grp, TOP_K)[1]
    e_idx = (grp[:, None] * EXPERTS_PER_GROUP + loc).astype(jnp.int32)
    gate = jnp.take_along_axis(aff, e_idx, axis=1)
    gate = gate / gate.sum(-1, keepdims=True)
    n_assign = n * TOP_K
    blk = Q_BLOCK if n_assign >= Q_BLOCK * N_EXPERTS else 16
    n_blocks = -(-n_assign // blk) + N_EXPERTS
    flat_e = e_idx.reshape(-1)
    flat_tok = jnp.arange(n_assign, dtype=jnp.int32) // TOP_K
    order = jnp.argsort(flat_e)
    e_sorted = flat_e[order]
    counts = jnp.bincount(flat_e, length=N_EXPERTS)
    padded = (counts + blk - 1) // blk * blk
    pad_end = jnp.cumsum(padded)
    pad_start = pad_end - padded
    start = jnp.cumsum(counts) - counts
    dest = pad_start[e_sorted] + jnp.arange(n_assign, dtype=jnp.int32) - start[e_sorted]
    slot_tok = jnp.full((n_blocks * blk,), n, jnp.int32).at[dest].set(flat_tok[order])
    slot_gate = jnp.zeros((n_blocks * blk,), jnp.float32).at[dest].set(gate.reshape(-1)[order])
    blk_exp = jnp.minimum(jnp.searchsorted(pad_end, jnp.arange(n_blocks, dtype=jnp.int32) * blk,
                                           side='right'), N_EXPERTS - 1)
    x_pad = jnp.concatenate([xf, jnp.zeros((1, D), xf.dtype)], axis=0)

    def expert_block(args):
        tok, e = args
        gt, up = jnp.split(x_pad[tok] @ w_in[e], 2, axis=-1)
        return (jax.nn.silu(gt) * up) @ w_out[e]

    y_slots = lax.map(expert_block, (slot_tok.reshape(n_blocks, blk), blk_exp))
    y_slots = y_slots.reshape(-1, D).astype(jnp.float32) * slot_gate[:, None]
    y = jnp.zeros((n + 1, D), jnp.float32).at[slot_tok].add(y_slots)[:n]
    return y.reshape(B, T, D).astype(h.dtype)

def trunk(x, c, pos, q_rows, wkv0, shift0, k_buf, v_buf, p):
    B, T, D = x.shape
    new_wkv, new_shift = [], []
    k_new = v_new = k_all = v_all = None
    for layer in range(DEPTH):
        sh, sc, gt = ada_mod(c, p['ada_w'][layer, 0], p['ada_b'][layer, 0], 3)
        hm = x * (1 + sc) + sh
        if layer < N_A_LAYERS:
            i = layer
            mix, last_h, S = rwkv7_time_mix(
                hm, shift0[i], wkv0[i], p['rwkv_mu'][i], p['rwkv_w_rkv'][i], p['rwkv_w0'][i],
                p['rwkv_w1'][i], p['rwkv_w2'][i], p['rwkv_a0'][i], p['rwkv_a1'][i], p['rwkv_a2'][i],
                p['rwkv_g1'][i], p['rwkv_g2'][i], p['rwkv_k_k'][i], p['rwkv_k_a'][i], p['rwkv_r_k'][i],
                p['rwkv_lnx_g'][i], p['rwkv_lnx_b'][i], p['rwkv_w_o'][i])
            new_wkv.append(S)
            new_shift.append(last_h)
        else:
            if layer == N_A_LAYERS:
                kv_sh, kv_sc = ada_mod(c, p['kv_ada_w'], p['kv_ada_b'], 2)
                kv = ((x * (1 + kv_sc) + kv_sh) @ p['w_kv']).reshape(B, T, 2, KV_HEADS, HEAD_DIM)
                k_new = partial_rotary(kv[:, :, 0], pos)
                v_new = kv[:, :, 1]
                k_all = jnp.concatenate([k_buf.astype(k_new.dtype), k_new], axis=1)
                v_all = jnp.concatenate([v_buf.astype(v_new.dtype), v_new], axis=1)
            j = layer - N_A_LAYERS
            q = (hm @ p['w_q'][j]).reshape(B, T, N_GROUPS_B, Q_HEADS, HEAD_DIM)
            q = partial_rotary(q, pos).reshape(B, T, N_GROUPS_B, KV_HEADS, REP, HEAD_DIM)
            o = dilated_attention(q, k_all, v_all, q_rows)
            mix = o.reshape(B, T, Q_HEADS * HEAD_DIM).astype(x.dtype) @ p['w_o_attn'][j]
        x = layer_norm(DN_ALPHA * x + gt * mix, p['ln_g'][layer, 0], p['ln_b'][layer, 0])
        sh2, sc2, gt2 = ada_mod(c, p['ada_w'][layer, 1], p['ada_b'][layer, 1], 3)
        ff = moe_ffn(x * (1 + sc2) + sh2, p['router_w'], p['router_b'],
                     p['moe_w_in'][layer], p['moe_w_out'][layer])
        x = layer_norm(DN_ALPHA * x + gt2 * ff, p['ln_g'][layer, 1], p['ln_b'][layer, 1])
    return x, jnp.stack(new_wkv), jnp.stack(new_shift), k_new, v_new

def setup_inputs(seed: int = 0) -> dict:
    key = jax.random.key(seed)
    kit = iter(list(jax.random.split(key, 48)))

    def nrm(shape, s):
        return jax.random.normal(next(kit), shape, jnp.float32) * s

    D = D_MODEL
    NA, NB = N_A_LAYERS, N_B_LAYERS
    wbuf = min(WINDOW_MAX, PAST_LEN)
    inp = {}
    inp['x_prompt'] = nrm((BATCH, SEQ, D), 1.0)
    inp['x_sample'] = nrm((DEC_BATCH, DEC_SEQ, D), 1.0)
    inp['state_wkv'] = nrm((NA, DEC_BATCH, RWKV_HEADS, RWKV_HEAD, RWKV_HEAD), 0.3)
    inp['state_shift'] = nrm((NA, DEC_BATCH, D), 1.0)
    inp['cache_k'] = nrm((DEC_BATCH, wbuf, KV_HEADS, HEAD_DIM), 1.0)
    inp['cache_v'] = nrm((DEC_BATCH, wbuf, KV_HEADS, HEAD_DIM), 1.0)
    inp['c_prompt'] = nrm((BATCH, D), 1.0)
    inp['c_sample'] = nrm((DEC_BATCH, D), 1.0)
    inp['ada_w'] = nrm((DEPTH, 2, D, 3 * D), 0.5 * D ** -0.5)
    inp['ada_b'] = nrm((DEPTH, 2, 3 * D), 0.01)
    inp['ln_g'] = 1.0 + nrm((DEPTH, 2, D), 0.02)
    inp['ln_b'] = nrm((DEPTH, 2, D), 0.02)
    inp['rwkv_mu'] = jax.random.uniform(next(kit), (NA, 6, D), jnp.float32)
    inp['rwkv_w_rkv'] = nrm((NA, 3, D, D), D ** -0.5)
    inp['rwkv_w0'] = -1.5 + nrm((NA, D), 0.5)
    inp['rwkv_w1'] = nrm((NA, D, DECAY_LORA), D ** -0.5)
    inp['rwkv_w2'] = nrm((NA, DECAY_LORA, D), 0.1 * DECAY_LORA ** -0.5)
    inp['rwkv_a0'] = nrm((NA, D), 0.1)
    inp['rwkv_a1'] = nrm((NA, D, AAA_LORA), D ** -0.5)
    inp['rwkv_a2'] = nrm((NA, AAA_LORA, D), 0.1 * AAA_LORA ** -0.5)
    inp['rwkv_g1'] = nrm((NA, D, GATE_LORA), D ** -0.5)
    inp['rwkv_g2'] = nrm((NA, GATE_LORA, D), GATE_LORA ** -0.5)
    inp['rwkv_k_k'] = 0.85 + nrm((NA, D), 0.02)
    inp['rwkv_k_a'] = 1.0 + nrm((NA, D), 0.02)
    inp['rwkv_r_k'] = nrm((NA, RWKV_HEADS, RWKV_HEAD), 0.1)
    inp['rwkv_lnx_g'] = 1.0 + nrm((NA, D), 0.02)
    inp['rwkv_lnx_b'] = nrm((NA, D), 0.02)
    inp['rwkv_w_o'] = nrm((NA, D, D), DN_BETA * D ** -0.5)
    inp['w_q'] = nrm((NB, D, N_GROUPS_B * Q_HEADS * HEAD_DIM), D ** -0.5)
    inp['w_kv'] = nrm((D, 2 * KV_HEADS * HEAD_DIM), D ** -0.5)
    inp['kv_ada_w'] = nrm((D, 2 * D), 0.5 * D ** -0.5)
    inp['kv_ada_b'] = nrm((2 * D,), 0.01)
    inp['w_o_attn'] = nrm((NB, Q_HEADS * HEAD_DIM, D), DN_BETA * (Q_HEADS * HEAD_DIM) ** -0.5)
    inp['router_w'] = nrm((D, N_EXPERTS), D ** -0.5)
    inp['router_b'] = nrm((N_EXPERTS,), 0.01)
    inp['moe_w_in'] = nrm((DEPTH, N_EXPERTS, D, 2 * D_EXPERT), D ** -0.5)
    inp['moe_w_out'] = nrm((DEPTH, N_EXPERTS, D_EXPERT, D), DN_BETA * D_EXPERT ** -0.5)
    return inp

def reference(x_prompt, x_sample, state_wkv, state_shift, cache_k, cache_v, c_prompt, c_sample,
              ada_w, ada_b, ln_g, ln_b, rwkv_mu, rwkv_w_rkv, rwkv_w0, rwkv_w1, rwkv_w2,
              rwkv_a0, rwkv_a1, rwkv_a2, rwkv_g1, rwkv_g2, rwkv_k_k, rwkv_k_a, rwkv_r_k,
              rwkv_lnx_g, rwkv_lnx_b, rwkv_w_o, w_q, w_kv, kv_ada_w, kv_ada_b, w_o_attn,
              router_w, router_b, moe_w_in, moe_w_out):
    p = {'ada_w': ada_w, 'ada_b': ada_b, 'ln_g': ln_g, 'ln_b': ln_b,
         'rwkv_mu': rwkv_mu, 'rwkv_w_rkv': rwkv_w_rkv, 'rwkv_w0': rwkv_w0, 'rwkv_w1': rwkv_w1,
         'rwkv_w2': rwkv_w2, 'rwkv_a0': rwkv_a0, 'rwkv_a1': rwkv_a1, 'rwkv_a2': rwkv_a2,
         'rwkv_g1': rwkv_g1, 'rwkv_g2': rwkv_g2, 'rwkv_k_k': rwkv_k_k, 'rwkv_k_a': rwkv_k_a,
         'rwkv_r_k': rwkv_r_k, 'rwkv_lnx_g': rwkv_lnx_g, 'rwkv_lnx_b': rwkv_lnx_b,
         'rwkv_w_o': rwkv_w_o, 'w_q': w_q, 'w_kv': w_kv, 'kv_ada_w': kv_ada_w,
         'kv_ada_b': kv_ada_b, 'w_o_attn': w_o_attn, 'router_w': router_w,
         'router_b': router_b, 'moe_w_in': moe_w_in, 'moe_w_out': moe_w_out}
    bp, tp = x_prompt.shape[0], x_prompt.shape[1]
    pos_p = jnp.arange(tp, dtype=jnp.int32)
    wkv_zero = jnp.zeros((N_A_LAYERS, bp, RWKV_HEADS, RWKV_HEAD, RWKV_HEAD), jnp.float32)
    shift_zero = jnp.zeros((N_A_LAYERS, bp, D_MODEL), x_prompt.dtype)
    kv_empty = jnp.zeros((bp, 0, KV_HEADS, HEAD_DIM), x_prompt.dtype)
    y_prompt, wkv_p, shift_p, k_p, v_p = trunk(x_prompt, c_prompt, pos_p, pos_p, wkv_zero,
                                               shift_zero, kv_empty, kv_empty, p)
    keep = min(WINDOW_MAX, tp)
    k_p = k_p[:, tp - keep:]
    v_p = v_p[:, tp - keep:]
    ts = x_sample.shape[1]
    wbuf = cache_k.shape[1]
    pos_s = PAST_LEN + jnp.arange(ts, dtype=jnp.int32)
    rows_s = wbuf + jnp.arange(ts, dtype=jnp.int32)
    y_sample, wkv_s, shift_s, k_s, v_s = trunk(x_sample, c_sample, pos_s, rows_s, state_wkv,
                                               state_shift, cache_k, cache_v, p)
    return (y_prompt, y_sample, wkv_p, shift_p, k_p, v_p, wkv_s, shift_s, k_s, v_s)


_drawn_inputs = setup_inputs


def setup_inputs(seed=0):
    import zlib

    import numpy as np

    out = dict(_drawn_inputs(seed))
    spreads = {}
    factors = {'cache_k': 5.46,
     'cache_v': 4.311,
     'rwkv_w1': 3.684,
     'rwkv_w2': 3.623,
     'rwkv_k_k': 138.18,
     'rwkv_lnx_g': 28.368,
     'rwkv_lnx_b': 29.589,
     'w_q': 3.716,
     'kv_ada_b': 4.356,
     'rwkv_r_k': 4.151}
    for name, (base, spread) in spreads.items():
        noise = np.random.default_rng([zlib.crc32(name.encode()), seed]).standard_normal(out[name].shape)
        drawn = base * np.exp(spread * noise) if base else spread * noise
        out[name] = jnp.asarray(drawn.astype(out[name].dtype))
    for name, factor in factors.items():
        out[name] = (out[name] * factor).astype(out[name].dtype)
    return out
```

```python
from contextlib import ExitStack

import numpy as np

import concourse.bass as bass
from concourse import mybir

F32 = mybir.dt.float32
I32 = mybir.dt.int32
U32 = mybir.dt.uint32
ALU = mybir.AluOpType
ACT = mybir.ActivationFunctionType
AX = mybir.AxisListType.X
ds = bass.ds

P = 128
D = 1024
KC = D // P
NP = 1024
NS = 8
NT = NP + NS
TILES = NP // P
NC = NS + 1
SL = 344
H, HD = 16, 64
CH = 64
GN_EPS = 64e-5
LN_EPS = 1e-5
ALPHA = 4.0 ** 0.25
assert 3 * SL == NT


class Pool_:

    def __init__(self, nc, tag):
        self.nc, self.tag, self.ctx, self.sems = nc, tag, ExitStack(), []

    def __enter__(self):
        self.ctx.__enter__()
        return self

    def __exit__(self, *a):
        self.nc.clear_and_free_semaphores(self.sems)
        self.nc.all_engine_barrier()
        return self.ctx.__exit__(*a)

    def sb(self, name, shape, dt=F32):
        return self.ctx.enter_context(self.nc.sbuf_tensor(f"{self.tag}_{name}", shape, dt))

    def ps(self, name, shape, dt=F32):
        return self.ctx.enter_context(self.nc.psum_tensor(f"{self.tag}_{name}", shape, dt))

    def sem(self, name):
        self.sems.append(self.nc.alloc_semaphore(f"{self.tag}_{name}"))
        return self.sems[-1]


class Chain:

    def __init__(self, eng, sem):
        self.eng, self.sem, self.base, self.n = eng, sem, 0, 0

    def __call__(self, ins):
        ins.then_inc(self.sem, 1)
        self.n += 1
        self.eng.wait_ge(self.sem, self.base + self.n)


def phase_ada(nc, T):
    SLOTS = 6
    with Pool_(nc, "ada") as A:
        ident = A.sb("ident", [P, P])
        c9 = A.sb("c9", [NC, D])
        sg = A.sb("sg", [NC, D])
        cT = A.sb("cT", [P, KC, NC])
        w = A.sb("w", [P, SLOTS, KC, 512])
        bias = A.sb("bias", [NC, 3 * D])
        row = A.sb("row", [NC, 3 * D])
        ps_c = A.ps("ps_c", [P, KC, 16])
        ps_o = A.ps("ps_o", [NC, SLOTS, 512])
        s_c = A.sem("c_loaded")
        s_sig = A.sem("sigmoid_done")
        s_silu = A.sem("silu_done")
        s_tr = A.sem("c_transposed")
        s_cT = A.sem("cT_ready")
        s_w = [A.sem(f"w_loaded{j}") for j in range(SLOTS)]
        s_mm = A.sem("slice_multiplied")
        s_ev = A.sem("banks_free")
        s_bias = A.sem("bias_loaded")
        s_one = A.sem("bias_plus_one")
        s_out = A.sem("rows_stored")
        wv = T["ada_w"].rearrange("l s (k p) n -> (l s) p k n", p=P)
        bv = T["ada_b"].rearrange("l s n -> (l s) n")
        kvw = T["kv_ada_w"].rearrange("(k p) n -> p k n", p=P)
        NM = 4
        with nc.Block() as block:

            @block.sync
            def _(sp):
                sp.dma_start(c9[0:NS, :], T["c_sample"]).then_inc(s_c, 16)
                sp.dma_start(c9[NS:NC, :], T["c_prompt"]).then_inc(s_c, 16)
                sp.dma_start(ident[:], T["k_ident"]).then_inc(s_c, 16)
                for j in range(SLOTS):
                    sp.dma_start(w[:, j], wv[0, :, :, j * 512:(j + 1) * 512]).then_inc(s_w[j], 16)
                with sp.Fori(0, NM - 1) as m:
                    for j in range(SLOTS):
                        sp.wait_ge(s_mm, m * SLOTS + (j + 1))
                        sp.dma_start(w[:, j], wv[ds(m + 1, 1), :, :, j * 512:(j + 1) * 512]
                                     .rearrange("o p k n -> (o p) k n")).then_inc(s_w[j], 16)
                for j in range(4):
                    sp.wait_ge(s_mm, (NM - 1) * SLOTS + j + 1)
                    sp.dma_start(w[:, j], kvw[:, :, j * 512:(j + 1) * 512]).then_inc(s_w[j], 16)

            @block.scalar
            def _(act):
                act.wait_ge(s_c, 48)
                act.activation(sg[:], c9[:], ACT.Sigmoid).then_inc(s_sig, 1)
                act.dma_start(bias[:], bv[0:1, :].broadcast_to([NC, 3 * D])).then_inc(s_bias, 16)
                with act.Fori(0, NM - 1) as m:
                    act.wait_ge(s_ev, m * SLOTS + 2 * SLOTS)
                    act.dma_start(T["ada_d"][ds(m, 1)].rearrange("o a n -> (o a) n"), row[:]).then_inc(s_out, 16)
                    act.dma_start(bias[:], bv[ds(m + 1, 1), :].broadcast_to([NC, 3 * D])).then_inc(s_bias, 16)
                act.wait_ge(s_ev, (NM + 1) * SLOTS)
                act.dma_start(T["ada_d"][NM - 1], row[:]).then_inc(s_out, 16)
                act.dma_start(bias[:, 0:2 * D], T["kv_ada_b"].broadcast_to([NC, 2 * D])).then_inc(s_bias, 16)
                act.wait_ge(s_ev, (NM + 1) * SLOTS + 4)
                act.dma_start(T["kva_d"], row[:, 0:2 * D]).then_inc(s_out, 16)
                act.wait_ge(s_out, 16 * (NM + 1))

            @block.vector
            def _(dve):
                dve.wait_ge(s_sig, 1)
                dve.tensor_tensor(sg[:], sg[:], c9[:], ALU.mult).then_inc(s_silu, 1)
                dve.wait_ge(s_tr, 1)
                dve.tensor_copy(cT[:], ps_c[:, :, 0:NC]).then_inc(s_cT, 1)
                dve.sem_inc(s_ev, SLOTS)

                def slices(m, n):
                    dve.wait_ge(s_bias, m * 16 + 16)
                    dve.tensor_scalar(bias[:, D:2 * D], bias[:, D:2 * D], 1.0, None, ALU.add).then_inc(s_one, 1)
                    for j in range(n):
                        dve.wait_ge(s_mm, m * SLOTS + (j + 1))
                        if j == 0:
                            if not isinstance(m, int) or m:
                                dve.wait_ge(s_out, m * 16)
                            dve.wait_ge(s_one, m + 1)
                        c = slice(j * 512, (j + 1) * 512)
                        ins = dve.tensor_tensor(row[:, c], ps_o[:, j], bias[:, c], ALU.add)
                        ins.then_inc(s_ev, 1)

                slices(0, SLOTS)
                with dve.Fori(1, NM) as m:
                    slices(m, SLOTS)
                slices(NM, 4)

            @block.tensor
            def _(pe):
                pe.wait_ge(s_silu, 1)
                pe.wait_ge(s_c, 48)
                for k in range(KC):
                    ins = pe.transpose(ps_c[:, k, 0:NC], sg[:, k * P:(k + 1) * P], ident[0:NC, 0:NC])
                ins.then_inc(s_tr, 1)
                pe.wait_ge(s_cT, 1)

                def slices(m, n):
                    for j in range(n):
                        pe.wait_ge(s_w[j], m * 16 + 16)
                        pe.wait_ge(s_ev, m * SLOTS + (j + 1))
                        for k in range(KC):
                            ins = pe.matmul(ps_o[:, j], cT[:, k, :], w[:, j, k, :], start=(k == 0), stop=(k == KC - 1))
                        ins.then_inc(s_mm, 1)

                with pe.Fori(0, NM) as m:
                    slices(m, SLOTS)
                slices(NM, 4)


def phase_mix(nc, T):
    with Pool_(nc, "mix") as A:
        ident = A.sb("ident", [P, P])
        ada = A.sb("ada", [NC, 2 * D])
        mod = A.sb("mod", [P, 2, KC, NC])
        hT = A.sb("hT", [P, KC, 1 + NT])
        xx = A.sb("xx", [P, KC, NT])
        mix = A.sb("mix", [P, 2, KC, NT])
        x = mix[:, :, :, :].rearrange("p a k n -> p (a k n)")[:, 0:TILES * D].rearrange("p (t n) -> p t n", t=TILES)
        xs = A.sb("xs", [NS, D])
        sh0 = A.sb("sh0", [NS, D])
        mu = A.sb("mu", [P, 6, KC])
        wr = A.sb("wr", [P, 4, KC, P])
        w1 = A.sb("w1", [P, KC, 160])
        w2 = A.sb("w2", [P, D])
        g2b = A.sb("g2b", [32, D])
        hid = A.sb("hid", [P, NT])
        hid2 = A.sb("hid2", [32, NT])
        ev = A.sb("ev", [P, 2, NT])
        ps = [A.ps(f"ps{i}", [P, 3, 512]) for i in range(2)]
        pm = A.ps("pm", [P, 2, 512])
        s_ld = A.sem("small_loaded")
        s_x = A.sem("x_loaded")
        s_mt = A.sem("mod_transposed")
        s_m = A.sem("mod_ready")
        s_z = A.sem("dve_chain")
        s_xt = A.sem("x_transposed")
        s_h = A.sem("h_half_ready")
        s_xx = A.sem("xx_ready")
        s_sh = A.sem("shift_ready")
        s_mx = A.sem("mix_ready")
        s_wr = [A.sem(f"wr_loaded{i}") for i in range(4)]
        s_w1 = A.sem("w1_loaded")
        s_w2 = A.sem("w2_loaded")
        s_g = A.sem("group_done")
        s_e = A.sem("group_evacuated")
        s_evf = [A.sem(f"ev_stored{i}") for i in range(2)]
        s_st = A.sem("shift_stored")
        with nc.Block() as block:
            wv = T["rwkv_w_rkv"].rearrange("a m (k p) n -> (a m) p k n", p=P)

            G_R = 0
            G_W = 24
            G_A = G_W + 9
            G_G = G_A + 9
            G_END = G_G + 10
            LORA = [(G_W, "rwkv_w1", "rwkv_w2", 64, ACT.Tanh, 3), (G_A, "rwkv_a1", "rwkv_a2", 64, ACT.Copy, 4),
                    (G_G, "rwkv_g1", "rwkv_g2", 160, ACT.Sigmoid, 5)]

            @block.sync
            def _(sp):
                sp.dma_start(ident[:], T["k_ident"]).then_inc(s_ld, 16)
                sp.dma_start(ada[:], T["ada_d"][0, :, 0:2 * D]).then_inc(s_ld, 16)
                sp.dma_start(xs[:], T["x_sample"]).then_inc(s_ld, 16)
                sp.dma_start(sh0[:], T["state_shift"]).then_inc(s_ld, 16)
                sp.dma_start(mu[:], T["mu_c"]).then_inc(s_ld, 16)
                sp.dma_start(x, T["x_prompt"].rearrange("(t p) n -> p t n", p=P)).then_inc(s_x, 16)
                for j in range(4):
                    sp.dma_start(wr[:, j], wv[0, :, :, j * P:(j + 1) * P]).then_inc(s_wr[j], 16)
                for f in range(1, 6):
                    for j in range(4):
                        sp.wait_ge(s_g, 4 * (f - 1) + j + 1)
                        o = (f % 2) * 4 + j
                        sp.dma_start(wr[:, j], wv[f // 2, :, :, o * P:(o + 1) * P]).then_inc(s_wr[j], 16)
                for n, (g0, a1, a2, wid, _, _) in enumerate(LORA):
                    if n:
                        sp.wait_ge(s_g, g0)
                    sp.dma_start(w1[:, :, 0:wid], T[a1].rearrange("(k p) n -> p k n", p=P)).then_inc(s_w1, 16)
                    sp.dma_start(w2[0:min(wid, P), :], T[a2][0:min(wid, P), :]).then_inc(s_w2, 16)
                    if wid > P:
                        sp.dma_start(g2b[:], T[a2][P:wid, :]).then_inc(s_w2, 16)

            def outputs():
                for m in range(3):
                    for o in range(KC):
                        yield G_R + 8 * m + o, m, o
                for g0, first, m in ((G_W, 1, 3), (G_A, 1, 4), (G_G, 2, 5)):
                    for o in range(KC):
                        yield g0 + first + o, m, o

            @block.gpsimd
            def _(pool):
                for n, (g, m, o) in enumerate(outputs()):
                    pool.wait_ge(s_e, g + 1 + 2)
                    pool.dma_start(T["proj_d"][m, o * P:(o + 1) * P, :], ev[:, n % 2]).then_inc(s_evf[n % 2], 16)
                pool.wait_ge(s_sh, 1)
                pool.dma_start(T["shift_prompt"].rearrange("(k p) -> p k", p=P), hT[:, :, NP],
                               allow_slow_non_contiguous=True).then_inc(s_st, 16)
                pool.dma_start(T["shift_sample"], xs[:]).then_inc(s_st, 16)
                pool.wait_ge(s_st, 32)
                pool.wait_ge(s_evf[0], 16 * 24)
                pool.wait_ge(s_evf[1], 16 * 24)

            @block.vector
            def _(dve):
                link = Chain(dve, s_z)
                link(dve.memset(hT[:, :, 0:1], 0.0))
                dve.wait_ge(s_mt, 1)
                dve.tensor_copy(mod[:].rearrange("p a k c -> p (a k) c"),
                                pm[:, 0, 0:2 * KC * 16].rearrange("p (a c) -> p a c", c=16)[:, :, 0:NC]).then_inc(s_m, 1)
                dve.wait_ge(s_m, 1)
                for u in range(2 * KC):
                    k, half = divmod(u, 2)
                    dve.wait_ge(s_xt, u + 1)
                    dve.tensor_scalar(hT[:, k, 1 + half * 512:1 + half * 512 + 512], ps[u % 2][:, 0, :],
                                      mod[:, 1, k, NS:NC], mod[:, 0, k, NS:NC], ALU.mult, ALU.add).then_inc(s_h, 1)
                dve.wait_ge(s_xt, 2 * KC + 1)
                hs = hT[:, :, 1 + NP:1 + NT]
                v = pm[:, 0, 0:KC * NS].rearrange("p (k s) -> p k s", s=NS)
                link(dve.tensor_tensor(hs, v, mod[:, 1, :, 0:NS], ALU.mult))
                link(dve.tensor_tensor(hs, hs, mod[:, 0, :, 0:NS], ALU.add))
                dve.tensor_tensor(xx[:, :, NP:NT], pm[:, 1, 0:KC * NS].rearrange("p (k s) -> p k s", s=NS), hs,
                                  ALU.subtract).then_inc(s_xx, 1)
                dve.wait_ge(s_h, 2 * KC)
                for k in range(KC):
                    dve.tensor_tensor(xx[:, k, 0:NP], hT[:, k, 0:NP], hT[:, k, 1:1 + NP], ALU.subtract).then_inc(s_xx, 1)
                link(dve.tensor_tensor(xs[:], xs[:], ada[0:NS, D:2 * D], ALU.mult))
                dve.tensor_tensor(xs[:], xs[:], ada[0:NS, 0:D], ALU.add).then_inc(s_sh, 1)
                dve.wait_ge(s_xx, KC + 1)
                for m, row in enumerate((0, 2, 3, 1, 4, 5)):
                    if m >= 2:
                        dve.wait_ge(s_g, (8, 16, 24, G_W + 1)[m - 2])
                    for k in range(KC):
                        dve.scalar_tensor_tensor(out=mix[:, m % 2, k, :], in0=xx[:, k, :], scalar=mu[:, row, k:k + 1],
                                                 in1=hT[:, k, 1:1 + NT], op0=ALU.mult, op1=ALU.add).then_inc(s_mx, 1)

            @block.tensor
            def _(pe):
                pe.wait_ge(s_ld, 80)
                for a in range(2):
                    for k in range(KC):
                        o = (a * KC + k) * 16
                        ins = pe.transpose(pm[:, 0, o:o + NC], ada[:, a * D + k * P:a * D + (k + 1) * P], ident[0:NC, 0:NC])
                ins.then_inc(s_mt, 1)
                pe.wait_ge(s_x, 16)
                for u in range(2 * KC):
                    k, half = divmod(u, 2)
                    if u >= 2:
                        pe.wait_ge(s_h, u - 1)
                    for t in range(4):
                        ins = pe.transpose(ps[u % 2][:, 0, t * P:(t + 1) * P], x[:, 4 * half + t, k * P:(k + 1) * P], ident[:])
                    ins.then_inc(s_xt, 1)
                pe.wait_ge(s_m, 1)
                for k in range(KC):
                    pe.transpose(pm[:, 0, k * NS:(k + 1) * NS], xs[:, k * P:(k + 1) * P], ident[0:NS, 0:NS])
                    ins = pe.transpose(pm[:, 1, k * NS:(k + 1) * NS], sh0[:, k * P:(k + 1) * P], ident[0:NS, 0:NS])
                ins.then_inc(s_xt, 1)
                pe.wait_ge(s_h, 2 * KC)

                def group(g, parts, rows=P):
                    pe.wait_ge(s_e, g + 1)
                    for i, (lhsT, rhs) in enumerate(parts):
                        for s in range(3):
                            ins = pe.matmul(ps[g % 2][0:rows, s, 0:SL], lhsT, rhs[:, s * SL:(s + 1) * SL],
                                            start=(i == 0), stop=(i == len(parts) - 1))
                    ins.then_inc(s_g, 1)
                    return ins

                for m in range(3):
                    pe.wait_ge(s_mx, KC * (m + 1))
                    for o in range(KC):
                        n = m * KC + o
                        pe.wait_ge(s_wr[n % 4], 16 * (n // 4 + 1))
                        group(n, [(wr[:, n % 4, k, :], mix[:, m % 2, k, :]) for k in range(KC)])
                for n, (g0, _, _, wid, _, m) in enumerate(LORA):
                    pe.wait_ge(s_mx, KC * (m + 1))
                    pe.wait_ge(s_w1, 16 * (n + 1))
                    g = g0
                    for lo in range(0, wid, P):
                        hi = min(wid, lo + P)
                        group(g, [(w1[:, k, lo:hi], mix[:, m % 2, k, :]) for k in range(KC)], rows=hi - lo)
                        g += 1
                    pe.wait_ge(s_w2, 16 * (n + 1) + 16 * (wid > P))
                    pe.wait_ge(s_e, g + 2)
                    r = min(wid, P)
                    for o in range(KC):
                        c = slice(o * P, (o + 1) * P)
                        parts = [(w2[0:r, c], hid[0:r, :])]
                        if wid > P:
                            parts.append((g2b[:, c], hid2[:]))
                        group(g + o, parts)

            @block.scalar
            def _(act):
                act.sem_inc(s_e, 2)
                stored = {g: n for n, (g, _, _) in enumerate(outputs())}
                funcs = {G_W: (ACT.Tanh, hid, 64), G_A: (ACT.Copy, hid, 64), G_G: (ACT.Sigmoid, hid, P),
                         G_G + 1: (ACT.Sigmoid, hid2, 32)}
                for g in range(G_END):
                    act.wait_ge(s_g, g + 1)
                    if g in stored:
                        n = stored[g]
                        if n >= 2:
                            act.wait_ge(s_evf[n % 2], 16 * (n // 2))
                        dst, rows, f = ev[:, n % 2], P, ACT.Copy
                    else:
                        f, dst, rows = funcs[g]
                        dst = dst[0:rows, :]
                    act.activation(dst.rearrange("p (s n) -> p s n", s=3), ps[g % 2][0:rows, :, 0:SL], f).then_inc(s_e, 1)


EXP_HALF = float(np.exp(-0.5))
LEVELS = 5


class Steps:

    def __init__(self, sem, names):
        self.sem, self.names, self.at = sem, list(names), {n: i for i, n in enumerate(names)}
        assert len(self.at) == len(self.names)
        self.n = 0

    def open(self, eng):
        eng.sem_inc(self.sem, len(self.names))

    def step(self, name, ins):
        assert self.names[self.n] == name, (self.names[self.n], name)
        self.n = (self.n + 1) % len(self.names)
        ins.then_inc(self.sem, 1)

    def skip(self, eng, name, i):
        assert self.names[self.n] == name, (self.names[self.n], name)
        eng.wait_ge(self.sem, self.count(name, i) - 1)
        eng.sem_inc(self.sem, 1)
        self.n = (self.n + 1) % len(self.names)

    def count(self, name, i):
        return i * len(self.names) + (len(self.names) + self.at[name] + 1)

    def before(self, name, i):
        return i * len(self.names) + (self.at[name] + 1)

    def wait(self, eng, name, i, apart=None):
        wait_at(eng, self.sem, self.count(name, i), apart)

    def wait_before(self, eng, name, i, apart=None):
        wait_at(eng, self.sem, self.before(name, i), apart)


def wait_at(eng, sem, value, apart=None):
    if isinstance(value, int) and value <= 0:
        return
    eng.wait_ge(sem, value)
    if apart is not None:
        eng.sem_inc(apart, 1)


def phase_wkv(nc, T):
    UN = 16
    with Pool_(nc, "wkv") as A:
        ident = A.sb("ident", [P, P])
        bones = A.sb("bones", [P, P])
        maskg = A.sb("maskg", [P, 2, P])
        mask1 = A.sb("mask1", [P, P])
        mask1t = A.sb("mask1t", [P, P])
        mlev = A.sb("mlev", [P, LEVELS, P])
        seg = A.sb("seg", [P, NT])
        par = A.sb("par", [P, 5])
        raw = A.sb("raw", [P, 5, NT])
        R, K, V, W, L = (raw[:, i, :] for i in range(5))
        SQ = A.sb("SQ", [P, NT])
        RN = A.sb("RN", [P, NT])
        KK = A.sb("KK", [P, NT])
        KH = A.sb("KH", [P, NT])
        C = A.sb("C", [P, NT])
        E0 = A.sb("E0", [P, NT])
        E1 = A.sb("E1", [P, NT])
        EI = A.sb("EI", [P, NT])
        AR = A.sb("AR", [P, 2, NT])
        BN = A.sb("BN", [P, NT])
        BH = A.sb("BH", [P, NT])
        KHH = A.sb("KHH", [P, NT])
        RK = A.sb("RK", [P, NT])
        tok = A.sb("tok", [P, 4, TILES, P])
        SS = A.sb("SS", [NS, 6, P])
        GB = A.sb("GB", [P, UN, 2, P])
        GK = A.sb("GK", [P, UN, 2, P])
        TB = A.sb("TB", [P, 4, 2, 4, P])
        XB = A.sb("XB", [P, 4, 4, P])
        X0 = A.sb("X0", [P, 4, 4, HD])
        Q = A.sb("Q", [P, UN, HD])
        PT = A.sb("PT", [P, TILES, P])
        UB = A.sb("UB", [P, 2, 2, HD])
        ST = A.sb("ST", [P, 4, HD])
        SW = A.sb("SW", [P, 2, HD])
        Y = A.sb("Y", [P, NP])
        SO = A.sb("SO", [HD, P])
        ps = A.ps("ps", [P, 8, 512])
        s_nil = A.sem("waits_apart")
        s_k = A.sem("constants_loaded")
        s_raw = A.sem("raw_loaded")
        s_bo = A.sem("bonus_stored")
        s_y = A.sem("y_stored")
        s_so = A.sem("state_stored")
        s_ss = A.sem("sample_vectors_stored")

        tr = [(a, h) for a in range(4) for h in range(2)]
        order = []
        for l in range(LEVELS):
            order += [("X", l, 0), ("X", l, 1), ("T", l, 0), ("X", l, 2), ("T", l, 1), ("X", l, 3), ("T", l, 2), ("T", l, 3)]
        NAMES_PE = ["n2", "bonus", "smp"] + [f"tr{a}{h}" for a, h in tr]
        for g in range(4):
            NAMES_PE += [f"gb{g}", f"gk{g}", f"ga{g}"]
        NAMES_PE += [f"{k}{l}{g}" for k, l, g in order]
        for g in range(4):
            NAMES_PE += [f"z{g}", f"pt{g}", f"q{g}"]
        for n in range(16):
            NAMES_PE += [f"u{n}", f"s{n}"]
            if n % 2:
                NAMES_PE += [f"y{n // 2}"]
        NAMES_PE += ["fin"]
        NAMES_DVE = ["zero", "kkr", "rmax", "rinv", "kk", "logw", "scan", "kh", "rt", "bn", "bh", "khh", "at", "bo"]
        for g in range(4):
            NAMES_DVE += [f"gb{g}", f"gk{g}", f"ga{g}"]
        NAMES_DVE += [f"{k}{l}{g}" for k, l, g in order]
        NAMES_DVE += [f"pt{g}" for g in range(4)]
        for n in range(16):
            NAMES_DVE += [f"u{n}", f"s{n}"]
        NAMES_ACT = ["sgw", "alr", "sq", "n2", "e1", "ei", "e0", "smp"] + [f"tr{a}{h}" for a, h in tr]
        for g in range(4):
            NAMES_ACT += [f"z{g}", f"q{g}"]
        for n in range(16):
            NAMES_ACT += [f"sw{n}"]
            if n % 2:
                NAMES_ACT += [f"y{n // 2}"]
        NAMES_ACT += ["fin"]
        NAMES_POOL = ["t1", "cm", "rr", "rk"]
        for g in range(4):
            NAMES_POOL += [f"ti{g}", f"tm{g}", f"tt{g}"]
        pe_ = Steps(A.sem("pe_steps"), NAMES_PE)
        dv_ = Steps(A.sem("dve_steps"), NAMES_DVE)
        ac_ = Steps(A.sem("act_steps"), NAMES_ACT)
        po_ = Steps(A.sem("pool_steps"), NAMES_POOL)
        NCH = KC

        def unit(g, u):
            return 2 * g + u % 2, u // 2

        def uid(t, h):
            return 4 * (t // 2) + 2 * h + t % 2

        with nc.Block() as block:

            @block.sync
            def _(sp):
                for dst, src in ((ident, "k_ident"), (bones, "k_bones"), (maskg, "k_maskg"), (mask1, "k_mask1"),
                                 (mask1t, "k_mask1t"), (mlev, "k_mlev")):
                    sp.dma_start(dst[:], T[src]).then_inc(s_k, 16)
                sp.dma_start(seg[:], T["k_seg"].broadcast_to([P, NT])).then_inc(s_k, 16)
                for s in (s_bo, s_y, s_so, s_ss):
                    sp.sem_inc(s, 16)
                with sp.Fori(0, NCH) as c:
                    dv_.wait_before(sp, "bo", c)
                    pe_.wait_before(sp, "tr31", c)
                    po_.wait_before(sp, "rk", c)
                    ac_.wait_before(sp, "e0", c, apart=s_nil)
                    for i in range(5):
                        sp.dma_start(raw[:, i, :], T["proj_d"][i, ds(c * P, P), :]).then_inc(s_raw, 16)
                    sp.dma_start(par[:], T["wkv_par"][ds(c, 1)].rearrange("o p n -> (o p) n")).then_inc(s_raw, 16)
                    dv_.wait(sp, "bo", c, apart=s_nil)
                    sp.dma_start(T["bonus_d"][ds(c * P, P), :], RK[:]).then_inc(s_bo, 16)
                    ac_.wait(sp, "smp", c, apart=s_nil)
                    sp.dma_start(T["sv_d"][:, :, ds(c * P, P)].rearrange("a s n -> s a n"), SS[:]).then_inc(s_ss, 16)
                    ac_.wait(sp, "y7", c, apart=s_nil)
                    sp.dma_start(T["y_d"][ds(c * P, P), 0:NP], Y[:]).then_inc(s_y, 16)
                    ac_.wait(sp, "fin", c, apart=s_nil)
                    sp.dma_start(T["wkv_prompt"][ds(c * 2, 2)].rearrange("h i j -> i h j"),
                                 SO[:].rearrange("i (h j) -> i h j", h=2)).then_inc(s_so, 16)
                for s in (s_bo, s_y, s_so, s_ss):
                    sp.wait_ge(s, 16 * NCH + 16)

            @block.scalar
            def _(act):
                ac_.open(act)
                act.wait_ge(s_k, 16 * 7)
                with act.Fori(0, NCH) as c:
                    def step(name, *a, **k):
                        ac_.step(name, act.activation(*a, **k))

                    act.wait_ge(s_raw, c * 96 + 96)
                    step("sgw", W, W, ACT.Sigmoid, bias=par[:, 0:1])
                    step("alr", L, L, ACT.Sigmoid, bias=par[:, 1:2])
                    step("sq", SQ[:], K, ACT.Square, scale=par[:, 2:3])
                    pe_.wait(act, "n2", c)
                    step("n2", RN[:].rearrange("p (s n) -> p s n", s=3), ps[:, 0:3, 0:SL], ACT.Sqrt)
                    dv_.wait(act, "scan", c)
                    step("e1", E1[:], C[:], ACT.Exp)
                    step("ei", EI[:], C[:], ACT.Exp, scale=-1.0)
                    po_.wait(act, "cm", c)
                    step("e0", E0[:], E0[:], ACT.Exp)
                    pe_.wait(act, "smp", c)
                    act.wait_ge(s_ss, c * 16 + 16)
                    step("smp", SS[:].rearrange("s a n -> s (a n)"), ps[0:NS, 6:8, :].rearrange("s b n -> s (b n)")[:, 0:6 * P], ACT.Copy)
                    for n, (a, h) in enumerate(tr):
                        pe_.wait(act, f"tr{a}{h}", c)
                        step(f"tr{a}{h}", tok[:, a, 4 * h:4 * h + 4, :].rearrange("p t n -> p (t n)"), ps[:, n % 2, :], ACT.Copy)
                    for g in range(4):
                        pe_.wait(act, f"z{g}", c)
                        step(f"z{g}", X0[:, g].rearrange("p u n -> p (u n)"), ps[:, 6, 0:256], ACT.Copy)
                        pe_.wait(act, f"q{g}", c)
                        step(f"q{g}", Q[:, 4 * g:4 * g + 4].rearrange("p u n -> p (u n)"), ps[:, 7, 0:256], ACT.Copy)
                    for n in range(16):
                        if n:
                            dv_.wait(act, f"s{n - 1}", c)
                        else:
                            dv_.wait(act, "zero", c)
                        step(f"sw{n}", SW[:, n % 2], ST[:, n % 4], ACT.Copy, scale=E1[:, n * CH + CH - 1:n * CH + CH])
                        if n % 2:
                            t = n // 2
                            pe_.wait(act, f"y{t}", c)
                            if n == 1:
                                act.wait_ge(s_y, c * 16 + 16)
                            step(f"y{t}", Y[:, t * P:(t + 1) * P], ps[:, t % 2, 0:P], ACT.Copy)
                    pe_.wait(act, "fin", c)
                    act.wait_ge(s_so, c * 16 + 16)
                    step("fin", SO[:], ps[0:HD, 6, 0:P], ACT.Copy)

            @block.gpsimd
            def _(pool):
                po_.open(pool)
                pool.wait_ge(s_k, 16 * 7)
                with pool.Fori(0, NCH) as c:
                    ac_.wait(pool, "alr", c, apart=s_nil)
                    po_.step("t1", pool.tensor_scalar(KH[:], L, -1.0, par[:, 3:4], ALU.add, ALU.mult))
                    dv_.wait(pool, "scan", c, apart=s_nil)
                    po_.step("cm", pool.tensor_tensor(E0[:], C[:], W, ALU.subtract))
                    wait_at(pool, s_bo, c * 16 + 16, s_nil)
                    po_.step("rr", pool.tensor_scalar(RK[:], R, par[:, 4:5], None, ALU.mult))
                    po_.wait(pool, "rr", c, apart=s_nil)
                    dv_.wait(pool, "kh", c, apart=s_nil)
                    po_.step("rk", pool.tensor_tensor(RK[:], RK[:], KH[:], ALU.mult))
                    for g in range(4):
                        bc = lambda m: m[:].rearrange("p (o n) -> p o n", o=1).broadcast_to([P, 4, P])
                        Tg, Ttg = TB[:, g, 0], TB[:, g, 1]
                        dv_.wait(pool, f"ga{g}", c, apart=s_nil)
                        po_.step(f"ti{g}", pool.tensor_tensor(Tg, Tg, bc(ident), ALU.add))
                        po_.step(f"tm{g}", pool.tensor_tensor(Ttg, GB[:, 4 * g:4 * g + 4, 0, :], bc(mask1t), ALU.mult))
                        po_.wait(pool, f"tm{g}", c, apart=s_nil)
                        po_.step(f"tt{g}", pool.tensor_tensor(Ttg, Ttg, bc(ident), ALU.add))

            @block.vector
            def _(dve):
                dv_.open(dve)
                dve.wait_ge(s_k, 16 * 7)
                with dve.Fori(0, NCH) as c:
                    def tt(name, out, a, b, op=ALU.mult):
                        dv_.step(name, dve.tensor_tensor(out, a, b, op))

                    dve.wait_ge(s_raw, c * 96 + 96)
                    pe_.wait_before(dve, "fin", c)
                    dv_.step("zero", dve.memset(ST[:, 0], 0.0))
                    dv_.step("kkr", dve.tensor_scalar(KK[:], K, par[:, 2:3], None, ALU.mult))
                    ac_.wait(dve, "n2", c)
                    dv_.step("rmax", dve.tensor_scalar(RN[:], RN[:], 1e-12, None, ALU.max))
                    dv_.wait(dve, "rmax", c)
                    dv_.step("rinv", dve.reciprocal(RN[:], RN[:]))
                    dv_.wait(dve, "rinv", c)
                    tt("kk", KK[:], KK[:], RN[:])
                    ac_.wait(dve, "sgw", c)
                    dv_.step("logw", dve.tensor_scalar(W, W, -EXP_HALF, None, ALU.mult))
                    dv_.wait(dve, "logw", c)
                    dv_.step("scan", dve.tensor_tensor_scan(C[:], seg[:], W, 0.0, ALU.mult, ALU.add))
                    po_.wait(dve, "t1", c)
                    dv_.step("kh", dve.scalar_tensor_tensor(out=KH[:], in0=KH[:], scalar=1.0, in1=K, op0=ALU.add, op1=ALU.mult))
                    ac_.wait(dve, "e1", c)
                    tt("rt", AR[:, 1], R, E1[:])
                    dv_.step("bn", dve.scalar_tensor_tensor(out=BN[:], in0=KK[:], scalar=-1.0, in1=L, op0=ALU.mult, op1=ALU.mult))
                    ac_.wait(dve, "ei", c)
                    dv_.wait(dve, "bn", c)
                    tt("bh", BH[:], BN[:], EI[:])
                    tt("khh", KHH[:], KH[:], EI[:])
                    ac_.wait(dve, "e0", c)
                    tt("at", AR[:, 0], KK[:], E0[:])
                    pe_.wait(dve, "bonus", c)
                    dv_.step("bo", dve.tensor_tensor(RK[:].rearrange("p (s n) -> p s n", s=3), ps[:, 3:6, 0:SL],
                                                     V.rearrange("p (s n) -> p s n", s=3), ALU.mult))
                    mg = maskg[:].rearrange("p (o a) n -> p o a n", o=1).broadcast_to([P, 4, 2, P])
                    for g in range(4):
                        u = slice(4 * g, 4 * g + 4)
                        for nm, G, b in (("gb", GB, 2), ("gk", GK, 4)):
                            pe_.wait(dve, f"{nm}{g}", c)
                            tt(f"{nm}{g}", G[:, u], ps[:, b:b + 2, :].rearrange("p b (v a n) -> p (b v) a n", a=2, n=P), mg)
                        pe_.wait(dve, f"ga{g}", c)
                        tt(f"ga{g}", TB[:, g, 0].rearrange("p (h v) n -> p h v n", h=2), ps[:, 6:8, 0:256].rearrange("p h (v n) -> p h v n", n=P),
                           mask1[:].rearrange("p (a b n) -> p a b n", a=1, b=1).broadcast_to([P, 2, 2, P]))
                    for k, l, g in order:
                        pe_.wait(dve, f"{k}{l}{g}", c)
                        if k == "X":
                            tt(f"X{l}{g}", XB[:, g], ps[:, g % 2, :].rearrange("p (u n) -> p u n", u=4),
                               mlev[:, l:l + 1, :].broadcast_to([P, 4, P]))
                        else:
                            b = 2 + 2 * (g % 2)
                            a0 = 0 if l < LEVELS - 1 else 1
                            tt(f"T{l}{g}", TB[:, g, a0:2].rearrange("p a u n -> p a (u n)"), ps[:, b + a0:b + 2, :],
                               TB[:, g, a0:2].rearrange("p a u n -> p a (u n)"), ALU.add)
                    for g in range(4):
                        pe_.wait(dve, f"pt{g}", c)
                        dv_.step(f"pt{g}", dve.tensor_copy(PT[:, 2 * g:2 * g + 2].rearrange("p t n -> p (t n)"), ps[:, g % 2, 0:256]))
                    for n in range(16):
                        t, q = divmod(n, 2)
                        rows = slice(q * CH, q * CH + CH)
                        pe_.wait(dve, f"u{n}", c)
                        if n == 0:
                            ac_.wait(dve, "q3", c)
                        if n >= 4:
                            pe_.wait(dve, f"y{t - 2}", c)
                        tt(f"u{n}", UB[rows, t % 2], ps[rows, 2:4, 0:HD],
                           Q[rows, uid(t, 0):uid(t, 1) + 1:2, :], ALU.add)
                        pe_.wait(dve, f"s{n}", c)
                        ac_.wait(dve, f"sw{n}", c)
                        dv_.step(f"s{n}", dve.scalar_tensor_tensor(
                            out=ST[:, (n + 1) % 4], in0=ps[:, 4 + q, 0:HD], scalar=E1[:, n * CH + CH - 1:n * CH + CH],
                            in1=SW[:, n % 2], op0=ALU.mult, op1=ALU.add))

            @block.tensor
            def _(pe):
                pe_.open(pe)
                pe.wait_ge(s_k, 16 * 7)
                with pe.Fori(0, NCH) as c:
                    ac_.wait(pe, "sq", c)
                    ac_.wait_before(pe, "y7", c)
                    dv_.wait_before(pe, "s15", c)
                    for s in range(3):
                        ins = pe.matmul(ps[:, s, 0:SL], bones[:], SQ[:, s * SL:(s + 1) * SL], start=True, stop=True)
                    pe_.step("n2", ins)
                    po_.wait(pe, "rk", c)
                    for s in range(3):
                        ins = pe.matmul(ps[:, 3 + s, 0:SL], bones[:], RK[:, s * SL:(s + 1) * SL], start=True, stop=True)
                    pe_.step("bonus", ins)
                    ac_.wait_before(pe, "fin", c)
                    dv_.wait(pe, "khh", c)
                    for i, x in enumerate((R, E1[:], KH[:], V, KK[:], BN[:])):
                        ins = pe.transpose(ps[0:NS, 6 + i // 4, (i % 4) * P:(i % 4 + 1) * P], x[:, NP:NT], ident[:])
                    pe_.step("smp", ins)
                    for n, (a, h) in enumerate(tr):
                        x = (AR[:, 0, :], V, BH[:], KHH[:])[a]
                        if n == 0:
                            dv_.wait(pe, "at", c)
                        if n >= 2:
                            ac_.wait(pe, "tr%d%d" % tr[n - 2], c)
                        for t in range(4):
                            ins = pe.transpose(ps[:, n % 2, t * P:(t + 1) * P], x[:, (4 * h + t) * P:(4 * h + t + 1) * P], ident[:])
                        pe_.step(f"tr{a}{h}", ins)
                    for g in range(4):
                        for nm, x, b in (("gb", BH, 2), ("gk", KHH, 4)):
                            if g:
                                dv_.wait(pe, f"{nm}{g - 1}", c)
                            else:
                                dv_.wait(pe, "bo", c)
                            for u in range(4):
                                t, h = unit(g, u)
                                r, cols = slice(h * HD, h * HD + HD), slice(t * P, t * P + P)
                                ins = pe.matmul(ps[:, b + u // 2, (u % 2) * 256:(u % 2) * 256 + 256], x[r, cols], AR[r, :, cols],
                                                start=True, stop=True)
                            pe_.step(f"{nm}{g}", ins)
                        if g:
                            dv_.wait(pe, f"ga{g - 1}", c)
                        else:
                            ac_.wait(pe, "smp", c)
                        for u in range(4):
                            t, h = unit(g, u)
                            r, cols = slice(h * HD, h * HD + HD), slice(t * P, t * P + P)
                            ins = pe.matmul(ps[:, 6 + h, (u % 2) * P:(u % 2 + 1) * P], AR[r, 0, cols], BH[r, cols], start=True, stop=True)
                        pe_.step(f"ga{g}", ins)
                    ac_.wait(pe, "tr31", c)
                    for k, l, g in order:
                        if k == "X":
                            if l == 0:
                                po_.wait(pe, f"tt{g}", c)
                            else:
                                dv_.wait(pe, f"T{l - 1}{g}", c)
                            if g >= 2:
                                dv_.wait(pe, f"X{l}{g - 2}", c)
                            for u in range(4):
                                ins = pe.matmul(ps[:, g % 2, u * P:(u + 1) * P], GB[:, 4 * g + u, 0, :], TB[:, g, 0, u, :],
                                                start=True, stop=True)
                        else:
                            dv_.wait(pe, f"X{l}{g}", c)
                            if g >= 2:
                                dv_.wait(pe, f"T{l}{g - 2}", c)
                            elif l == 0:
                                dv_.wait(pe, "gk3", c)
                            b = 2 + 2 * (g % 2)
                            for u in range(4):
                                cols = slice(u * P, (u + 1) * P)
                                if l < LEVELS - 1:
                                    pe.matmul(ps[:, b, cols], TB[:, g, 1, u, :], XB[:, g, u, :], start=True, stop=True)
                                ins = pe.matmul(ps[:, b + 1, cols], XB[:, g, u, :], TB[:, g, 1, u, :], start=True, stop=True)
                        pe_.step(f"{k}{l}{g}", ins)
                    for g in range(4):
                        if g:
                            ac_.wait(pe, f"z{g - 1}", c)
                        else:
                            dv_.wait(pe, "ga3", c)
                        for u in range(4):
                            t, h = unit(g, u)
                            ins = pe.matmul(ps[:, 6, u * HD:(u + 1) * HD], GK[:, 4 * g + u, 0, :], tok[:, 1, t, h * HD:h * HD + HD],
                                            start=True, stop=True)
                        pe_.step(f"z{g}", ins)
                        dv_.wait(pe, f"T{LEVELS - 1}{g}", c)
                        if g >= 2:
                            dv_.wait(pe, f"pt{g - 2}", c)
                        for u in range(4):
                            t, h = unit(g, u)
                            ins = pe.matmul(ps[h * HD:h * HD + HD, g % 2, (u % 2) * P:(u % 2 + 1) * P],
                                            tok[:, 0, t, h * HD:h * HD + HD], TB[:, g, 1, u, :], start=True, stop=True)
                        pe_.step(f"pt{g}", ins)
                        ac_.wait(pe, f"z{g}", c)
                        if g:
                            ac_.wait(pe, f"q{g - 1}", c)
                        for u in range(4):
                            ins = pe.matmul(ps[:, 7, u * HD:(u + 1) * HD], TB[:, g, 1, u, :], X0[:, g, u, :], start=True, stop=True)
                        pe_.step(f"q{g}", ins)
                    for n in range(16):
                        t, q = divmod(n, 2)
                        rows = slice(q * CH, q * CH + CH)
                        dv_.wait(pe, f"s{n - 1}" if n else "pt3", c, apart=s_nil)
                        for h in range(2):
                            hr = slice(h * HD, h * HD + HD)
                            ins = pe.matmul(ps[rows, 2 + h, 0:HD], PT[hr, t, rows], ST[hr, n % 4, :],
                                            start=True, stop=True)
                        pe_.step(f"u{n}", ins)
                        for h in range(2):
                            hr = slice(h * HD, h * HD + HD)
                            pe.matmul(ps[hr, 4 + q, 0:HD], tok[rows, 3, t, hr], tok[rows, 1, t, hr], start=True, stop=False)
                        dv_.wait(pe, f"u{n}", c, apart=s_nil)
                        for h in range(2):
                            hr = slice(h * HD, h * HD + HD)
                            ins = pe.matmul(ps[hr, 4 + q, 0:HD], tok[rows, 2, t, hr], UB[rows, t % 2, h, :], start=False, stop=True)
                        pe_.step(f"s{n}", ins)
                        if q:
                            if t >= 2:
                                ac_.wait(pe, f"y{t - 2}", c)
                            for h in range(2):
                                hr, u = slice(h * HD, h * HD + HD), uid(t, h)
                                o = ps[hr, t % 2, 0:P]
                                pe.matmul(o, UB[:, t % 2, h, :], GB[:, u, 1, :], start=True, stop=False, skip_group_check=True)
                                pe.matmul(o, tok[:, 1, t, hr], GK[:, u, 1, :], start=False, stop=False, skip_group_check=True)
                                for qq in range(2):
                                    m = 2 * t + qq
                                    ins = pe.matmul(ps[hr, t % 2, qq * CH:(qq + 1) * CH], ST[hr, m % 4, :],
                                                    AR[hr, 1, t * P + qq * CH:t * P + (qq + 1) * CH],
                                                    start=False, stop=True, skip_group_check=True)
                            pe_.step(f"y{t}", ins)
                    dv_.wait(pe, "s15", c, apart=s_nil)
                    pe_.step("fin", pe.transpose(ps[0:HD, 6, 0:P], ST[:, 0, :], ident[:]))


def wkv_consts():
    i = np.arange(P)
    t, s = i[:, None], i[None, :]
    same = (t // CH) == (s // CH)
    one = np.float32
    out = {"k_ident": np.eye(P, dtype=one)}
    out["k_bones"] = ((t // HD) == (s // HD)).astype(one)
    out["k_maskg"] = np.stack([(same & (t < s)).astype(one), (same & (t <= s)).astype(one)], 1)
    lev = [((t // (2 * m)) == (s // (2 * m))) & ((t // m) % 2 == 1) & ((s // m) % 2 == 0) for m in (1, 2, 4, 8, 16, 32)]
    out["k_mask1"] = lev[0].astype(one)
    out["k_mask1t"] = np.ascontiguousarray(lev[0].T).astype(one)
    out["k_mlev"] = np.stack(lev[1:], 1).astype(one)
    n = np.arange(NT)
    out["k_seg"] = ((n % CH != 0) & (n < NP)).astype(one)[None]
    return out


NTP = 9 * P
TT = NTP // P
ZC = NTP + P
NE, NG, EG = 32, 4, 8
BIG = 1e30


def phase_sample(nc, T):
    with Pool_(nc, "smp") as A:
        ident = A.sb("ident", [P, P])
        v = A.sb("v", [P, 6, HD])
        S = A.sb("S", [P, HD, HD])
        T1 = A.sb("T1", [P, HD, HD])
        T2 = A.sb("T2", [P, HD, HD])
        T3 = A.sb("T3", [P, HD, HD])
        sa = A.sb("sa", [P, HD])
        y = A.sb("y", [P, HD])
        ys = A.sb("ys", [NS, D])
        ysT = A.sb("ysT", [P, KC, NS])
        ps = A.ps("ps", [P, KC, NS])
        s_ld = A.sem("loaded")
        s_v = A.sem("dve_steps")
        s_p = A.sem("pool_steps")
        s_y = A.sem("y_stored")
        s_S = A.sem("state_stored")
        s_yl = A.sem("y_token_rows")
        s_t = A.sem("y_transposed")
        s_c = A.sem("yT_ready")
        s_o = A.sem("yT_stored")
        vec = lambda i: v[:, i]
        key = lambda x: x.rearrange("p (o j) -> p o j", o=1).broadcast_to([P, HD, HD])
        val = lambda x: x.rearrange("p (i o) -> p i o", o=1).broadcast_to([P, HD, HD])
        with nc.Block() as block:

            @block.sync
            def _(sp):
                sp.dma_start(S[:], T["state_wkv"]).then_inc(s_ld, 16)
                sp.dma_start(v[:], T["sv_d"].rearrange("a s (h d) -> (s h) a d", d=HD)).then_inc(s_ld, 16)
                sp.dma_start(ident[:], T["k_ident"]).then_inc(s_ld, 16)
                sp.wait_ge(s_v, 5)
                sp.dma_start(T["wkv_sample"], T2[:]).then_inc(s_S, 16)
                sp.wait_ge(s_v, 7)
                sp.dma_start(T["ys_d"].rearrange("s (h d) -> (s h) d", d=HD), y[:]).then_inc(s_y, 16)
                sp.wait_ge(s_y, 16)
                sp.dma_start(ys[:], T["ys_d"]).then_inc(s_yl, 16)
                sp.wait_ge(s_c, 1)
                sp.dma_start(T["y_d"].rearrange("(c p) n -> p c n", p=P)[:, :, NP:NT], ysT[:]).then_inc(s_o, 16)
                sp.wait_ge(s_o, 16)
                sp.wait_ge(s_S, 16)

            @block.vector
            def _(dve):
                link = Chain(dve, s_v)
                dve.wait_ge(s_ld, 48)
                link(dve.tensor_tensor(T1[:], S[:], key(vec(4)), ALU.mult))
                link(dve.tensor_reduce(sa[:], T1[:], AX, ALU.add))
                link(dve.tensor_tensor(T1[:], val(sa[:]), key(vec(5)), ALU.mult))
                dve.wait_ge(s_p, 2)
                link(dve.tensor_tensor(T1[:], T1[:], T3[:], ALU.add))
                link(dve.tensor_tensor(T2[:], T2[:], T1[:], ALU.add))
                link(dve.tensor_tensor(T1[:], T2[:], key(vec(0)), ALU.mult))
                link(dve.tensor_reduce(y[:], T1[:], AX, ALU.add))
                dve.wait_ge(s_t, 1)
                dve.tensor_copy(ysT[:], ps[:]).then_inc(s_c, 1)

            @block.gpsimd
            def _(pool):
                pool.wait_ge(s_ld, 48)
                pool.tensor_tensor(T2[:], S[:], key(vec(1)), ALU.mult).then_inc(s_p, 1)
                pool.tensor_tensor(T3[:], val(vec(3)), key(vec(2)), ALU.mult).then_inc(s_p, 1)

            @block.tensor
            def _(pe):
                pe.wait_ge(s_ld, 48)
                pe.wait_ge(s_yl, 16)
                for k in range(KC):
                    ins = pe.transpose(ps[:, k, :], ys[:, k * P:(k + 1) * P], ident[0:NS, 0:NS])
                ins.then_inc(s_t, 1)


def phase_gn(nc, T):
    with Pool_(nc, "gn") as A:
        bones = A.sb("bones", [P, P])
        par = A.sb("par", [P, 2, KC])
        y = A.sb("y", [P, 2, 3, NT])
        sq = A.sb("sq", [P, NT])
        rs = A.sb("rs", [P, NT])
        z = A.sb("z", [P, 2, ZC])
        ps = [A.ps(f"ps{i}", [P, 3, 512]) for i in range(2)]
        s_nil = A.sem("waits_apart")
        s_k = A.sem("constants_loaded")
        s_ld = [A.sem(f"rows_loaded{i}") for i in range(2)]
        s_st = [A.sem(f"z_stored{i}") for i in range(2)]
        s_z = A.sem("pads_zeroed")
        three = lambda x: x.rearrange("p (s n) -> p s n", s=3)
        N = [f"{n}{i}" for i in range(2) for n in ("yc", "eps", "rs", "yn", "aff", "bo", "z")]
        dv_ = Steps(A.sem("dve_steps"), N)
        pe_ = Steps(A.sem("pe_steps"), ["mean0", "var0", "mean1", "var1"])
        ac_ = Steps(A.sem("act_steps"), ["sq0", "var0", "sq1", "var1"])
        NPAIR = KC // 2
        with nc.Block() as block:

            @block.sync
            def _(sp):
                sp.dma_start(bones[:], T["k_bones64"]).then_inc(s_k, 16)
                sp.dma_start(par[:], T["gn_par"]).then_inc(s_k, 16)
                with sp.Fori(0, NPAIR) as c:
                    for i in range(2):
                        dv_.wait_before(sp, f"z{i}", c, apart=s_nil)
                        rows = ds(c * (2 * P) + i * P, P)
                        sp.dma_start(y[:, i, 0, :], T["y_d"][rows, :]).then_inc(s_ld[i], 16)
                        sp.dma_start(y[:, i, 1, :], T["bonus_d"][rows, :]).then_inc(s_ld[i], 16)
                        sp.dma_start(y[:, i, 2, :], T["proj_d"][5, rows, :]).then_inc(s_ld[i], 16)

            @block.scalar
            def _(act):
                ac_.open(act)
                for s in s_st:
                    act.sem_inc(s, 16)
                with act.Fori(0, NPAIR) as c:
                    for i in range(2):
                        dv_.wait(act, f"yc{i}", c)
                        ac_.step(f"sq{i}", act.activation(sq[:], y[:, i, 0, :], ACT.Square))
                        dv_.wait(act, f"eps{i}", c)
                        ac_.step(f"var{i}", act.activation(three(rs[:]), three(rs[:]), ACT.Sqrt))
                        dv_.wait(act, f"z{i}", c, apart=s_nil)
                        act.dma_start(T["z_d"][ds(c * (2 * P) + i * P, P), :], z[:, i]).then_inc(s_st[i], 16)
                for s in s_st:
                    act.wait_ge(s, 16 * NPAIR + 16)

            @block.gpsimd
            def _(pool):
                pool.memset(z[:, :, NT:ZC], 0.0).then_inc(s_z, 1)

            @block.vector
            def _(dve):
                dv_.open(dve)
                dve.wait_ge(s_k, 32)
                dve.wait_ge(s_z, 1)
                with dve.Fori(0, NPAIR) as c:
                    for i in range(2):
                        Y = y[:, i, 0, :]
                        pe_.wait(dve, f"mean{i}", c)
                        dv_.step(f"yc{i}", dve.tensor_tensor(three(Y), three(Y), ps[0][:, :, 0:SL], ALU.subtract))
                        pe_.wait(dve, f"var{i}", c)
                        dv_.step(f"eps{i}", dve.tensor_scalar(three(rs[:]), ps[1][:, :, 0:SL], GN_EPS, None, ALU.add))
                        ac_.wait(dve, f"var{i}", c)
                        dv_.step(f"rs{i}", dve.reciprocal(rs[:], rs[:]))
                        dv_.wait(dve, f"rs{i}", c)
                        dv_.step(f"yn{i}", dve.tensor_tensor(Y, Y, rs[:], ALU.mult))
                        dv_.wait(dve, f"yn{i}", c)
                        k = c * 2 + i
                        dv_.step(f"aff{i}", dve.tensor_scalar(Y, Y, par[:, 0, ds(k, 1)], par[:, 1, ds(k, 1)], ALU.mult, ALU.add))
                        dv_.wait(dve, f"aff{i}", c)
                        dv_.step(f"bo{i}", dve.tensor_tensor(Y, Y, y[:, i, 1, :], ALU.add))
                        dve.wait_ge(s_st[i], c * 16 + 16)
                        dv_.wait(dve, f"bo{i}", c)
                        dv_.step(f"z{i}", dve.tensor_tensor(z[:, i, 0:NT], Y, y[:, i, 2, :], ALU.mult))

            @block.tensor
            def _(pe):
                pe_.open(pe)
                pe.wait_ge(s_k, 32)
                with pe.Fori(0, NPAIR) as c:
                    for i in range(2):
                        pe.wait_ge(s_ld[i], c * 48 + 48)
                        (dv_.wait if i else dv_.wait_before)(pe, f"yc{1 - i}", c)
                        for s in range(3):
                            ins = pe.matmul(ps[0][:, s, 0:SL], bones[:], y[:, i, 0, s * SL:(s + 1) * SL], start=True, stop=True)
                        pe_.step(f"mean{i}", ins)
                        ac_.wait(pe, f"sq{i}", c)
                        for s in range(3):
                            ins = pe.matmul(ps[1][:, s, 0:SL], bones[:], sq[:, s * SL:(s + 1) * SL], start=True, stop=True)
                        pe_.step(f"var{i}", ins)


def phase_post(nc, T, layer):
    tag = f"post{layer}"
    W_O = T["w_o"][layer]
    with Pool_(nc, tag) as A:
        ident = A.sb("ident", [P, P])
        low = A.sb("low", [P, P])
        ones = A.sb("ones", [P, P])
        wo = A.sb("wo", [P, KC, D])
        rw = A.sb("rw", [P, KC, NE])
        rb = A.sb("rb", [P, NE])
        iota = A.sb("iota", [P, NE])
        down = A.sb("down", [P, EG])
        valid = A.sb("valid", [P, TT])
        mod = A.sb("mod", [P, 2, 3, D])
        ln = A.sb("ln", [P, 2, D])
        zt = A.sb("zt", [P, 2, KC, P])
        x = A.sb("x", [P, 2, D])
        t1 = A.sb("t1", [P, D])
        x1 = A.sb("x1", [P, 2, D])
        xm = A.sb("xm", [P, 2, D])
        xmT = A.sb("xmT", [P, KC, P])
        st = A.sb("st", [P, 2, 6])
        mv = A.sb("mv", [P, 2])
        rs = A.sb("rs", [P, 1])
        lg = A.sb("lg", [P, TT, NE])
        aff = A.sb("aff", [P, TT, NE])
        sel = A.sb("sel", [P, TT, NE])
        eq = A.sb("eq", [P, TT, NE])
        m1 = A.sb("m1", [P, 2, TT * NG])
        r1 = A.sb("r1", [P, TT * NG])
        oh = A.sb("oh", [P, TT, 2, NE])
        gsum = A.sb("gsum", [P, TT, NG])
        geq = A.sb("geq", [P, TT, NG])
        gm = A.sb("gm", [P, TT])
        gr = A.sb("gr", [P, TT])
        ta = A.sb("ta", [P, TT, 2, NE])
        ga = A.sb("ga", [P, TT, 2])
        gt2 = A.sb("gt2", [P, TT])
        M = A.sb("M", [P, TT, NE])
        Mp = A.sb("Mp", [P, TT + 1, NE])
        EK = A.sb("EK", [P, TT * 2])
        RK = A.sb("RK", [P, TT * 2])
        GT = A.sb("GT", [P, TT * 2])
        cnt = A.sb("cnt", [P, NE])
        cmp_ = A.sb("cmp", [P, 8, TT * 2 + NE])
        nov = A.sb("nov", [P, NE])
        incl = A.sb("incl", [P, NE])
        q = A.sb("q", [P, TT * 2])
        base = A.sb("base", [P, TT * 2])
        q0 = A.sb("q0", [P, TT * 2])
        blk = A.sb("blk", [P, TT * 2])
        rem = A.sb("rem", [P, TT * 2])
        slotf = A.sb("slotf", [P, TT * 2])
        tixf = A.sb("tixf", [P, TT * 2])
        sloti = A.sb("sloti", [P, TT * 2], I32)
        tixi = A.sb("tixi", [P, TT * 2], I32)
        be = A.sb("be", [1, 16, NE])
        bef = A.sb("bef", [1, 2 + 48])
        pr = A.sb("pr", [1, 8])
        bei = A.sb("bei", [1, 2 + 48], I32)
        tokid = A.sb("tokid", [P, TT], I32)
        dummy = A.sb("dummy", [P, 2])
        zero48 = A.sb("zero48", [P, 48], I32)
        ps_mm = A.ps("ps_mm", [P, 2, 2, 512])
        ps_tr = A.ps("ps_tr", [P, 2, 512])
        ps_lg = A.ps("ps_lg", [P, NE])
        ps_rk = A.ps("ps_rk", [P, TT, NE])
        s_nil = A.sem("waits_apart")
        s_k = A.sem("constants_loaded")
        s_mz = A.sem("mod_zeroed")
        s_zt = [A.sem(f"z_tile_loaded{j}") for j in range(2)]
        s_x = [A.sem(f"x_loaded{j}") for j in range(2)]
        s_x1 = [A.sem(f"x1_stored{j}") for j in range(2)]
        s_xm = [A.sem(f"xm_stored{j}") for j in range(2)]
        s_init = A.sem("table_cleared")
        s_sc = A.sem("tokens_scattered")
        s_res = A.sem("routing_stored")
        both = lambda *names: [f"{x}{j}" for j in range(2) for x in names]
        dv_ = Steps(A.sem("dve_steps"), both("gmul", "res", "st0", "st1", "ag", "eps", "rs", "xn", "xg", "x1"))
        pe_ = Steps(A.sem("pe_steps"), both("mm", "tr", "lg"))
        ac_ = Steps(A.sem("act_steps"), both("sd", "xmT", "lg"))
        po_ = Steps(A.sem("pool_steps"), both("xs", "xm"))
        s_aff = A.sem("affinities_ready")
        s_M = A.sem("assignments_ready")
        s_rk = A.sem("ranks_summed")
        s_fin = A.sem("final_steps")
        s_cnt = A.sem("routing_chain")
        s_mm0 = A.sem("first_product")
        HALF = TT // 2
        NK = 16 * 18
        with nc.Block() as block:

            def tiles(eng, body):
                with eng.Fori(0, HALF) as i:
                    for j in range(2):
                        body(i, j, i * 2 + j)
                body(HALF, 0, TT - 1)

            rows = lambda t: ds(t * P, P) if not isinstance(t, int) else slice(t * P, t * P + P)

            @block.sync
            def _(sp):
                for dst, src in ((ident, T["k_ident"]), (low, T["k_low"]), (ones, T["k_ones"]), (iota, T["k_iota"]),
                                 (valid, T["k_valid"]), (tokid, T["k_tokid"]), (dummy, T["k_dummy"]),
                                 (rw, T["router_w"].rearrange("(k p) e -> p k e", p=P)),
                                 (rb, T["router_b"].broadcast_to([P, NE])),
                                 (wo, W_O.rearrange("(k p) n -> p k n", p=P))):
                    sp.dma_start(dst[:], src).then_inc(s_k, 16)
                for i in range(2):
                    sp.dma_start(ln[:, i], T["ln_gb"][layer * 2, i:i + 1, :].broadcast_to([P, D])).then_inc(s_k, 16)
                sp.wait_ge(s_mz, 1)
                a0, a1 = T["ada_d"][2 * layer], T["ada_d"][2 * layer + 1]
                for j, (a, lo) in enumerate(((a0, 2 * D), (a1, 0), (a1, D))):
                    sp.dma_start(mod[:, 0, j], a[NS:NC, lo:lo + D].broadcast_to([P, D])).then_inc(s_k, 16)
                    sp.dma_start(mod[0:NS, 1, j], a[0:NS, lo:lo + D]).then_inc(s_k, 16)
                zv = T["z_d"].rearrange("(k p) n -> p k n", p=P)
                for j in range(2):
                    sp.dma_start(zt[:, j], zv[:, :, j * P:(j + 1) * P]).then_inc(s_zt[j], 16)

                def body(i, j, t):
                    dv_.wait_before(sp, f"res{j}", i, apart=s_nil)
                    sp.dma_start(x[:, j], T["x_in"][layer][rows(t), :]).then_inc(s_x[j], 16)
                    if isinstance(t, int):
                        return
                    if j:
                        pe_.wait(sp, "mm0", i, apart=s_nil)
                    else:
                        sp.wait_ge(s_mm0, 1)
                        pe_.wait_before(sp, "mm1", i, apart=s_nil)
                    sp.dma_start(zt[:, j], zv[:, :, ds((t + 2) * P, P)]).then_inc(s_zt[j], 16)

                tiles(sp, body)
                sp.wait_ge(s_fin, 2)
                sp.dma_start(T["blk_d"][layer], bei[:]).then_inc(s_res, 16)
                sp.dma_start(T["slot_d"][layer], sloti[:]).then_inc(s_res, 16)
                sp.dma_start(T["gate_d"][layer], GT[:]).then_inc(s_res, 16)
                sp.wait_ge(s_res, 48)

            @block.gpsimd
            def _(pool):
                po_.open(pool)
                pool.memset(mod[:, 1], 0.0).then_inc(s_mz, 1)
                pool.memset(zero48[:], 0).then_inc(s_mz, 1)
                pool.wait_ge(s_mz, 2)
                pool.dma_start(T["table_d"][layer][0:48 * P, :].rearrange("(r b) o -> r (b o)", b=48), zero48[:]).then_inc(s_init, 16)
                pool.wait_ge(s_k, NK)

                def body(i, j, t):
                    kind = 1 if isinstance(t, int) else 0
                    dv_.wait(pool, f"x1{j}", i, apart=s_nil)
                    wait_at(pool, s_xm[j], i * 16 + 16, s_nil)
                    pe_.wait_before(pool, f"tr{j}", i, apart=s_nil)
                    po_.step(f"xs{j}", pool.tensor_tensor(xm[:, j], x1[:, j], mod[:, kind, 2], ALU.mult))
                    po_.wait(pool, f"xs{j}", i, apart=s_nil)
                    po_.step(f"xm{j}", pool.tensor_tensor(xm[:, j], xm[:, j], mod[:, kind, 1], ALU.add))

                tiles(pool, body)
                pool.wait_ge(s_fin, 2)
                pool.wait_ge(s_init, 16)
                for i in range(TT * 2):
                    pool.indirect_dma_start(T["table_d"][layer], bass.IndirectOffsetOnAxis(ap=tixi[:, i:i + 1], axis=0),
                                            tokid[:, i // 2:i // 2 + 1], None).then_inc(s_sc, 16)
                pool.wait_ge(s_sc, 16 * TT * 2)

            @block.scalar
            def _(act):
                ac_.open(act)
                for s in s_x1 + s_xm:
                    act.sem_inc(s, 16)

                def body(i, j, t):
                    dv_.wait(act, f"eps{j}", i)
                    ac_.step(f"sd{j}", act.activation(rs[:], rs[:], ACT.Sqrt))
                    dv_.wait(act, f"x1{j}", i, apart=s_nil)
                    act.dma_start(T["x1_d"][rows(t), :], x1[:, j]).then_inc(s_x1[j], 16)
                    po_.wait(act, f"xm{j}", i, apart=s_nil)
                    act.dma_start(T["xm_d"][rows(t), :], xm[:, j]).then_inc(s_xm[j], 16)
                    pe_.wait(act, f"tr{j}", i)
                    ac_.step(f"xmT{j}", act.activation(xmT[:].rearrange("p (b k) n -> p b (k n)", b=2), ps_tr[:], ACT.Copy))
                    pe_.wait(act, f"lg{j}", i)
                    dst = lg[:, ds(t, 1), :].rearrange("p o e -> p (o e)") if not isinstance(t, int) else lg[:, t]
                    ac_.step(f"lg{j}", act.activation(dst, ps_lg[:], ACT.Copy))

                tiles(act, body)
                ac_.wait(act, "lg0", HALF)
                act.activation(aff[:], lg[:], ACT.Sigmoid).then_inc(s_aff, 1)
                for s in s_x1 + s_xm:
                    act.wait_ge(s, 16 * (HALF + 1 + (s in (s_x1[0], s_xm[0]))))

            @block.vector
            def _(dve):
                dv_.open(dve)
                link = Chain(dve, s_cnt)
                link(dve.memset(Mp[:, 0], 0.0))
                dve.wait_ge(s_k, NK)
                link(dve.tensor_scalar(down[:], iota[:, 0:EG], -1.0, float(EG), ALU.mult, ALU.add))

                def body(i, j, t):
                    kind = 1 if isinstance(t, int) else 0

                    def op(name, ins, then=False):
                        dv_.step(f"{name}{j}", ins)
                        if then:
                            dv_.wait(dve, f"{name}{j}", i, apart=s_nil if then == "apart" else None)

                    if j:
                        pe_.wait(dve, "mm0", i)
                    else:
                        dve.wait_ge(s_mm0, 1)
                        pe_.wait_before(dve, "mm1", i)
                    op("gmul", dve.tensor_tensor(t1[:].rearrange("p (b n) -> p b n", b=2), ps_mm[:, j],
                                                 mod[:, kind, 0].rearrange("p (b n) -> p b n", b=2), ALU.mult), True)
                    dve.wait_ge(s_x[j], i * 16 + 16)
                    op("res", dve.scalar_tensor_tensor(out=t1[:], in0=x[:, j], scalar=ALPHA, in1=t1[:], op0=ALU.mult, op1=ALU.add), True)
                    op("st0", dve.bn_stats(st[:, 0], t1[:, 0:512]))
                    op("st1", dve.bn_stats(st[:, 1], t1[:, 512:D]), "apart")
                    op("ag", dve.bn_aggr(mv[:], st[:]), True)
                    op("eps", dve.tensor_scalar(rs[:], mv[:, 1:2], LN_EPS, None, ALU.add))
                    ac_.wait(dve, f"sd{j}", i)
                    op("rs", dve.reciprocal(rs[:], rs[:]), True)
                    op("xn", dve.tensor_scalar(t1[:], t1[:], mv[:, 0:1], rs[:], ALU.subtract, ALU.mult), True)
                    po_.wait_before(dve, f"xs{j}", i)
                    wait_at(dve, s_x1[j], i * 16 + 16)
                    op("xg", dve.tensor_tensor(x1[:, j], t1[:], ln[:, 0], ALU.mult), True)
                    op("x1", dve.tensor_tensor(x1[:, j], x1[:, j], ln[:, 1], ALU.add))

                tiles(dve, body)

                dve.wait_ge(s_aff, 1)
                link(dve.tensor_tensor(sel[:], aff[:], rb[:].rearrange("p (o e) -> p o e", o=1).broadcast_to([P, TT, NE]), ALU.add))
                groups = lambda a: a.rearrange("p t (g j) -> p (t g) j", g=NG)
                wide = lambda a, n: a.rearrange("p (m o) -> p m o", o=1).broadcast_to([P, a.shape[1], n])
                dn = lambda m, n: down[:, EG - n:].rearrange("p (o j) -> p o j", o=1).broadcast_to([P, m, n])
                for k in range(2):
                    s3, e3, o3 = groups(sel[:]), groups(eq[:]), oh[:, :, k, :].rearrange("p t (g j) -> p t g j", g=NG)
                    e4 = eq[:].rearrange("p t (g j) -> p t g j", g=NG)
                    link(dve.tensor_reduce(m1[:, k], s3, AX, ALU.max))
                    link(dve.tensor_tensor(e3, s3, wide(m1[:, k], EG), ALU.is_equal))
                    link(dve.tensor_tensor(e3, e3, dn(TT * NG, EG), ALU.mult))
                    link(dve.tensor_reduce(r1[:], e3, AX, ALU.max))
                    link(dve.tensor_tensor(e3, dn(TT * NG, EG), wide(r1[:], EG), ALU.is_equal))
                    link(dve.tensor_copy(o3, e4))
                    if k == 0:
                        link(dve.scalar_tensor_tensor(out=s3, in0=e3, scalar=-BIG, in1=s3, op0=ALU.mult, op1=ALU.add))
                link(dve.tensor_tensor(gsum[:].rearrange("p t g -> p (t g)"), m1[:, 0], m1[:, 1], ALU.add))
                link(dve.tensor_reduce(gm[:], gsum[:], AX, ALU.max))
                link(dve.tensor_tensor(geq[:], gsum[:], wide(gm[:], NG), ALU.is_equal))
                link(dve.tensor_tensor(geq[:], geq[:], dn(TT, NG), ALU.mult))
                link(dve.tensor_reduce(gr[:], geq[:], AX, ALU.max))
                link(dve.tensor_tensor(geq[:], dn(TT, NG), wide(gr[:], NG), ALU.is_equal))
                g5 = geq[:].rearrange("p t (g o) -> p t g o", o=1).broadcast_to([P, TT, NG, EG])
                for k in range(2):
                    o4 = oh[:, :, k, :].rearrange("p t (g j) -> p t g j", g=NG)
                    link(dve.tensor_tensor(o4, o4, g5, ALU.mult))
                flat = lambda a: a.rearrange("p t k e -> p (t k) e")
                io = iota[:].rearrange("p (o e) -> p o e", o=1).broadcast_to([P, TT * 2, NE])
                af = aff[:].rearrange("p t (o e) -> p t o e", o=1).broadcast_to([P, TT, 2, NE])
                link(dve.tensor_tensor(flat(ta[:]), flat(oh[:]), io, ALU.mult))
                link(dve.tensor_reduce(EK[:], flat(ta[:]), AX, ALU.add))
                link(dve.tensor_tensor(ta[:], oh[:], af, ALU.mult))
                link(dve.tensor_reduce(ga[:].rearrange("p t k -> p (t k)"), flat(ta[:]), AX, ALU.add))
                link(dve.tensor_reduce(gt2[:], ga[:], AX, ALU.add))
                link(dve.reciprocal(gt2[:], gt2[:]))
                link(dve.tensor_tensor(GT[:].rearrange("p (t k) -> p t k", k=2), ga[:], wide(gt2[:], 2), ALU.mult))
                link(dve.tensor_tensor(oh[:].rearrange("p t k e -> p t (k e)"), oh[:].rearrange("p t k e -> p t (k e)"),
                                       wide(valid[:], 2 * NE), ALU.mult))
                link(dve.tensor_tensor(M[:], oh[:, :, 0], oh[:, :, 1], ALU.add))
                for t in range(TT - 1):
                    link(dve.tensor_tensor(Mp[:, t + 1], Mp[:, t], M[:, t], ALU.add))
                dve.tensor_tensor(Mp[:, TT], Mp[:, TT - 1], M[:, TT - 1], ALU.add).then_inc(s_M, 1)
                dve.wait_ge(s_rk, 1)
                rkb = ps_rk[:].rearrange("p t (o e) -> p t o e", o=1).broadcast_to([P, TT, 2, NE])
                link(dve.tensor_tensor(ta[:], oh[:], rkb, ALU.mult))
                link(dve.tensor_reduce(RK[:], flat(ta[:]), AX, ALU.add))
                link(dve.tensor_copy(cnt[:], ps_lg[:]))
                for jj in range(8):
                    link(dve.tensor_scalar(cmp_[:, jj, 0:TT * 2], RK[:], 128.0 * (jj + 1), None, ALU.is_ge))
                for jj in range(8):
                    link(dve.tensor_scalar(cmp_[:, jj, TT * 2:], cnt[:], 128.0 * (jj + 1), None, ALU.is_gt))
                link(dve.tensor_reduce(q[:], cmp_[:, :, 0:TT * 2].rearrange("p j n -> p n j"), AX, ALU.add))
                link(dve.tensor_reduce(nov[:], cmp_[:, :, TT * 2:].rearrange("p j n -> p n j"), AX, ALU.add))
                link(dve.tensor_tensor_scan(incl[:], ones[:, 0:NE], nov[:], 0.0, ALU.mult, ALU.add))
                link(dve.tensor_tensor(nov[:], incl[:], nov[:], ALU.subtract))
                link(dve.tensor_tensor(flat(ta[:]), flat(oh[:]), nov[:].rearrange("p (o e) -> p o e", o=1).broadcast_to([P, TT * 2, NE]),
                                       ALU.mult))
                link(dve.tensor_reduce(base[:], flat(ta[:]), AX, ALU.add))
                link(dve.tensor_scalar(q0[:], q[:], 0.0, None, ALU.is_equal))
                link(dve.scalar_tensor_tensor(out=base[:], in0=base[:], scalar=float(NE - 1), in1=q[:], op0=ALU.add, op1=ALU.add))
                link(dve.tensor_tensor(blk[:], EK[:], base[:], ALU.subtract))
                link(dve.tensor_tensor(blk[:], blk[:], q0[:], ALU.mult))
                link(dve.tensor_tensor(blk[:], blk[:], base[:], ALU.add))
                link(dve.scalar_tensor_tensor(out=rem[:], in0=q[:], scalar=-128.0, in1=RK[:], op0=ALU.mult, op1=ALU.add))
                link(dve.scalar_tensor_tensor(out=slotf[:], in0=blk[:], scalar=128.0, in1=rem[:], op0=ALU.mult, op1=ALU.add))
                vb = valid[:].rearrange("p (t o) -> p t o", o=1).broadcast_to([P, TT, 2])
                tk = lambda a: a[:].rearrange("p (t k) -> p t k", k=2)
                link(dve.tensor_tensor(tk(slotf), tk(slotf), vb, ALU.mult))
                link(dve.scalar_tensor_tensor(out=tixf[:], in0=rem[:], scalar=48.0, in1=blk[:], op0=ALU.mult, op1=ALU.add))
                db = dummy[:].rearrange("p (o k) -> p o k", o=1).broadcast_to([P, TT, 2])
                link(dve.tensor_tensor(tk(tixf), tk(tixf), db, ALU.subtract))
                link(dve.tensor_tensor(tk(tixf), tk(tixf), vb, ALU.mult))
                link(dve.tensor_tensor(tk(tixf), tk(tixf), db, ALU.add))
                link(dve.tensor_copy(sloti[:], slotf[:]))
                dve.tensor_copy(tixi[:], tixf[:]).then_inc(s_fin, 1)
                link(dve.tensor_tensor(be[:], incl[0:1, :].rearrange("p (o e) -> p o e", o=1).broadcast_to([1, 16, NE]),
                                       iota[0:1, 0:16].rearrange("p (b o) -> p b o", o=1).broadcast_to([1, 16, NE]), ALU.is_le))
                link(dve.tensor_reduce(bef[:, 1 + NE:49], be[:], AX, ALU.add))
                link(dve.tensor_scalar(bef[:, 1 + NE:49], bef[:, 1 + NE:49], float(NE - 1), None, ALU.min))
                link(dve.tensor_copy(bef[:, 1:1 + NE], iota[0:1, :]))
                link(dve.memset(bef[:, 49:50], 0.0))
                link(dve.tensor_scalar(pr[:], iota[0:1, 0:8], 2.0, incl[0:1, NE - 1:NE], ALU.mult, ALU.is_lt))
                link(dve.tensor_reduce(bef[:, 0:1], pr[:], AX, ALU.add))
                link(dve.tensor_scalar(bef[:, 0:1], bef[:, 0:1], NE / 2, None, ALU.add))
                dve.tensor_copy(bei[:], bef[:]).then_inc(s_fin, 1)

            @block.tensor
            def _(pe):
                pe_.open(pe)
                pe.wait_ge(s_k, NK)

                def product(j):
                    for b in range(2):
                        for k in range(KC):
                            ins = pe.matmul(ps_mm[:, j, b], zt[:, j, k, :], wo[:, k, b * 512:(b + 1) * 512],
                                            start=(k == 0), stop=(k == KC - 1))
                    return ins

                pe.wait_ge(s_zt[0], 16)
                product(0).then_inc(s_mm0, 1)

                def body(i, j, t):
                    if not isinstance(t, int):
                        (dv_.wait if j else dv_.wait_before)(pe, f"gmul{1 - j}", i, apart=s_nil)
                        pe.wait_ge(s_zt[1 - j], i * 16 + 16 + 16 * j)
                        pe_.step(f"mm{j}", product(1 - j))
                    else:
                        pe_.skip(pe, "mm0", i)
                    po_.wait(pe, f"xm{j}", i, apart=s_nil)
                    (ac_.wait if j else ac_.wait_before)(pe, f"xmT{1 - j}", i, apart=s_nil)
                    for k in range(KC):
                        ins = pe.transpose(ps_tr[:, k // 4, (k % 4) * P:(k % 4 + 1) * P], xm[:, j, k * P:(k + 1) * P], ident[:])
                    pe_.step(f"tr{j}", ins)
                    ac_.wait(pe, f"xmT{j}", i, apart=s_nil)
                    (ac_.wait if j else ac_.wait_before)(pe, f"lg{1 - j}", i, apart=s_nil)
                    for k in range(KC):
                        ins = pe.matmul(ps_lg[:], xmT[:, k, :], rw[:, k, :], start=(k == 0), stop=(k == KC - 1))
                    pe_.step(f"lg{j}", ins)

                tiles(pe, body)
                pe.wait_ge(s_M, 1)
                for w, m, first in ((low, M[:], True), (ones, Mp[:, 0:TT], False)):
                    pe.matmul(ps_rk[:].rearrange("p t e -> p (t e)"), w[:], m.rearrange("p t e -> p (t e)"), start=first, stop=not first)
                pe.matmul(ps_lg[:], ones[:], Mp[:, TT], start=True, stop=True).then_inc(s_rk, 1)


def post_consts():
    one = np.float32
    i = np.arange(P)
    out = {"k_low": (i[:, None] < i[None, :]).astype(one), "k_ones": np.ones((P, P), one)}
    out["k_bones64"] = ((i[:, None] // HD) == (i[None, :] // HD)).astype(one) / HD
    out["k_iota"] = np.broadcast_to(np.arange(NE, dtype=one), (P, NE)).copy()
    tok = np.arange(NTP).reshape(TT, P).T
    out["k_valid"] = np.ascontiguousarray(tok < NT).astype(one)
    out["k_tokid"] = np.ascontiguousarray(tok).astype(np.int32)
    out["k_dummy"] = np.stack([48 * P + i, 49 * P + i], 1).astype(one)
    return out


NBLK = 48
DE = 512
KE = DE // P


def phase_init(nc, T):
    with Pool_(nc, "init") as A:
        z = A.sb("z", [P, D])
        s_z = A.sem("zeroed")
        s_c = A.sem("copied")
        with nc.Block() as block:

            @block.vector
            def _(dve):
                dve.memset(z[:], 0.0).then_inc(s_z, 1)

            @block.sync
            def _(sp):
                sp.dma_start(T["x_in"][0][0:NP, :], T["x_prompt"]).then_inc(s_c, 16)
                sp.dma_start(T["x_in"][0][NP:NT, :], T["x_sample"]).then_inc(s_c, 16)
                sp.wait_ge(s_z, 1)
                sp.dma_start(T["x_in"][0][NT:NTP, :], z[0:NTP - NT, :]).then_inc(s_c, 16)
                sp.dma_start(T["ysl_d"][NE * P:, :].rearrange("(b p) n -> p b n", p=P),
                             z[:].rearrange("p (o n) -> p o n", o=1).broadcast_to([P, NBLK - NE, D])).then_inc(s_c, 16)
                sp.wait_ge(s_c, 64)


def phase_moe(nc, T, layer):
    W_IN, W_OUT = T["moe_w_in"][layer], T["moe_w_out"][layer]
    with Pool_(nc, f"moe{layer}") as A:
        ident = A.sb("ident", [P, P])
        bei = A.sb("bei", [1, 2 + NBLK], I32)
        idx = A.sb("idx", [P, NBLK + 2], I32)
        col = A.sb("col", [P, 2], I32)
        X = A.sb("X", [P, 2, D])
        xT = A.sb("xT", [P, 2, KC, P])
        wi = A.sb("wi", [P, 2, KC, 2 * DE])
        wo = A.sb("wo", [P, 2, KE, D])
        sg = A.sb("sg", [P, DE])
        h = A.sb("h", [P, DE])
        hT = A.sb("hT", [P, KE, P])
        y = A.sb("y", [P, 2, D])
        ps_x = A.ps("ps_x", [P, 2, 512])
        ps_h = A.ps("ps_h", [P, 2, 512])
        ps_a = A.ps("ps_a", [P, 512])
        ps_y = A.ps("ps_y", [P, 2, 512])
        s_nil = A.sem("waits_apart")
        s_k = A.sem("constants_loaded")
        s_ix = A.sem("table_padded")
        s_wi = [A.sem(f"w_in_loaded{j}") for j in range(2)]
        s_wo = [A.sem(f"w_out_loaded{j}") for j in range(2)]
        s_x = [A.sem(f"rows_gathered{j}") for j in range(2)]
        s_y = [A.sem(f"y_stored{j}") for j in range(2)]
        s_x0 = A.sem("first_xT")
        pe_ = Steps(A.sem("pe_steps"), [f"{n}{j}" for j in range(2) for n in ("gate", "up", "xT", "hT", "y0", "y1")])
        ac_ = Steps(A.sem("act_steps"), [f"{n}{j}" for j in range(2) for n in ("silu", "hT", "y0")])
        dv_ = Steps(A.sem("dve_steps"), [f"{n}{j}" for j in range(2) for n in ("h", "xT", "y1")])
        po_ = Steps(A.sem("pool_steps"), ["col0", "col1"])

        def pairs(eng):
            eng.wait_ge(s_k, 48)
            return eng.value_load(bei[0:1, 0:1], min_val=NE // 2, max_val=NBLK // 2)

        with nc.Block() as block:

            @block.sync
            def _(sp):
                sp.dma_start(bei[:], T["blk_d"][layer]).then_inc(s_k, 16)
                sp.dma_start(idx[:, 0:NBLK], T["table_d"][layer][0:NBLK * P, :].rearrange("(r b) o -> r (b o)", b=NBLK)).then_inc(s_k, 16)
                sp.dma_start(ident[:], T["k_ident"]).then_inc(s_k, 16)
                for j in range(2):
                    sp.dma_start(wi[:, j], W_IN[j].rearrange("(k p) n -> p k n", p=P)).then_inc(s_wi[j], 16)
                    sp.dma_start(wo[:, j], W_OUT[j].rearrange("(k p) n -> p k n", p=P)).then_inc(s_wo[j], 16)
                n = pairs(sp)
                with sp.Fori(0, n - 1) as i:
                    for j in range(2):
                        e = sp.value_load(bei[0:1, ds(i * 2 + (3 + j), 1)], min_val=0, max_val=NE - 1)
                        pe_.wait(sp, f"up{j}", i, apart=s_nil)
                        sp.dma_start(wi[:, j], W_IN[ds(e, 1)].rearrange("o (k p) n -> p (o k) n", p=P)).then_inc(s_wi[j], 16)
                        pe_.wait(sp, f"y1{j}", i, apart=s_nil)
                        sp.dma_start(wo[:, j], W_OUT[ds(e, 1)].rearrange("o (k p) n -> p (o k) n", p=P)).then_inc(s_wo[j], 16)

            @block.gpsimd
            def _(pool):
                pool.memset(idx[:, NBLK:], 0).then_inc(s_ix, 1)
                pool.wait_ge(s_ix, 1)
                po_.open(pool)
                n = pairs(pool)

                def gather(j):
                    pool.indirect_dma_start(X[:, j], None, T["xm_d"], bass.IndirectOffsetOnAxis(ap=col[:, j:j + 1], axis=0)
                                            ).then_inc(s_x[j], 16)

                for j in range(2):
                    pool.tensor_copy(col[:, j:j + 1], idx[:, j:j + 1]).then_inc(s_ix, 1)
                    pool.wait_ge(s_ix, 2 + j)
                    gather(j)
                pool.wait_ge(s_x0, 1)
                with pool.Fori(0, n) as i:
                    for j in range(2):
                        pe_.wait(pool, f"xT{1 - j}", i, apart=s_nil) if j else pe_.wait_before(pool, "xT1", i, apart=s_nil)
                        pool.wait_ge(s_x[j], i * 16 + 16)
                        po_.step(f"col{j}", pool.tensor_copy(col[:, j:j + 1], idx[:, ds(i * 2 + (2 + j), 1)]))
                        po_.wait(pool, f"col{j}", i, apart=s_nil)
                        gather(j)
                for j in range(2):
                    wait_at(pool, s_x[j], n * 16 + 16, s_nil)

            @block.tensor
            def _(pe):
                pe_.open(pe)
                n = pairs(pe)

                def transposes(j):
                    for k in range(KC):
                        ins = pe.transpose(ps_x[:, k // 4, (k % 4) * P:(k % 4 + 1) * P], X[:, j, k * P:(k + 1) * P], ident[:])
                    return ins

                pe.wait_ge(s_x[0], 16)
                transposes(0).then_inc(s_x0, 1)
                with pe.Fori(0, n) as i:
                    for j in range(2):
                        if j:
                            dv_.wait(pe, "xT0", i, apart=s_nil)
                        else:
                            dv_.wait_before(pe, "xT1", i, apart=s_nil)
                            pe.wait_ge(s_x0, 2)
                        pe.wait_ge(s_wi[j], i * 16 + 16)
                        for half, name in enumerate(("gate", "up")):
                            (ac_.wait if j else ac_.wait_before)(pe, f"silu{1 - j}", i, apart=s_nil)
                            if half:
                                (dv_.wait if j else dv_.wait_before)(pe, f"h{1 - j}", i, apart=s_nil)
                            for k in range(KC):
                                ins = pe.matmul(ps_h[:, half], xT[:, j, k, :], wi[:, j, k, half * DE:(half + 1) * DE],
                                                start=(k == 0), stop=(k == KC - 1))
                            pe_.step(f"{name}{j}", ins)
                        pe.wait_ge(s_x[1 - j], i * 16 + 16 + 16 * j)
                        pe_.step(f"xT{j}", transposes(1 - j))
                        dv_.wait(pe, f"h{j}", i, apart=s_nil)
                        for k in range(KE):
                            ins = pe.transpose(ps_a[:, k * P:(k + 1) * P], h[:, k * P:(k + 1) * P], ident[:])
                        pe_.step(f"hT{j}", ins)
                        ac_.wait(pe, f"hT{j}", i, apart=s_nil)
                        pe.wait_ge(s_wo[j], i * 16 + 16)
                        for half in range(2):
                            if half:
                                (dv_.wait if j else dv_.wait_before)(pe, f"y1{1 - j}", i, apart=s_nil)
                            else:
                                (ac_.wait if j else ac_.wait_before)(pe, f"y0{1 - j}", i, apart=s_nil)
                            for k in range(KE):
                                ins = pe.matmul(ps_y[:, half], hT[:, k, :], wo[:, j, k, half * 512:(half + 1) * 512],
                                                start=(k == 0), stop=(k == KE - 1))
                            pe_.step(f"y{half}{j}", ins)

            @block.scalar
            def _(act):
                ac_.open(act)
                for s in s_y:
                    act.sem_inc(s, 16)
                n = pairs(act)
                with act.Fori(0, n) as i:
                    for j in range(2):
                        pe_.wait(act, f"gate{j}", i)
                        (dv_.wait if j else dv_.wait_before)(act, f"h{1 - j}", i)
                        ac_.step(f"silu{j}", act.activation(sg[:], ps_h[:, 0], ACT.Silu))
                        pe_.wait(act, f"hT{j}", i)
                        ac_.step(f"hT{j}", act.activation(hT[:].rearrange("p k n -> p (k n)"), ps_a[:], ACT.Copy))
                        pe_.wait(act, f"y0{j}", i)
                        act.wait_ge(s_y[j], i * 16 + 16)
                        ac_.step(f"y0{j}", act.activation(y[:, j, 0:512], ps_y[:, 0], ACT.Copy))
                        ac_.wait(act, f"y0{j}", i)
                        dv_.wait(act, f"y1{j}", i, apart=s_nil)
                        act.dma_start(T["ysl_d"][ds(i * (2 * P) + j * P, P), :], y[:, j]).then_inc(s_y[j], 16)
                for j in range(2):
                    wait_at(act, s_y[j], n * 16 + 16, s_nil)

            @block.vector
            def _(dve):
                dv_.open(dve)
                n = pairs(dve)
                xTv = lambda j: xT[:, j].rearrange("p (b k) n -> p b (k n)", b=2)
                dve.wait_ge(s_x0, 1)
                dve.tensor_copy(xTv(0), ps_x[:]).then_inc(s_x0, 1)
                with dve.Fori(0, n) as i:
                    for j in range(2):
                        ac_.wait(dve, f"silu{j}", i)
                        pe_.wait(dve, f"up{j}", i)
                        (pe_.wait if j else pe_.wait_before)(dve, f"hT{1 - j}", i)
                        dv_.step(f"h{j}", dve.tensor_tensor(h[:], sg[:], ps_h[:, 1], ALU.mult))
                        pe_.wait(dve, f"xT{j}", i)
                        dv_.step(f"xT{j}", dve.tensor_copy(xTv(1 - j), ps_x[:]))
                        pe_.wait(dve, f"y1{j}", i)
                        dve.wait_ge(s_y[j], i * 16 + 16)
                        dv_.step(f"y1{j}", dve.tensor_copy(y[:, j, 512:D], ps_y[:, 1]))


def phase_combine(nc, T, layer):
    out = T["x_in"][1] if layer == 0 else None
    with Pool_(nc, f"comb{layer}") as A:
        slot = A.sb("slot", [P, 2 * TT], I32)
        col = A.sb("col", [P, 2, 2], I32)
        gate = A.sb("gate", [P, 2 * TT])
        mod = A.sb("mod", [P, 2, D])
        ln = A.sb("ln", [P, 2, D])
        x = A.sb("x", [P, 2, D])
        Y = A.sb("Y", [P, 2, 2, D])
        o = A.sb("o", [P, 2, D])
        st = A.sb("st", [P, 2, 6])
        mv = A.sb("mv", [P, 2])
        rs = A.sb("rs", [P, 1])
        s_nil = A.sem("waits_apart")
        s_k = A.sem("constants_loaded")
        s_z = A.sem("mod_zeroed")
        s_x = [A.sem(f"x_loaded{j}") for j in range(2)]
        s_g = [A.sem(f"rows_gathered{j}") for j in range(2)]
        s_o = [A.sem(f"x_stored{j}") for j in range(2)]
        N = [f"{n}{j}" for j in range(2) for n in ("g0", "g1", "gm", "res", "st0", "st1", "ag", "eps", "rs", "xn", "xg", "xb")]
        dv_ = Steps(A.sem("dve_steps"), N)
        ac_ = Steps(A.sem("act_steps"), ["sd0", "sd1"])
        po_ = Steps(A.sem("pool_steps"), ["ca0", "cb0", "ca1", "cb1"])
        HALF = TT // 2
        assert TT % 2
        with nc.Block() as block:

            def tiles(eng, body):
                with eng.Fori(0, HALF) as i:
                    for j in range(2):
                        body(i, j, i * 2 + j)
                body(HALF, 0, TT - 1)

            rows = lambda t: ds(t * P, P) if not isinstance(t, int) else slice(t * P, t * P + P)
            cols = lambda t, k: ds(t * 2 + k, 1) if not isinstance(t, int) else slice(t * 2 + k, t * 2 + k + 1)

            @block.sync
            def _(sp):
                sp.dma_start(slot[:], T["slot_d"][layer]).then_inc(s_k, 16)
                sp.dma_start(gate[:], T["gate_d"][layer]).then_inc(s_k, 16)
                for i in range(2):
                    sp.dma_start(ln[:, i], T["ln_gb"][layer * 2 + 1, i:i + 1, :].broadcast_to([P, D])).then_inc(s_k, 16)
                a = T["ada_d"][2 * layer + 1]
                sp.wait_ge(s_z, 1)
                sp.dma_start(mod[:, 0], a[NS:NC, 2 * D:3 * D].broadcast_to([P, D])).then_inc(s_k, 16)
                sp.dma_start(mod[0:NS, 1], a[0:NS, 2 * D:3 * D]).then_inc(s_k, 16)

                def body(i, j, t):
                    dv_.wait_before(sp, f"res{j}", i, apart=s_nil)
                    sp.dma_start(x[:, j], T["x1_d"][rows(t), :]).then_inc(s_x[j], 16)

                tiles(sp, body)

            @block.gpsimd
            def _(pool):
                po_.open(pool)
                pool.memset(mod[:, 1], 0.0).then_inc(s_z, 1)
                pool.wait_ge(s_k, 96)

                def body(i, j, t):
                    dv_.wait_before(pool, f"xg{j}", i, apart=s_nil)
                    po_.step(f"ca{j}", pool.tensor_copy(col[:, j, 0:1], slot[:, cols(t, 0)]))
                    po_.step(f"cb{j}", pool.tensor_copy(col[:, j, 1:2], slot[:, cols(t, 1)]))
                    po_.wait(pool, f"cb{j}", i, apart=s_nil)
                    for k in range(2):
                        pool.indirect_dma_start(Y[:, j, k], None, T["ysl_d"], bass.IndirectOffsetOnAxis(ap=col[:, j, k:k + 1], axis=0)
                                                ).then_inc(s_g[j], 16)

                tiles(pool, body)
                pool.wait_ge(s_g[0], 32 * (HALF + 1))
                pool.wait_ge(s_g[1], 32 * HALF)

            @block.scalar
            def _(act):
                ac_.open(act)
                for s in s_o:
                    act.sem_inc(s, 16)

                def body(i, j, t):
                    dv_.wait(act, f"eps{j}", i)
                    ac_.step(f"sd{j}", act.activation(rs[:], rs[:], ACT.Sqrt))
                    dv_.wait(act, f"xb{j}", i, apart=s_nil)
                    if isinstance(t, int) and layer == 1:
                        act.dma_start(T["y_sample"], o[0:NS, j]).then_inc(s_o[j], 16)
                    else:
                        act.dma_start((out if layer == 0 else T["y_prompt"])[rows(t), :], o[:, j]).then_inc(s_o[j], 16)

                tiles(act, body)
                act.wait_ge(s_o[0], 16 * (HALF + 2))
                act.wait_ge(s_o[1], 16 * (HALF + 1))

            @block.vector
            def _(dve):
                dv_.open(dve)
                dve.wait_ge(s_k, 96)

                def body(i, j, t):
                    kind = 1 if isinstance(t, int) else 0

                    def op(name, ins, then=True):
                        dv_.step(f"{name}{j}", ins)
                        if then:
                            dv_.wait(dve, f"{name}{j}", i, apart=s_nil if then == "apart" else None)

                    a, b = Y[:, j, 0], Y[:, j, 1]
                    dve.wait_ge(s_g[j], i * 32 + 32)
                    op("g0", dve.tensor_scalar(a, a, gate[:, cols(t, 0)], None, ALU.mult))
                    op("g1", dve.scalar_tensor_tensor(out=a, in0=b, scalar=gate[:, cols(t, 1)], in1=a, op0=ALU.mult, op1=ALU.add))
                    op("gm", dve.tensor_tensor(a, a, mod[:, kind], ALU.mult))
                    dve.wait_ge(s_x[j], i * 16 + 16)
                    op("res", dve.scalar_tensor_tensor(out=a, in0=x[:, j], scalar=ALPHA, in1=a, op0=ALU.mult, op1=ALU.add))
                    op("st0", dve.bn_stats(st[:, 0], a[:, 0:512]), False)
                    op("st1", dve.bn_stats(st[:, 1], a[:, 512:D]), "apart")
                    op("ag", dve.bn_aggr(mv[:], st[:]))
                    op("eps", dve.tensor_scalar(rs[:], mv[:, 1:2], LN_EPS, None, ALU.add), False)
                    ac_.wait(dve, f"sd{j}", i)
                    op("rs", dve.reciprocal(rs[:], rs[:]))
                    op("xn", dve.tensor_scalar(a, a, mv[:, 0:1], rs[:], ALU.subtract, ALU.mult))
                    dve.wait_ge(s_o[j], i * 16 + 16)
                    op("xg", dve.tensor_tensor(o[:, j], a, ln[:, 0], ALU.mult))
                    op("xb", dve.tensor_tensor(o[:, j], o[:, j], ln[:, 1], ALU.add), False)

                tiles(dve, body)


NG3 = 3
DIL = (1, 4, 16)
KVH, REP = 4, 4
ROT = 16
PASS = HD - ROT
PAST = 256
NEG = -1e30
QR = NG3 * H * ROT
QP = NG3 * H * PASS
NR, NPS = QR // P, QP // P
SCALE = HD ** -0.5


def phase_qkv(nc, T):
    with Pool_(nc, "qkv") as A:
        ident = A.sb("ident", [P, P])
        rotp = A.sb("rotp", [P, P])
        ada = A.sb("ada", [NC, 4, D])
        mod = A.sb("mod", [P, 4, KC, NC])
        x = A.sb("x", [P, TT, D])
        kc = x[0:HD].rearrange("p t n -> p (t n)")[:, 0:2 * KVH * NP].rearrange("p (a h n) -> p a h n", a=2, h=KVH)
        hh = A.sb("hh", [P, 2, KC, NT])
        cos = A.sb("cos", [P, NT])
        sin = A.sb("sin", [P, NT])
        ctok = A.sb("ctok", [P, TT, 2, 8])
        wkv = A.sb("wkv", [P, KC, 512])
        wr = A.sb("wr", [P, 4, KC, P])
        kv = A.sb("kv", [P, 2, 512])
        tmp = A.sb("tmp", [P, 4, KVH, 8])
        kn = A.sb("kn", [HD, 2, KVH, P])
        raw = A.sb("raw", [P, NT])
        t1 = A.sb("t1", [P, NT])
        t2 = A.sb("t2", [P, NT])
        ev = A.sb("ev", [P, 2, NT])
        qsT = A.sb("qsT", [P, NR + NPS, NS])
        qs = A.sb("qs", [NS, (NR + NPS) * P])
        ps = [A.ps(f"ps{i}", [P, 3, 512]) for i in range(2)]
        pm = A.ps("pm", [P, 2, 512])
        s_nil = A.sem("waits_apart")
        s_ld = A.sem("constants_loaded")
        s_x = A.sem("x_loaded")
        s_mt = A.sem("mod_transposed")
        s_m = A.sem("mod_ready")
        s_z = A.sem("dve_chain")
        s_xt = A.sem("x_transposed")
        s_h = A.sem("h_ready")
        s_kvp = A.sem("kv_product")
        s_kve = A.sem("kv_evacuated")
        s_kvr = A.sem("kv_rotated")
        s_kt = A.sem("k_transposed")
        s_kn = A.sem("k_copied")
        s_kvs = [A.sem(f"kv_stored{i}") for i in range(2)]
        s_kns = [A.sem(f"k_natural_stored{i}") for i in range(2)]
        s_kcs = A.sem("k_classes_stored")
        s_wr = [A.sem(f"w_loaded{i}") for i in range(4)]
        s_q = A.sem("q_product")
        s_raw = A.sem("q_raw")
        s_rp = A.sem("q_swapped")
        s_rm = A.sem("q_rotated")
        s_e = A.sem("q_ready")
        s_evs = [A.sem(f"q_stored{i}") for i in range(2)]
        s_qt = A.sem("sample_q_transposed")
        s_qs = A.sem("sample_q_ready")
        s_qd = A.sem("sample_q_stored")
        NCH = NR + NPS
        wv = T["w_q"].rearrange("(k p) (c n) -> p k c n", p=P, n=P)

        def group(n):
            return n // (NR // NG3) if n < NR else (n - NR) // (NPS // NG3)

        def classes(v, g, half=None):
            d = DIL[g]
            v = v[:, 0:NP].rearrange("p (c n) -> p n c", c=d)
            return v if half is None else v[:, half * 512 // d:(half + 1) * 512 // d, :]

        tokens = lambda v, g: v.rearrange("p (n c) -> p n c", c=DIL[g])
        with nc.Block() as block:

            @block.sync
            def _(sp):
                for dst, src in ((ident[:], T["k_ident"]), (rotp[:], T["k_rotp"]), (ada[:, 0:2], T["ada_d"][2, :, 0:2 * D].rearrange("c (a n) -> c a n", a=2)),
                                 (ada[:, 2:4], T["kva_d"].rearrange("c (a n) -> c a n", a=2)), (cos[:], T["k_cos"]),
                                 (sin[:], T["k_sin"]), (ctok[:], T["k_ctok"])):
                    sp.dma_start(dst, src).then_inc(s_ld, 16)
                sp.dma_start(x[:], T["x_in"][1].rearrange("(t p) n -> p t n", p=P)).then_inc(s_x, 16)
                sp.dma_start(wkv[:], T["w_kv"].rearrange("(k p) n -> p k n", p=P)).then_inc(s_ld, 16)
                for j in range(4):
                    sp.dma_start(wr[:, j], wv[:, :, j, :]).then_inc(s_wr[j], 16)
                for n in range(4, NCH):
                    sp.wait_ge(s_q, n - 3)
                    sp.dma_start(wr[:, n % 4], wv[:, :, n, :]).then_inc(s_wr[n % 4], 16)

            @block.gpsimd
            def _(pool):
                for t in range(TT):
                    r = slice(t * P, t * P + P)
                    j = t % 2
                    pool.wait_ge(s_kvr, t + 1)
                    if t < TILES:
                        pool.dma_start(T["k_prompt"][r, :], kv[:, j, 0:256]).then_inc(s_kvs[j], 16)
                        pool.dma_start(T["v_prompt"][r, :], kv[:, j, 256:512]).then_inc(s_kvs[j], 16)
                        for g, d in enumerate(DIL):
                            dst = T["v_d"][g].rearrange("(c n) f -> n c f", c=d)[t * P // d:(t + 1) * P // d]
                            pool.dma_start(dst, kv[:, j, 256:512]).then_inc(s_kvs[j], 16)
                        pool.wait_ge(s_kn, t + 1)
                        pool.dma_start(T["k_d"][0, :, :, r].rearrange("h d n -> d h n"), kn[:, j]).then_inc(s_kns[j], 16)
                    else:
                        pool.dma_start(T["k_sample"], kv[0:NS, j, 0:256]).then_inc(s_kvs[j], 16)
                        pool.dma_start(T["v_sample"], kv[0:NS, j, 256:512]).then_inc(s_kvs[j], 16)
                for g in (1, 2):
                    pool.dma_start(T["k_d"][g].rearrange("h d n -> d h n"), kc[:, g - 1]).then_inc(s_kcs, 16)
                for n in range(NCH):
                    pool.wait_ge(s_e, n + 1)
                    dst = T["qr_d"][n * P:(n + 1) * P, :] if n < NR else T["qp_d"][(n - NR) * P:(n - NR + 1) * P, :]
                    pool.dma_start(dst, ev[:, n % 2, 0:NP]).then_inc(s_evs[n % 2], 16)
                pool.wait_ge(s_qs, NCH // 4)
                pool.dma_start(T["qs_d"], qs[:]).then_inc(s_qd, 16)
                pool.wait_ge(s_qd, 16)
                pool.wait_ge(s_kcs, 32)
                pool.wait_ge(s_kvs[0], 16 * (5 * 4 + 2))
                pool.wait_ge(s_kvs[1], 16 * 5 * 4)
                for j in range(2):
                    pool.wait_ge(s_evs[j], 16 * NCH // 2)
                    pool.wait_ge(s_kns[j], 16 * TILES // 2)

            @block.vector
            def _(dve):
                link = Chain(dve, s_z)
                for a in range(2):
                    dve.wait_ge(s_mt, a + 1)
                    dve.tensor_copy(mod[:, 2 * a:2 * a + 2].rearrange("p a k c -> p (a k) c"),
                                    pm[:, a, 0:2 * KC * 16].rearrange("p (a c) -> p a c", c=16)[:, :, 0:NC]).then_inc(s_m, 1)
                dve.wait_ge(s_m, 2)
                for u in range(2 * KC):
                    k, half = divmod(u, 2)
                    dve.wait_ge(s_xt, u + 1)
                    for a in range(2):
                        ins = dve.tensor_scalar(hh[:, a, k, half * 512:half * 512 + 512], ps[u % 2][:, 0, :],
                                                mod[:, 2 * a + 1, k, NS:NC], mod[:, 2 * a, k, NS:NC], ALU.mult, ALU.add)
                    ins.then_inc(s_h, 1)
                dve.wait_ge(s_xt, 2 * KC + 1)
                v = pm[:, 0, 0:KC * NS].rearrange("p (k s) -> p k s", s=NS)
                for a in range(2):
                    hs = hh[:, a, :, NP:NT]
                    link(dve.tensor_tensor(hs, v, mod[:, 2 * a + 1, :, 0:NS], ALU.mult))
                    ins = dve.tensor_tensor(hs, hs, mod[:, 2 * a, :, 0:NS], ALU.add)
                ins.then_inc(s_h, 1)
                for t in range(TT):
                    r = P if t < TILES else NS
                    j = t % 2
                    dve.wait_ge(s_kve, t + 1)
                    kh = kv[0:r, j, 0:256].rearrange("p (h d) -> p h d", h=KVH)
                    a, b = kh[:, :, 0:8], kh[:, :, 8:16]
                    c = ctok[0:r, t, 0:1, :].broadcast_to([r, KVH, 8])
                    s = ctok[0:r, t, 1:2, :].broadcast_to([r, KVH, 8])
                    for i, (o, m) in enumerate(((a, c), (b, s), (b, c), (a, s))):
                        ins = dve.tensor_tensor(tmp[0:r, i], o, m, ALU.mult)
                    link(ins)
                    dve.tensor_tensor(a, tmp[0:r, 0], tmp[0:r, 1], ALU.subtract)
                    dve.tensor_tensor(b, tmp[0:r, 2], tmp[0:r, 3], ALU.add).then_inc(s_kvr, 1)
                    if t < TILES:
                        dve.wait_ge(s_kt, t + 1)
                        src = ps[j][0:HD, 1, :].rearrange("p (h n) -> p h n", h=KVH)
                        if t >= 2:
                            dve.wait_ge(s_kns[j], 16 * (t // 2))
                        dve.tensor_copy(kn[:, j], src)
                        for g in (1, 2):
                            d = DIL[g]
                            for hd in range(KVH):
                                ins = dve.tensor_copy(
                                    kc[:, g - 1, hd].rearrange("p (c n) -> p n c", c=d)[:, t * P // d:(t + 1) * P // d, :],
                                    src[:, hd].rearrange("p (n c) -> p n c", c=d))
                        ins.then_inc(s_kn, 1)
                for n in range(NR):
                    dve.wait_ge(s_raw, n + 1)
                    dve.tensor_tensor(t1[:], raw[:], cos[:], ALU.mult)
                    dve.wait_ge(s_rp, n + 1)
                    link(dve.tensor_tensor(t2[:, 0:NP].rearrange("p (s n) -> p s n", s=2), ps[1 - n % 2][:, 0:2, :],
                                           sin[:, 0:NP].rearrange("p (s n) -> p s n", s=2), ALU.mult))
                    link(dve.tensor_tensor(t2[:, NP:NT], ps[1 - n % 2][:, 2, 0:NS], sin[:, NP:NT], ALU.mult))
                    if n >= 2:
                        dve.wait_ge(s_evs[n % 2], 16 * (n // 2))
                    g = group(n)
                    dve.tensor_tensor(classes(ev[:, n % 2], g), tokens(t1[:, 0:NP], g), tokens(t2[:, 0:NP], g), ALU.add)
                    dve.tensor_tensor(qsT[:, n], t1[:, NP:NT], t2[:, NP:NT], ALU.add).then_inc(s_e, 1)

            @block.tensor
            def _(pe):
                pe.wait_ge(s_ld, 16 * 8)
                for b in range(2):
                    for a in range(2):
                        for k in range(KC):
                            o = (a * KC + k) * 16
                            ins = pe.transpose(pm[:, b, o:o + NC], ada[:, 2 * b + a, k * P:(k + 1) * P], ident[0:NC, 0:NC])
                    ins.then_inc(s_mt, 1)
                pe.wait_ge(s_x, 16)
                for u in range(2 * KC):
                    k, half = divmod(u, 2)
                    if u >= 2:
                        pe.wait_ge(s_h, u - 1)
                    for t in range(4):
                        ins = pe.transpose(ps[u % 2][:, 0, t * P:(t + 1) * P], x[:, 4 * half + t, k * P:(k + 1) * P], ident[:])
                    ins.then_inc(s_xt, 1)
                pe.wait_ge(s_m, 1)
                for k in range(KC):
                    ins = pe.transpose(pm[:, 0, k * NS:(k + 1) * NS], x[0:NS, TILES, k * P:(k + 1) * P], ident[0:NS, 0:NS])
                ins.then_inc(s_xt, 1)
                pe.wait_ge(s_h, 2 * KC + 1)

                def k_transposes(t):
                    pe.wait_ge(s_kvr, t + 1)
                    if t >= 2:
                        pe.wait_ge(s_kn, t - 1)
                    for hd in range(KVH):
                        ins = pe.transpose(ps[t % 2][0:HD, 1, hd * P:(hd + 1) * P], kv[:, t % 2, hd * HD:(hd + 1) * HD], ident[:])
                    ins.then_inc(s_kt, 1)

                for t in range(TT):
                    r = P if t < TILES else NS
                    if t >= 2:
                        pe.wait_ge(s_kve, t - 1)
                    for k in range(KC):
                        ins = pe.matmul(pm[0:r, t % 2, :], hh[:, 1, k, t * P:t * P + r], wkv[:, k, :], start=(k == 0), stop=(k == KC - 1))
                    ins.then_inc(s_kvp, 1)
                    if t:
                        k_transposes(t - 1)
                pe.wait_ge(s_kn, TILES)
                pe.wait_ge(s_kve, TT)

                def product(n):
                    pe.wait_ge(s_wr[n % 4], 16 * (n // 4 + 1))
                    for k in range(KC):
                        for s, w in enumerate((512, 512, NS)):
                            ins = pe.matmul(ps[n % 2][:, s, 0:w], wr[:, n % 4, k, :], hh[:, 0, k, s * 512:s * 512 + w],
                                            start=(k == 0), stop=(k == KC - 1))
                    ins.then_inc(s_q, 1)

                for n in range(NR):
                    if n:
                        pe.wait_ge(s_e, n)
                    product(n)
                    pe.wait_ge(s_raw, n + 1)
                    for s, w in enumerate((512, 512, NS)):
                        ins = pe.matmul(ps[1 - n % 2][:, s, 0:w], rotp[:], raw[:, s * 512:s * 512 + w], start=True, stop=True)
                    ins.then_inc(s_rp, 1)
                for n in range(NR, NCH):
                    pe.wait_ge(s_e, max(n - 1, NR))
                    product(n)
                for b in range(NCH // 4):
                    if b == 0:
                        pe.wait_ge(s_e, NCH)
                    if b >= 2:
                        pe.wait_ge(s_qs, b - 1)
                    for i in range(4):
                        ins = pe.transpose(pm[0:NS, b % 2, i * P:(i + 1) * P], qsT[:, 4 * b + i, :], ident[:])
                    ins.then_inc(s_qt, 1)

            @block.scalar
            def _(act):
                for t in range(TT):
                    r = P if t < TILES else NS
                    act.wait_ge(s_kvp, t + 1)
                    if t >= 2:
                        act.wait_ge(s_kvs[t % 2], 16 * 5 * (t // 2))
                        act.wait_ge(s_kt, t - 1)
                    act.activation(kv[0:r, t % 2, :], pm[0:r, t % 2, :], ACT.Copy).then_inc(s_kve, 1)
                for n in range(NR):
                    act.wait_ge(s_q, n + 1)
                    if n:
                        act.wait_ge(s_e, n)
                    act.activation(raw[:, 0:NP].rearrange("p (s n) -> p s n", s=2), ps[n % 2][:, 0:2, :], ACT.Copy)
                    act.activation(raw[:, NP:NT], ps[n % 2][:, 2, 0:NS], ACT.Copy).then_inc(s_raw, 1)
                for n in range(NR, NCH):
                    g = group(n)
                    act.wait_ge(s_q, n + 1)
                    act.wait_ge(s_evs[n % 2], 16 * (n // 2))
                    act.activation(qsT[:, n], ps[n % 2][:, 2, 0:NS], ACT.Copy)
                    for half in range(2):
                        ins = act.activation(classes(ev[:, n % 2], g, half), tokens(ps[n % 2][:, half, :], g), ACT.Copy)
                    ins.then_inc(s_e, 1)
                for b in range(NCH // 4):
                    act.wait_ge(s_qt, b + 1)
                    act.activation(qs[:, b * 512:(b + 1) * 512], pm[0:NS, b % 2, :], ACT.Copy).then_inc(s_qs, 1)


def attend_units():
    out = []
    for g, d in enumerate(DIL):
        n = NP // d // P
        for b in range(TILES):
            before = n > 1 and b % n > 0
            out.append((g, b, 1 + before, 0 if before else (1 if n else 2)))
    return out


def phase_attend(nc, T):
    units = attend_units()
    U = len(units)
    with Pool_(nc, "att") as A:
        ident = A.sb("ident", [P, P])
        mk = A.sb("mk", [P, 3, 2 * P])
        q = A.sb("q", [HD, NG3, REP, NP])
        k = A.sb("k", [HD, NG3, NP])
        v = A.sb("v", [P, NG3, TILES, HD])
        S = A.sb("S", [P, 2, REP, 2 * P])
        PT = A.sb("PT", [P, 2, 2, REP * P])
        nm = A.sb("nm", [P, 2, REP])
        ml = A.sb("ml", [P, U, 2, REP])
        rl = A.sb("rl", [P, 2, REP])
        o = A.sb("o", [P, 4, REP * HD])
        ps_s = [A.ps(f"ps_s{j}", [P, REP, 2 * P]) for j in range(2)]
        ps_t = A.ps("ps_t", [P, 2, 512])
        ps_o = A.ps("ps_o", [P, 2, 512])
        s_nil = A.sem("waits_apart")
        s_k = A.sem("constants_loaded")
        s_qk = [A.sem(f"q_k_loaded{g}") for g in range(NG3)]
        s_v = [A.sem(f"v_loaded{g}") for g in range(NG3)]
        s_st = [A.sem(f"unit_stored{x}") for x in range(4)]
        s_ml = A.sem("sums_stored")
        slots = lambda first, *names: first + [x for u in range(U) for n in names
                                               for x in ([f"{n}{u}"] if n[0] in "tpro" else [f"{n}{u + 2}"] if u + 2 < U else [])]
        pe_ = Steps(A.sem("pe_steps"), slots(["s0", "s1"], "t", "s", "o"))
        dv_ = Steps(A.sem("dve_steps"), slots(["mask0", "max0", "neg0", "mask1", "max1", "neg1"], "pt", "rl", "mask", "max", "neg"))
        ac_ = Steps(A.sem("act_steps"), slots(["exp0", "exp1"], "o", "exp"))
        last = {g: max(u for u in range(U) if units[u][0] == g) for g in range(NG3)}

        def wait_back(eng, steps, name, u, back, h, apart=None):
            if u >= back:
                steps.wait(eng, f"{name}{u - back}", h, apart)
            else:
                steps.wait_before(eng, f"{name}{u - back + U}", h, apart)

        with nc.Block() as block:

            @block.sync
            def _(sp):
                sp.dma_start(mk[:], T["k_masks"].rearrange("m p n -> p m n")).then_inc(s_k, 16)
                sp.dma_start(ident[:], T["k_ident"]).then_inc(s_k, 16)
                for s in s_st:
                    sp.sem_inc(s, 16)
                sp.sem_inc(s_ml, 16)

                with sp.Fori(0, KVH) as h:
                    for u, (g, b, _, _) in enumerate(units):
                        ac_.wait(sp, f"o{u}", h, apart=s_nil)
                        sp.dma_start(T["o_d"][g * NP + b * P:g * NP + (b + 1) * P, ds(h * (REP * HD), REP * HD)], o[:, u % 4]).then_inc(s_st[u % 4], 16)
                    sp.dma_start(T["ml_d"].rearrange("(u p) x -> p u x", p=P)[:, :, ds(h * (2 * REP), 2 * REP)],
                                 ml[:].rearrange("p u a r -> p u (a r)")).then_inc(s_ml, 16)
                for s in s_st:
                    sp.wait_ge(s, 16 * (U // 4 * KVH + 1))
                sp.wait_ge(s_ml, 16 * (KVH + 1))

            @block.gpsimd
            def _(pool):
                def load(h, g):
                    if not isinstance(h, int):
                        pe_.wait_before(pool, f"s{last[g]}", h, apart=s_nil)
                    for d, t, at in ((ROT, "qr_d", 0), (PASS, "qp_d", ROT)):
                        pool.dma_start(q[at:at + d, g], T[t].rearrange("(g x) n -> g x n", g=NG3)[g][ds(h * (REP * d), REP * d), :]
                                       .rearrange("(r d) n -> d r n", r=REP)).then_inc(s_qk[g], 16)
                    pool.dma_start(k[:, g], T["k_d"][g].rearrange("h d n -> (h d) n")[ds(h * HD, HD), :]).then_inc(s_qk[g], 16)
                    if not isinstance(h, int):
                        pe_.wait_before(pool, f"o{last[g]}", h, apart=s_nil)
                    pool.dma_start(v[:, g], T["v_d"][g].rearrange("(b p) f -> p b f", p=P)[:, :, ds(h * HD, HD)]).then_inc(s_v[g], 16)

                for g in range(NG3):
                    load(0, g)
                with pool.Fori(1, KVH) as h:
                    for g in range(NG3):
                        load(h, g)
                for g in range(NG3):
                    pool.wait_ge(s_qk[g], 48 * KVH)
                    pool.wait_ge(s_v[g], 16 * KVH)

            @block.vector
            def _(dve):
                dv_.open(dve)
                dve.wait_ge(s_k, 32)
                with dve.Fori(0, KVH) as h:
                    def soft(u):
                        _, _, nk, m = units[u]
                        j, W = u % 2, nk * P
                        x = S[:, j, :, 0:W]
                        pe_.wait(dve, f"s{u}", h)
                        wait_back(dve, pe_, "t", u, 2, h)
                        dv_.step(f"mask{u}", dve.scalar_tensor_tensor(
                            out=x, in0=ps_s[j][:, :, 0:W], scalar=SCALE,
                            in1=mk[:, m:m + 1, 2 * P - W:2 * P].broadcast_to([P, REP, W]), op0=ALU.mult, op1=ALU.add))
                        dv_.wait(dve, f"mask{u}", h)
                        if u == 0:
                            dve.wait_ge(s_ml, h * 16 + 16)
                        dv_.step(f"max{u}", dve.tensor_reduce(ml[:, u, 0], x, AX, ALU.max))
                        dv_.wait(dve, f"max{u}", h)
                        wait_back(dve, ac_, "exp", u, 2, h)
                        dv_.step(f"neg{u}", dve.tensor_scalar(nm[:, j], ml[:, u, 0], -1.0, None, ALU.mult))

                    soft(0)
                    soft(1)
                    for u in range(U):
                        nk = units[u][2]
                        pe_.wait(dve, f"t{u}", h)
                        dv_.step(f"pt{u}", dve.tensor_copy(PT[:, u % 2, 0:nk], ps_t[:, 0:nk]))
                        ac_.wait(dve, f"exp{u}", h)
                        wait_back(dve, ac_, "o", u, 2, h)
                        dv_.step(f"rl{u}", dve.reciprocal(rl[:, u % 2], ml[:, u, 1]))
                        if u + 2 < U:
                            soft(u + 2)

            @block.scalar
            def _(act):
                ac_.open(act)
                with act.Fori(0, KVH) as h:
                    def exp(u):
                        j, W = u % 2, units[u][2] * P
                        dv_.wait(act, f"neg{u}", h)
                        for r in range(REP):
                            x = S[:, j, r, 0:W]
                            ins = act.activation(x, x, ACT.Exp, bias=nm[:, j, r:r + 1], accum_out=ml[:, u, 1, r:r + 1])
                        ac_.step(f"exp{u}", ins)

                    exp(0)
                    exp(1)
                    for u in range(U):
                        dv_.wait(act, f"rl{u}", h)
                        act.wait_ge(s_st[u % 4], h * (16 * U // 4) + 16 * (u // 4) + 16)
                        pe_.wait(act, f"o{u}", h)
                        for r in range(REP):
                            c = slice(r * HD, (r + 1) * HD)
                            ins = act.activation(o[:, u % 4, c], ps_o[:, u % 2, c], ACT.Copy, scale=rl[:, u % 2, r:r + 1])
                        ac_.step(f"o{u}", ins)
                        if u + 2 < U:
                            exp(u + 2)

            @block.tensor
            def _(pe):
                pe_.open(pe)
                pe.wait_ge(s_k, 32)
                with pe.Fori(0, KVH) as h:
                    def scores(u):
                        g, b, nk, _ = units[u]
                        pe.wait_ge(s_qk[g], h * 48 + 48)
                        wait_back(pe, dv_, "mask", u, 2, h, apart=s_nil)
                        for r in range(REP):
                            ins = pe.matmul(ps_s[u % 2][:, r, 0:nk * P], q[:, g, r, b * P:(b + 1) * P], k[:, g, (b + 1 - nk) * P:(b + 1) * P],
                                            start=True, stop=True)
                        pe_.step(f"s{u}", ins)

                    scores(0)
                    scores(1)
                    for u in range(U):
                        g, b, nk, _ = units[u]
                        ac_.wait(pe, f"exp{u}", h, apart=s_nil)
                        wait_back(pe, dv_, "pt", u, 1, h, apart=s_nil)
                        for x in range(nk):
                            for r in range(REP):
                                ins = pe.transpose(ps_t[:, x, r * P:(r + 1) * P], S[:, u % 2, r, x * P:(x + 1) * P], ident[:])
                        pe_.step(f"t{u}", ins)
                        if u + 2 < U:
                            scores(u + 2)
                        dv_.wait(pe, f"pt{u}", h, apart=s_nil)
                        pe.wait_ge(s_v[g], h * 16 + 16)
                        wait_back(pe, ac_, "o", u, 2, h, apart=s_nil)
                        for r in range(REP):
                            for x in range(nk):
                                ins = pe.matmul(ps_o[:, u % 2, r * HD:(r + 1) * HD], PT[:, u % 2, x, r * P:(r + 1) * P],
                                                v[:, g, b + 1 - nk + x, :], start=(x == 0), stop=(x == nk - 1))
                        pe_.step(f"o{u}", ins)


def attn_consts():
    one = np.float32
    out = {}
    rp = np.zeros((P, P), one)
    for i in range(P):
        b, r = divmod(i, ROT)
        if r < 8:
            rp[b * ROT + r + 8, i] = -1.0
        else:
            rp[b * ROT + r - 8, i] = 1.0
    out["k_rotp"] = rp
    half = ROT // 2
    inv = (one(500000.0) ** (-np.arange(half, dtype=one) * one(2.0) / one(ROT))).astype(one)
    pos = np.concatenate([np.arange(NP), np.full(NS, PAST)]).astype(one)
    ang = (pos[:, None] * inv[None, :]).astype(one)
    c, s = np.cos(ang).astype(one), np.sin(ang).astype(one)
    out["k_cos"] = np.ascontiguousarray(np.tile(c.T, (P // half, 1)))
    out["k_sin"] = np.ascontiguousarray(np.tile(s.T, (P // half, 1)))
    ct = np.zeros((NTP, 2, half), one)
    ct[:NT, 0], ct[:NT, 1] = c, s
    out["k_ctok"] = np.ascontiguousarray(ct.reshape(TT, P, 2, half).transpose(1, 0, 2, 3))
    i = np.arange(P)
    m = np.full((3, P, 2 * P), NEG, one)
    m[0, :, 0:P][i[None, :] >= i[:, None]] = 0.0
    causal = i[None, :] <= i[:, None]
    m[0, :, P:][causal] = 0.0
    m[1, :, P:][causal] = 0.0
    m[2, :, P:][causal & (i[None, :] // 64 == i[:, None] // 64)] = 0.0
    out["k_masks"] = m
    return out


def phase_sample_attend(nc, T):
    NK = [PAST // d + 1 if PAST // d < 128 else 129 for d in DIL]
    OFF = [sum(NK[:g]) for g in range(NG3)]
    ALL = sum(NK)
    GR = [slice(OFF[g], OFF[g] + NK[g]) for g in range(NG3)]
    with Pool_(nc, "satt") as A:
        ident = A.sb("ident", [P, P])
        q = A.sb("q", [P, NG3, HD])
        K = A.sb("K", [P, ALL, HD])
        V = A.sb("V", [P, ALL, HD])
        s = A.sb("s", [P, ALL])
        m = A.sb("m", [P, NG3])
        nm = A.sb("nm", [P, NG3])
        l = A.sb("l", [P, NG3])
        ls = A.sb("ls", [P, NG3])
        mx = A.sb("mx", [P, 4])
        w = A.sb("w", [P, NG3])
        rl = A.sb("rl", [P, NG3])
        z = A.sb("z", [P, HD])
        zr = A.sb("zr", [NS, D])
        zT = A.sb("zT", [P, KC, NS])
        ps = A.ps("ps", [P, KC, NS])
        s_q = A.sem("q_loaded")
        s_K = A.sem("keys_loaded")
        s_V = A.sem("values_loaded")
        s_d = A.sem("dve_steps")
        s_nm = A.sem("stage_ended")
        s_a = A.sem("act_steps")
        s_z = A.sem("z_stored")
        s_zl = A.sem("z_rows")
        s_t = A.sem("z_transposed")
        s_c = A.sem("zT_ready")
        s_o = A.sem("zT_stored")
        with nc.Block() as block:

            def rows(eng, dst, cache, new, sem):
                for g, d in enumerate(DIL):
                    n = NK[g] - 1
                    src = T[cache].rearrange("x (k s) d -> x k s d", s=d)[:, PAST // d - n:, 0, :]
                    for r in range(REP):
                        eng.dma_start(dst[r::REP, OFF[g]:OFF[g] + n], src).then_inc(sem, 16)
                        eng.dma_start(dst[r::REP, OFF[g] + n],
                                      T[new].rearrange("b (h d) -> (b h) d", h=KVH)).then_inc(sem, 16)

            @block.sync
            def _(sp):
                sp.dma_start(ident[:], T["k_ident"]).then_inc(s_q, 16)
                for b in range(NS):
                    for at, d, base in ((0, ROT, 0), (ROT, PASS, QR)):
                        sp.dma_start(q[b * H:(b + 1) * H, :, at:at + d],
                                     T["qs_d"][b, base:base + NG3 * H * d].rearrange("(g h d) -> h g d", g=NG3, h=H)).then_inc(s_q, 16)
                rows(sp, K, "cache_k", "k_sample", s_K)
                rows(sp, V, "cache_v", "v_sample", s_V)
                sp.wait_ge(s_nm, 3)
                sp.dma_start(T["zs_d"].rearrange("b (h d) -> (b h) d", h=H), z[:]).then_inc(s_z, 16)
                sp.wait_ge(s_z, 16)
                sp.dma_start(zr[:], T["zs_d"]).then_inc(s_zl, 16)
                sp.wait_ge(s_c, 1)
                sp.dma_start(T["z_d"].rearrange("(c p) n -> p c n", p=P)[:, :, NP:NT], zT[:]).then_inc(s_o, 16)
                sp.wait_ge(s_o, 16)

            @block.scalar
            def _(act):
                act.wait_ge(s_nm, 1)
                for g in range(NG3):
                    act.activation(s[:, GR[g]], s[:, GR[g]], ACT.Exp, bias=nm[:, g:g + 1], accum_out=l[:, g:g + 1]).then_inc(s_a, 1)
                act.wait_ge(s_a, 3)
                act.activation(ls[:], l[:], ACT.Ln).then_inc(s_a, 1)
                act.wait_ge(s_nm, 2)
                act.activation(w[:], ls[:], ACT.Exp).then_inc(s_a, 1)

            @block.vector
            def _(dve):
                link = Chain(dve, s_d)
                dve.wait_ge(s_q, 16 * (1 + 2 * NS))
                dve.wait_ge(s_K, 16 * 2 * REP * NG3)
                for g in range(NG3):
                    link(dve.tensor_tensor(K[:, GR[g]], K[:, GR[g]], q[:, g:g + 1].broadcast_to([P, NK[g], HD]), ALU.mult))
                link(dve.tensor_reduce(s[:], K[:], AX, ALU.add))
                link(dve.tensor_scalar(s[:], s[:], SCALE, None, ALU.mult))
                for g in range(NG3):
                    ins = dve.tensor_reduce(m[:, g:g + 1], s[:, GR[g]], AX, ALU.max)
                    link(ins)
                dve.tensor_scalar(nm[:], m[:], -1.0, None, ALU.mult).then_inc(s_nm, 1)
                dve.wait_ge(s_a, 4)
                link(dve.tensor_tensor(ls[:], ls[:], m[:], ALU.add))
                link(dve.tensor_reduce(mx[:, 0:1], ls[:], AX, ALU.max))
                dve.tensor_scalar(ls[:], ls[:], mx[:, 0:1], None, ALU.subtract).then_inc(s_nm, 1)
                link(dve.reciprocal(rl[:], l[:]))
                dve.wait_ge(s_a, 5)
                link(dve.tensor_reduce(mx[:, 1:2], w[:], AX, ALU.add))
                link(dve.reciprocal(mx[:, 2:3], mx[:, 1:2]))
                link(dve.tensor_scalar(w[:], w[:], mx[:, 2:3], None, ALU.mult))
                link(dve.tensor_tensor(w[:], w[:], rl[:], ALU.mult))
                for g in range(NG3):
                    link(dve.tensor_scalar(s[:, GR[g]], s[:, GR[g]], w[:, g:g + 1], None, ALU.mult))
                dve.wait_ge(s_V, 16 * 2 * REP * NG3)
                link(dve.tensor_tensor(V[:], V[:], s[:].rearrange("p (k o) -> p k o", o=1).broadcast_to([P, ALL, HD]), ALU.mult))
                dve.tensor_reduce(z[:], V[:].rearrange("p k d -> p d k"), AX, ALU.add).then_inc(s_nm, 1)
                dve.wait_ge(s_t, 1)
                dve.tensor_copy(zT[:], ps[:]).then_inc(s_c, 1)

            @block.tensor
            def _(pe):
                pe.wait_ge(s_q, 16 * (1 + 2 * NS))
                pe.wait_ge(s_zl, 16)
                for k in range(KC):
                    ins = pe.transpose(ps[:, k, :], zr[:, k * P:(k + 1) * P], ident[0:NS, 0:NS])
                ins.then_inc(s_t, 1)


def phase_attend_sum(nc, T):
    with Pool_(nc, "asum") as A:
        ident = A.sb("ident", [P, P])
        O = A.sb("O", [P, 2, NG3, D])
        ml = A.sb("ml", [P, 2, NG3, KVH, 2, REP])
        L = A.sb("L", [P, 2, NG3, H])
        mx = A.sb("mx", [P, 2, H])
        zT = A.sb("zT", [P, 2, KC * P])
        ps = [A.ps(f"ps{j}", [P, 2, 512]) for j in range(2)]
        s_nil = A.sem("waits_apart")
        s_k = A.sem("constants_loaded")
        s_ld = [A.sem(f"tile_loaded{j}") for j in range(2)]
        s_st = [A.sem(f"z_stored{j}") for j in range(2)]
        both = lambda *names: [f"{x}{j}" for j in range(2) for x in names]
        dv_ = Steps(A.sem("dve_steps"), both("lse", "mx", "sub", "sum", "rcp", "w", "m0", "m2", "a1", "a2"))
        ac_ = Steps(A.sem("act_steps"), both("ln", "exp", "zT"))
        po_ = Steps(A.sem("pool_steps"), both("m1"))
        pe_ = Steps(A.sem("pe_steps"), both("t"))
        bc = lambda x, n=HD: x.rearrange("p (h o) -> p h o", o=1).broadcast_to([P, x.shape[1], n])
        heads = lambda x: x.rearrange("p (h d) -> p h d", h=H)
        over = lambda x: x.rearrange("p (o h) -> p o h", o=1).broadcast_to([P, NG3, H])
        with nc.Block() as block:

            @block.sync
            def _(sp):
                sp.dma_start(ident[:], T["k_ident"]).then_inc(s_k, 16)
                with sp.Fori(0, TILES // 2) as i:
                    for j in range(2):
                        pe_.wait_before(sp, f"t{j}", i, apart=s_nil)
                        for g, d in enumerate(DIL):
                            n = P // d
                            for src, dst in ((T["o_d"], O[:, j, g, :]), (T["ml_d"], ml[:, j, g].rearrange("p h a r -> p (h a r)"))):
                                src = src[g * NP:(g + 1) * NP, :].rearrange("(c n) f -> n c f", c=d)
                                sp.dma_start(dst, src[ds(i * (2 * n) + j * n, n)]).then_inc(s_ld[j], 16)

            @block.gpsimd
            def _(pool):
                po_.open(pool)
                with pool.Fori(0, TILES // 2) as i:
                    for j in range(2):
                        pool.wait_ge(s_ld[j], i * 96 + 96)
                        dv_.wait(pool, f"w{j}", i, apart=s_nil)
                        o = heads(O[:, j, 1])
                        po_.step(f"m1{j}", pool.tensor_tensor(o, o, bc(L[:, j, 1]), ALU.mult))

            @block.scalar
            def _(act):
                ac_.open(act)
                for s in s_st:
                    act.sem_inc(s, 16)
                with act.Fori(0, TILES // 2) as i:
                    for j in range(2):
                        act.wait_ge(s_ld[j], i * 96 + 96)
                        (dv_.wait_before)(act, f"m2{j}", i)
                        po_.wait_before(act, f"m1{j}", i)
                        ac_.step(f"ln{j}", act.activation(L[:, j].rearrange("p g (h r) -> p g h r", h=KVH), ml[:, j, :, :, 1, :], ACT.Ln))
                        dv_.wait(act, f"sub{j}", i)
                        ac_.step(f"exp{j}", act.activation(L[:, j], L[:, j], ACT.Exp))
                        pe_.wait(act, f"t{j}", i)
                        act.wait_ge(s_st[j], i * 16 + 16)
                        ac_.step(f"zT{j}", act.activation(zT[:, j].rearrange("p (b n) -> p b n", b=2), ps[j][:], ACT.Copy))
                        ac_.wait(act, f"zT{j}", i, apart=s_nil)
                        act.dma_start(T["z_d"].rearrange("(k p) n -> p k n", p=P)[:, :, ds(i * (2 * P) + j * P, P)],
                                      zT[:, j].rearrange("p (k n) -> p k n", k=KC)).then_inc(s_st[j], 16)
                for j in range(2):
                    act.wait_ge(s_st[j], 16 * TILES // 2 + 16)

            @block.vector
            def _(dve):
                dv_.open(dve)
                with dve.Fori(0, TILES // 2) as i:
                    for j in range(2):
                        def op(name, ins, then=True):
                            dv_.step(f"{name}{j}", ins)
                            if then:
                                dv_.wait(dve, f"{name}{j}", i)

                        Lj = L[:, j]
                        L4 = Lj.rearrange("p g (h r) -> p g h r", h=KVH)
                        ac_.wait(dve, f"ln{j}", i)
                        dve.wait_ge(s_ld[j], i * 96 + 96)
                        op("lse", dve.tensor_tensor(L4, L4, ml[:, j, :, :, 0, :], ALU.add))
                        op("mx", dve.tensor_reduce(mx[:, j], Lj.rearrange("p g h -> p h g"), AX, ALU.max))
                        op("sub", dve.tensor_tensor(Lj, Lj, over(mx[:, j]), ALU.subtract))
                        ac_.wait(dve, f"exp{j}", i)
                        op("sum", dve.tensor_reduce(mx[:, j], Lj.rearrange("p g h -> p h g"), AX, ALU.add))
                        op("rcp", dve.reciprocal(mx[:, j], mx[:, j]))
                        op("w", dve.tensor_tensor(Lj, Lj, over(mx[:, j]), ALU.mult))
                        for g in (0, 2):
                            o = heads(O[:, j, g])
                            op(f"m{g}", dve.tensor_tensor(o, o, bc(L[:, j, g]), ALU.mult), g == 2)
                        op("a1", dve.tensor_tensor(O[:, j, 0], O[:, j, 0], O[:, j, 2], ALU.add))
                        po_.wait(dve, f"m1{j}", i)
                        op("a2", dve.tensor_tensor(O[:, j, 0], O[:, j, 0], O[:, j, 1], ALU.add), False)

            @block.tensor
            def _(pe):
                pe_.open(pe)
                pe.wait_ge(s_k, 16)
                with pe.Fori(0, TILES // 2) as i:
                    for j in range(2):
                        dv_.wait(pe, f"a2{j}", i, apart=s_nil)
                        ac_.wait_before(pe, f"zT{j}", i, apart=s_nil)
                        for k in range(KC):
                            ins = pe.transpose(ps[j][:, k // 4, (k % 4) * P:(k % 4 + 1) * P], O[:, j, 0, k * P:(k + 1) * P], ident[:])
                        pe_.step(f"t{j}", ins)


SCRATCH = {
    "ada_d": (4, NC, 3 * D), "kva_d": (NC, 2 * D), "x0_d": (NTP, D), "x2_d": (NTP, D),
    "proj_d": (6, D, NT), "bonus_d": (D, NT), "sv_d": (6, NS, D), "y_d": (D, NT), "ys_d": (NS, D),
    "z_d": (D, ZC), "x1_d": (NTP, D), "xm_d": (NTP, D), "ysl_d": (NBLK * P, D),
    "qr_d": (QR, NP), "qp_d": (QP, NP), "qs_d": (NS, QR + QP), "k_d": (NG3, KVH, HD, NP), "v_d": (NG3, NP, KVH * HD),
    "o_d": (NG3 * NP, D), "ml_d": (NG3 * NP, 2 * H), "zs_d": (NS, D),
}
OUTPUTS = [
    ("y_prompt", (NP, D), (1, NP, D)), ("y_sample", (NS, D), (NS, 1, D)),
    ("wkv_prompt", (H, HD, HD), (1, 1, H, HD, HD)), ("shift_prompt", (D,), (1, 1, D)),
    ("k_prompt", (NP, KVH * HD), (1, NP, KVH, HD)), ("v_prompt", (NP, KVH * HD), (1, NP, KVH, HD)),
    ("wkv_sample", (NS * H, HD, HD), (1, NS, H, HD, HD)), ("shift_sample", (NS, D), (1, NS, D)),
    ("k_sample", (NS, KVH * HD), (NS, 1, KVH, HD)), ("v_sample", (NS, KVH * HD), (NS, 1, KVH, HD)),
]


def yoco_step(nc, T):
    for name, shape in SCRATCH.items():
        T[name] = nc.dram_tensor("t_" + name, shape, F32, kind="Internal").ap()
    for name, shape, dt in (("table_d", ((NBLK + 2) * P, 1), I32), ("slot_d", (P, 2 * TT), I32),
                            ("gate_d", (P, 2 * TT), F32), ("blk_d", (1, 2 + NBLK), I32)):
        T[name] = [nc.dram_tensor(f"t_{name}{i}", shape, dt, kind="Internal").ap() for i in range(2)]
    T["x_in"] = [T["x0_d"], T["x2_d"]]
    T["w_o"] = [T["rwkv_w_o"], T["w_o_attn"]]
    phase_init(nc, T)
    phase_ada(nc, T)
    phase_mix(nc, T)
    phase_wkv(nc, T)
    phase_sample(nc, T)
    phase_gn(nc, T)
    phase_post(nc, T, 0)
    phase_moe(nc, T, 0)
    phase_combine(nc, T, 0)
    phase_qkv(nc, T)
    phase_attend(nc, T)
    phase_attend_sum(nc, T)
    phase_sample_attend(nc, T)
    phase_post(nc, T, 1)
    phase_moe(nc, T, 1)
    phase_combine(nc, T, 1)


def laid_out(inp):
    f = lambda name: np.asarray(inp[name])
    chunks = lambda a: a.reshape(KC, P)
    vec = lambda name: chunks(f(name).reshape(D))
    out = {"x_prompt": f("x_prompt")[0], "x_sample": f("x_sample")[:, 0], "state_wkv": f("state_wkv").reshape(NS * H, HD, HD),
           "state_shift": f("state_shift")[0], "c_prompt": f("c_prompt"), "c_sample": f("c_sample")}
    for name in ("cache_k", "cache_v"):
        out[name] = f(name).transpose(0, 2, 1, 3).reshape(NS * KVH, PAST, HD)
    for name in ("ada_w", "ada_b", "rwkv_w_rkv", "w_kv", "kv_ada_w", "router_w", "moe_w_in", "moe_w_out"):
        out[name] = f(name)
    out["kv_ada_b"] = f("kv_ada_b")[None]
    out["router_b"] = f("router_b")[None]
    for name in ("rwkv_w1", "rwkv_w2", "rwkv_a1", "rwkv_a2", "rwkv_g1", "rwkv_g2", "rwkv_w_o", "w_o_attn"):
        out[name] = f(name)[0]
    out["ln_gb"] = np.stack([f("ln_g").reshape(4, D), f("ln_b").reshape(4, D)], 1)
    out["mu_c"] = f("rwkv_mu").reshape(6, KC, P).transpose(2, 0, 1)
    out["wkv_par"] = np.stack([vec("rwkv_" + n) for n in ("w0", "a0", "k_k", "k_a", "r_k")], 2)
    out["gn_par"] = np.stack([vec("rwkv_lnx_g"), vec("rwkv_lnx_b")], 0).transpose(2, 0, 1)
    wq = f("w_q").reshape(D, NG3 * H, HD)
    out["w_q"] = np.concatenate([wq[:, :, :ROT].reshape(D, QR), wq[:, :, ROT:].reshape(D, QP)], 1)
    return out


def kernel(**inputs):
    import concourse.bacc as _bacc
    from concourse.bass_utils import run_bass_kernel_spmd as _run

    nc = _bacc.Bacc("TRN2", target_bir_lowering=False, num_devices=1)
    arrays, T = {}, {}
    for name, a in {**laid_out(inputs), **wkv_consts(), **post_consts(), **attn_consts()}.items():
        a = np.ascontiguousarray(a)
        arrays[f"in_{name}_dram"] = a
        T[name] = nc.dram_tensor(f"in_{name}_dram", a.shape, mybir.dt.from_np(a.dtype), kind="ExternalInput").ap()
    for i, (name, shape, _) in enumerate(OUTPUTS):
        T[name] = nc.dram_tensor(f"out_{i}_dram", shape, F32, kind="ExternalOutput").ap()
    yoco_step(nc, T)
    nc.compile()
    r = _run(nc, [arrays], core_ids=[0])
    return tuple(r.results[0][f"out_{i}_dram"].reshape(shape) for i, (_, _, shape) in enumerate(OUTPUTS))
```

```python
from contextlib import ExitStack

import numpy as np

import concourse.bass as bass
from concourse import mybir

F32 = mybir.dt.float32
I32 = mybir.dt.int32
U32 = mybir.dt.uint32
ALU = mybir.AluOpType
ACT = mybir.ActivationFunctionType
AX = mybir.AxisListType.X
ds = bass.ds

P = 128
D = 1024
KC = D // P
NP = 1024
NS = 8
NT = NP + NS
TILES = NP // P
NC = NS + 1
SL = 344
H, HD = 16, 64
CH = 64
GN_EPS = 64e-5
LN_EPS = 1e-5
ALPHA = 4.0 ** 0.25
assert 3 * SL == NT


class Pool_:

    def __init__(self, nc, tag):
        self.nc, self.tag, self.ctx, self.sems = nc, tag, ExitStack(), []

    def __enter__(self):
        self.ctx.__enter__()
        return self

    def __exit__(self, *a):
        self.nc.clear_and_free_semaphores(self.sems)
        self.nc.all_engine_barrier()
        return self.ctx.__exit__(*a)

    def sb(self, name, shape, dt=F32):
        return self.ctx.enter_context(self.nc.sbuf_tensor(f"{self.tag}_{name}", shape, dt))

    def ps(self, name, shape, dt=F32):
        return self.ctx.enter_context(self.nc.psum_tensor(f"{self.tag}_{name}", shape, dt))

    def sem(self, name):
        self.sems.append(self.nc.alloc_semaphore(f"{self.tag}_{name}"))
        return self.sems[-1]


class Chain:

    def __init__(self, eng, sem):
        self.eng, self.sem, self.base, self.n = eng, sem, 0, 0

    def __call__(self, ins):
        ins.then_inc(self.sem, 1)
        self.n += 1
        self.eng.wait_ge(self.sem, self.base + self.n)


def phase_ada(nc, T):
    SLOTS = 6
    with Pool_(nc, "ada") as A:
        ident = A.sb("ident", [P, P])
        c9 = A.sb("c9", [NC, D])
        sg = A.sb("sg", [NC, D])
        cT = A.sb("cT", [P, KC, NC])
        w = A.sb("w", [P, SLOTS, KC, 512])
        bias = A.sb("bias", [NC, 3 * D])
        row = A.sb("row", [NC, 3 * D])
        ps_c = A.ps("ps_c", [P, KC, 16])
        ps_o = A.ps("ps_o", [NC, SLOTS, 512])
        z = A.sb("z", [P, D])
        s_z = A.sem("zeros_ready")
        s_x = A.sem("x_copied")
        s_c = A.sem("c_loaded")
        s_sig = A.sem("sigmoid_done")
        s_silu = A.sem("silu_done")
        s_tr = A.sem("c_transposed")
        s_cT = A.sem("cT_ready")
        s_w = [A.sem(f"w_loaded{j}") for j in range(SLOTS)]
        s_mm = A.sem("slice_multiplied")
        s_ev = A.sem("banks_free")
        s_bias = A.sem("bias_loaded")
        s_one = A.sem("bias_plus_one")
        s_out = A.sem("rows_stored")
        wv = T["ada_w"].rearrange("l s (k p) n -> (l s) p k n", p=P)
        bv = T["ada_b"].rearrange("l s n -> (l s) n")
        kvw = T["kv_ada_w"].rearrange("(k p) n -> p k n", p=P)
        NM = 4
        with nc.Block() as block:

            @block.sync
            def _(sp):
                sp.dma_start(c9[0:NS, :], T["c_sample"]).then_inc(s_c, 16)
                sp.dma_start(c9[NS:NC, :], T["c_prompt"]).then_inc(s_c, 16)
                sp.dma_start(ident[:], T["k_ident"]).then_inc(s_c, 16)
                for j in range(SLOTS):
                    sp.dma_start(w[:, j], wv[0, :, :, j * 512:(j + 1) * 512]).then_inc(s_w[j], 16)
                with sp.Fori(0, NM - 1) as m:
                    for j in range(SLOTS):
                        sp.wait_ge(s_mm, m * SLOTS + (j + 1))
                        sp.dma_start(w[:, j], wv[ds(m + 1, 1), :, :, j * 512:(j + 1) * 512]
                                     .rearrange("o p k n -> (o p) k n")).then_inc(s_w[j], 16)
                for j in range(4):
                    sp.wait_ge(s_mm, (NM - 1) * SLOTS + j + 1)
                    sp.dma_start(w[:, j], kvw[:, :, j * 512:(j + 1) * 512]).then_inc(s_w[j], 16)

            @block.gpsimd
            def _(pool):
                pool.memset(z[:], 0.0).then_inc(s_z, 1)
                pool.wait_ge(s_c, 48)
                pool.dma_start(T["x_in"][0][0:NP, :], T["x_prompt"]).then_inc(s_x, 16)
                pool.dma_start(T["x_in"][0][NP:NT, :], T["x_sample"]).then_inc(s_x, 16)
                pool.wait_ge(s_z, 1)
                pool.dma_start(T["x_in"][0][NT:, :], z[0:9 * P - NT, :]).then_inc(s_x, 16)
                over = T["ysl_d"][33 * P:, :].rearrange("(b p) n -> p b n", p=P)
                pool.dma_start(over, z[:].rearrange("p (o n) -> p o n", o=1).broadcast_to([P, over.shape[1], D])).then_inc(s_x, 16)
                pool.wait_ge(s_x, 64)

            @block.scalar
            def _(act):
                act.wait_ge(s_c, 48)
                act.activation(sg[:], c9[:], ACT.Sigmoid).then_inc(s_sig, 1)
                act.dma_start(bias[:], bv[0:1, :].broadcast_to([NC, 3 * D])).then_inc(s_bias, 16)
                with act.Fori(0, NM - 1) as m:
                    act.wait_ge(s_ev, m * SLOTS + 2 * SLOTS)
                    act.dma_start(T["ada_d"][ds(m, 1)].rearrange("o a n -> (o a) n"), row[:]).then_inc(s_out, 16)
                    act.dma_start(bias[:], bv[ds(m + 1, 1), :].broadcast_to([NC, 3 * D])).then_inc(s_bias, 16)
                act.wait_ge(s_ev, (NM + 1) * SLOTS)
                act.dma_start(T["ada_d"][NM - 1], row[:]).then_inc(s_out, 16)
                act.dma_start(bias[:, 0:2 * D], T["kv_ada_b"].broadcast_to([NC, 2 * D])).then_inc(s_bias, 16)
                act.wait_ge(s_ev, (NM + 1) * SLOTS + 4)
                act.dma_start(T["kva_d"], row[:, 0:2 * D]).then_inc(s_out, 16)
                act.wait_ge(s_out, 16 * (NM + 1))

            @block.vector
            def _(dve):
                dve.wait_ge(s_sig, 1)
                dve.tensor_tensor(sg[:], sg[:], c9[:], ALU.mult).then_inc(s_silu, 1)
                dve.wait_ge(s_tr, 1)
                dve.tensor_copy(cT[:], ps_c[:, :, 0:NC]).then_inc(s_cT, 1)
                dve.sem_inc(s_ev, SLOTS)

                def slices(m, n):
                    dve.wait_ge(s_bias, m * 16 + 16)
                    dve.tensor_scalar(bias[:, D:2 * D], bias[:, D:2 * D], 1.0, None, ALU.add).then_inc(s_one, 1)
                    for j in range(n):
                        dve.wait_ge(s_mm, m * SLOTS + (j + 1))
                        if j == 0:
                            if not isinstance(m, int) or m:
                                dve.wait_ge(s_out, m * 16)
                            dve.wait_ge(s_one, m + 1)
                        c = slice(j * 512, (j + 1) * 512)
                        ins = dve.tensor_tensor(row[:, c], ps_o[:, j], bias[:, c], ALU.add)
                        ins.then_inc(s_ev, 1)

                slices(0, SLOTS)
                with dve.Fori(1, NM) as m:
                    slices(m, SLOTS)
                slices(NM, 4)

            @block.tensor
            def _(pe):
                pe.wait_ge(s_silu, 1)
                pe.wait_ge(s_c, 48)
                for k in range(KC):
                    ins = pe.transpose(ps_c[:, k, 0:NC], sg[:, k * P:(k + 1) * P], ident[0:NC, 0:NC])
                ins.then_inc(s_tr, 1)
                pe.wait_ge(s_cT, 1)

                def slices(m, n):
                    for j in range(n):
                        pe.wait_ge(s_w[j], m * 16 + 16)
                        pe.wait_ge(s_ev, m * SLOTS + (j + 1))
                        for k in range(KC):
                            ins = pe.matmul(ps_o[:, j], cT[:, k, :], w[:, j, k, :], start=(k == 0), stop=(k == KC - 1))
                        ins.then_inc(s_mm, 1)

                with pe.Fori(0, NM) as m:
                    slices(m, SLOTS)
                slices(NM, 4)


def phase_mix(nc, T):
    with Pool_(nc, "mix") as A:
        ident = A.sb("ident", [P, P])
        ada = A.sb("ada", [NC, 2 * D])
        mod = A.sb("mod", [P, 2, KC, NC])
        hT = A.sb("hT", [P, KC, 1 + NT])
        xx = A.sb("xx", [P, KC, NT])
        mix = A.sb("mix", [P, 2, KC, NT])
        x = mix[:, :, :, :].rearrange("p a k n -> p (a k n)")[:, 0:TILES * D].rearrange("p (t n) -> p t n", t=TILES)
        xs = A.sb("xs", [NS, D])
        sh0 = A.sb("sh0", [NS, D])
        mu = A.sb("mu", [P, 6, KC])
        wr = A.sb("wr", [P, 4, KC, P])
        w1 = A.sb("w1", [P, KC, 160])
        w2 = A.sb("w2", [P, D])
        g2b = A.sb("g2b", [32, D])
        hid = A.sb("hid", [P, NT])
        hid2 = A.sb("hid2", [32, NT])
        ev = A.sb("ev", [P, 2, NT])
        ps = [A.ps(f"ps{i}", [P, 3, 512]) for i in range(2)]
        pm = A.ps("pm", [P, 2, 512])
        s_ld = A.sem("small_loaded")
        s_x = A.sem("x_loaded")
        s_mt = A.sem("mod_transposed")
        s_m = A.sem("mod_ready")
        s_z = A.sem("dve_chain")
        s_xt = A.sem("x_transposed")
        s_h = A.sem("h_half_ready")
        s_xx = A.sem("xx_ready")
        s_sh = A.sem("shift_ready")
        s_mx = A.sem("mix_ready")
        s_wr = [A.sem(f"wr_loaded{i}") for i in range(4)]
        s_w1 = A.sem("w1_loaded")
        s_w2 = A.sem("w2_loaded")
        s_g = A.sem("group_done")
        s_e = A.sem("group_evacuated")
        s_evf = [A.sem(f"ev_stored{i}") for i in range(2)]
        s_st = A.sem("shift_stored")
        with nc.Block() as block:
            wv = T["rwkv_w_rkv"].rearrange("a m (k p) n -> (a m) p k n", p=P)

            G_R = 0
            G_W = 24
            G_A = G_W + 9
            G_G = G_A + 9
            G_END = G_G + 10
            LORA = [(G_W, "rwkv_w1", "rwkv_w2", 64, ACT.Tanh, 3), (G_A, "rwkv_a1", "rwkv_a2", 64, ACT.Copy, 4),
                    (G_G, "rwkv_g1", "rwkv_g2", 160, ACT.Sigmoid, 5)]

            @block.sync
            def _(sp):
                sp.dma_start(ident[:], T["k_ident"]).then_inc(s_ld, 16)
                sp.dma_start(ada[:], T["ada_d"][0, :, 0:2 * D]).then_inc(s_ld, 16)
                sp.dma_start(xs[:], T["x_sample"]).then_inc(s_ld, 16)
                sp.dma_start(sh0[:], T["state_shift"]).then_inc(s_ld, 16)
                sp.dma_start(mu[:], T["mu_c"]).then_inc(s_ld, 16)
                sp.dma_start(x, T["x_prompt"].rearrange("(t p) n -> p t n", p=P)).then_inc(s_x, 16)
                for j in range(4):
                    sp.dma_start(wr[:, j], wv[0, :, :, j * P:(j + 1) * P]).then_inc(s_wr[j], 16)
                for f in range(1, 6):
                    for j in range(4):
                        sp.wait_ge(s_g, 4 * (f - 1) + j + 1)
                        o = (f % 2) * 4 + j
                        sp.dma_start(wr[:, j], wv[f // 2, :, :, o * P:(o + 1) * P]).then_inc(s_wr[j], 16)
                for n, (g0, a1, a2, wid, _, _) in enumerate(LORA):
                    if n:
                        sp.wait_ge(s_g, g0)
                    sp.dma_start(w1[:, :, 0:wid], T[a1].rearrange("(k p) n -> p k n", p=P)).then_inc(s_w1, 16)
                    sp.dma_start(w2[0:min(wid, P), :], T[a2][0:min(wid, P), :]).then_inc(s_w2, 16)
                    if wid > P:
                        sp.dma_start(g2b[:], T[a2][P:wid, :]).then_inc(s_w2, 16)

            def outputs():
                for m in range(3):
                    for o in range(KC):
                        yield G_R + 8 * m + o, m, o
                for g0, first, m in ((G_W, 1, 3), (G_A, 1, 4), (G_G, 2, 5)):
                    for o in range(KC):
                        yield g0 + first + o, m, o

            @block.gpsimd
            def _(pool):
                for n, (g, m, o) in enumerate(outputs()):
                    pool.wait_ge(s_e, g + 1 + 2)
                    pool.dma_start(T["proj_d"][m, o * P:(o + 1) * P, :], ev[:, n % 2]).then_inc(s_evf[n % 2], 16)
                pool.wait_ge(s_sh, 1)
                pool.dma_start(T["shift_prompt"].rearrange("(k p) -> p k", p=P), hT[:, :, NP],
                               allow_slow_non_contiguous=True).then_inc(s_st, 16)
                pool.dma_start(T["shift_sample"], xs[:]).then_inc(s_st, 16)
                pool.wait_ge(s_st, 32)
                pool.wait_ge(s_evf[0], 16 * 24)
                pool.wait_ge(s_evf[1], 16 * 24)

            @block.vector
            def _(dve):
                link = Chain(dve, s_z)
                link(dve.memset(hT[:, :, 0:1], 0.0))
                dve.wait_ge(s_mt, 1)
                dve.tensor_copy(mod[:].rearrange("p a k c -> p (a k) c"),
                                pm[:, 0, 0:2 * KC * 16].rearrange("p (a c) -> p a c", c=16)[:, :, 0:NC]).then_inc(s_m, 1)
                dve.wait_ge(s_m, 1)
                for u in range(2 * KC):
                    k, half = divmod(u, 2)
                    dve.wait_ge(s_xt, u + 1)
                    dve.tensor_scalar(hT[:, k, 1 + half * 512:1 + half * 512 + 512], ps[u % 2][:, 0, :],
                                      mod[:, 1, k, NS:NC], mod[:, 0, k, NS:NC], ALU.mult, ALU.add).then_inc(s_h, 1)
                dve.wait_ge(s_xt, 2 * KC + 1)
                hs = hT[:, :, 1 + NP:1 + NT]
                v = pm[:, 0, 0:KC * NS].rearrange("p (k s) -> p k s", s=NS)
                link(dve.tensor_tensor(hs, v, mod[:, 1, :, 0:NS], ALU.mult))
                link(dve.tensor_tensor(hs, hs, mod[:, 0, :, 0:NS], ALU.add))
                dve.tensor_tensor(xx[:, :, NP:NT], pm[:, 1, 0:KC * NS].rearrange("p (k s) -> p k s", s=NS), hs,
                                  ALU.subtract).then_inc(s_xx, 1)
                dve.wait_ge(s_h, 2 * KC)
                for k in range(KC):
                    dve.tensor_tensor(xx[:, k, 0:NP], hT[:, k, 0:NP], hT[:, k, 1:1 + NP], ALU.subtract).then_inc(s_xx, 1)
                link(dve.tensor_tensor(xs[:], xs[:], ada[0:NS, D:2 * D], ALU.mult))
                dve.tensor_tensor(xs[:], xs[:], ada[0:NS, 0:D], ALU.add).then_inc(s_sh, 1)
                dve.wait_ge(s_xx, KC + 1)
                for m, row in enumerate((0, 2, 3, 1, 4, 5)):
                    if m >= 2:
                        dve.wait_ge(s_g, (8, 16, 24, G_W + 1)[m - 2])
                    for k in range(KC):
                        dve.scalar_tensor_tensor(out=mix[:, m % 2, k, :], in0=xx[:, k, :], scalar=mu[:, row, k:k + 1],
                                                 in1=hT[:, k, 1:1 + NT], op0=ALU.mult, op1=ALU.add).then_inc(s_mx, 1)

            @block.tensor
            def _(pe):
                pe.wait_ge(s_ld, 80)
                for a in range(2):
                    for k in range(KC):
                        o = (a * KC + k) * 16
                        ins = pe.transpose(pm[:, 0, o:o + NC], ada[:, a * D + k * P:a * D + (k + 1) * P], ident[0:NC, 0:NC])
                ins.then_inc(s_mt, 1)
                pe.wait_ge(s_x, 16)
                for u in range(2 * KC):
                    k, half = divmod(u, 2)
                    if u >= 2:
                        pe.wait_ge(s_h, u - 1)
                    for t in range(4):
                        ins = pe.transpose(ps[u % 2][:, 0, t * P:(t + 1) * P], x[:, 4 * half + t, k * P:(k + 1) * P], ident[:])
                    ins.then_inc(s_xt, 1)
                pe.wait_ge(s_m, 1)
                for k in range(KC):
                    pe.transpose(pm[:, 0, k * NS:(k + 1) * NS], xs[:, k * P:(k + 1) * P], ident[0:NS, 0:NS])
                    ins = pe.transpose(pm[:, 1, k * NS:(k + 1) * NS], sh0[:, k * P:(k + 1) * P], ident[0:NS, 0:NS])
                ins.then_inc(s_xt, 1)
                pe.wait_ge(s_h, 2 * KC)

                def group(g, parts, rows=P):
                    pe.wait_ge(s_e, g + 1)
                    for i, (lhsT, rhs) in enumerate(parts):
                        for s in range(3):
                            ins = pe.matmul(ps[g % 2][0:rows, s, 0:SL], lhsT, rhs[:, s * SL:(s + 1) * SL],
                                            start=(i == 0), stop=(i == len(parts) - 1))
                    ins.then_inc(s_g, 1)
                    return ins

                for m in range(3):
                    pe.wait_ge(s_mx, KC * (m + 1))
                    for o in range(KC):
                        n = m * KC + o
                        pe.wait_ge(s_wr[n % 4], 16 * (n // 4 + 1))
                        group(n, [(wr[:, n % 4, k, :], mix[:, m % 2, k, :]) for k in range(KC)])
                for n, (g0, _, _, wid, _, m) in enumerate(LORA):
                    pe.wait_ge(s_mx, KC * (m + 1))
                    pe.wait_ge(s_w1, 16 * (n + 1))
                    g = g0
                    for lo in range(0, wid, P):
                        hi = min(wid, lo + P)
                        group(g, [(w1[:, k, lo:hi], mix[:, m % 2, k, :]) for k in range(KC)], rows=hi - lo)
                        g += 1
                    pe.wait_ge(s_w2, 16 * (n + 1) + 16 * (wid > P))
                    pe.wait_ge(s_e, g + 2)
                    r = min(wid, P)
                    for o in range(KC):
                        c = slice(o * P, (o + 1) * P)
                        parts = [(w2[0:r, c], hid[0:r, :])]
                        if wid > P:
                            parts.append((g2b[:, c], hid2[:]))
                        group(g + o, parts)

            @block.scalar
            def _(act):
                act.sem_inc(s_e, 2)
                stored = {g: n for n, (g, _, _) in enumerate(outputs())}
                funcs = {G_W: (ACT.Tanh, hid, 64), G_A: (ACT.Copy, hid, 64), G_G: (ACT.Sigmoid, hid, P),
                         G_G + 1: (ACT.Sigmoid, hid2, 32)}
                for g in range(G_END):
                    act.wait_ge(s_g, g + 1)
                    if g in stored:
                        n = stored[g]
                        if n >= 2:
                            act.wait_ge(s_evf[n % 2], 16 * (n // 2))
                        dst, rows, f = ev[:, n % 2], P, ACT.Copy
                    else:
                        f, dst, rows = funcs[g]
                        dst = dst[0:rows, :]
                    act.activation(dst.rearrange("p (s n) -> p s n", s=3), ps[g % 2][0:rows, :, 0:SL], f).then_inc(s_e, 1)


EXP_HALF = float(np.exp(-0.5))
LEVELS = 5


class Steps:

    def __init__(self, sem, names):
        self.sem, self.names, self.at = sem, list(names), {n: i for i, n in enumerate(names)}
        assert len(self.at) == len(self.names)
        self.n = 0

    def open(self, eng):
        eng.sem_inc(self.sem, len(self.names))

    def step(self, name, ins):
        assert self.names[self.n] == name, (self.names[self.n], name)
        self.n = (self.n + 1) % len(self.names)
        ins.then_inc(self.sem, 1)

    def ahead(self, eng, steps):
        left = 0
        for n, name in enumerate(self.names):
            if name in steps:
                if left:
                    if n > left:
                        eng.wait_ge(self.sem, n - left)
                    eng.sem_inc(self.sem, left)
                    eng.wait_ge(self.sem, n)
                left = 0
                self.n = n
                steps[name](-1)
            else:
                left += 1
        if left:
            eng.wait_ge(self.sem, len(self.names) - left)
            eng.sem_inc(self.sem, left)
        self.n = 0

    def skip(self, eng, name, i):
        assert self.names[self.n] == name, (self.names[self.n], name)
        eng.wait_ge(self.sem, self.count(name, i) - 1)
        eng.sem_inc(self.sem, 1)
        self.n = (self.n + 1) % len(self.names)

    def count(self, name, i):
        return i * len(self.names) + (len(self.names) + self.at[name] + 1)

    def before(self, name, i):
        return i * len(self.names) + (self.at[name] + 1)

    def wait(self, eng, name, i, apart=None):
        wait_at(eng, self.sem, self.count(name, i), apart)

    def wait_before(self, eng, name, i, apart=None):
        wait_at(eng, self.sem, self.before(name, i), apart)


def wait_at(eng, sem, value, apart=None):
    if isinstance(value, int) and value <= 0:
        return
    eng.wait_ge(sem, value)
    if apart is not None:
        eng.sem_inc(apart, 1)


def phase_wkv(nc, T):
    UN = 16
    with Pool_(nc, "wkv") as A:
        ident = A.sb("ident", [P, P])
        bones = A.sb("bones", [P, P])
        maskg = A.sb("maskg", [P, 2, P])
        mask1 = A.sb("mask1", [P, P])
        mask1t = A.sb("mask1t", [P, P])
        mlev = A.sb("mlev", [P, LEVELS, P])
        seg = A.sb("seg", [P, NT])
        par = A.sb("par", [P, 5])
        raw = A.sb("raw", [P, 5, NT])
        R, K, V, W, L = (raw[:, i, :] for i in range(5))
        SQ = A.sb("SQ", [P, NT])
        RN = A.sb("RN", [P, NT])
        KK = A.sb("KK", [P, NT])
        KH = A.sb("KH", [P, NT])
        C = A.sb("C", [P, NT])
        E0 = A.sb("E0", [P, NT])
        E1 = A.sb("E1", [P, NT])
        EI = A.sb("EI", [P, NT])
        AR = A.sb("AR", [P, 2, NT])
        BN = A.sb("BN", [P, NT])
        BH = A.sb("BH", [P, NT])
        KHH = A.sb("KHH", [P, NT])
        RK = A.sb("RK", [P, NT])
        tok = A.sb("tok", [P, 4, TILES, P])
        SS = A.sb("SS", [NS, 6, P])
        GB = A.sb("GB", [P, UN, 2, P])
        GK = A.sb("GK", [P, UN, 2, P])
        TB = A.sb("TB", [P, 4, 2, 4, P])
        XB = A.sb("XB", [P, 4, 4, P])
        X0 = A.sb("X0", [P, 4, 4, HD])
        Q = A.sb("Q", [P, UN, HD])
        PT = A.sb("PT", [P, TILES, P])
        UB = A.sb("UB", [P, 2, 2, HD])
        ST = A.sb("ST", [P, 4, HD])
        SW = A.sb("SW", [P, 2, HD])
        Y = A.sb("Y", [P, NP])
        SO = A.sb("SO", [HD, P])
        ps = A.ps("ps", [P, 8, 512])
        s_nil = A.sem("waits_apart")
        s_k = A.sem("constants_loaded")
        s_raw = A.sem("raw_loaded")
        s_bo = A.sem("bonus_stored")
        s_y = A.sem("y_stored")
        s_so = A.sem("state_stored")
        s_ss = A.sem("sample_vectors_stored")

        tr = [(a, h) for a in range(4) for h in range(2)]
        order = []
        for l in range(LEVELS):
            order += [("X", l, 0), ("X", l, 1), ("T", l, 0), ("X", l, 2), ("T", l, 1), ("X", l, 3), ("T", l, 2), ("T", l, 3)]
        NEXT_PE = {4: ["n2a"], 5: ["n2b"], 6: ["n2c"]}
        NEXT_ACT = {1: ["sgw"], 2: ["alr"], 3: ["sq"], 5: ["n2a"], 6: ["n2b"], 7: ["n2c"]}
        RI = 6
        NEXT_DVE = {1: ["kkr"], 2: ["scan"], 4: ["kh"], 8: ["rmax"], 15: ["kk", "bn"]}
        for i in range(RI):
            NEXT_DVE[9 + i] = [f"rinv{i}"]
        NAMES_PE = ["bonus", "smp"] + [f"tr{a}{h}" for a, h in tr]
        for g in range(4):
            NAMES_PE += [f"gb{g}", f"gk{g}", f"ga{g}"]
        NAMES_PE += [f"{k}{l}{g}" for k, l, g in order]
        for g in range(4):
            NAMES_PE += [f"z{g}", f"pt{g}", f"q{g}"]
        for n in range(16):
            NAMES_PE += [f"u{n}", f"s{n}"]
            if n % 2:
                NAMES_PE += [f"y{n // 2}"]
            NAMES_PE += NEXT_PE.get(n, [])
        NAMES_PE += ["fin"]
        NAMES_DVE = ["zero", "rt", "bh", "khh", "at", "bo"]
        for g in range(4):
            NAMES_DVE += [f"gb{g}", f"gk{g}", f"ga{g}"]
        NAMES_DVE += [f"{k}{l}{g}" for k, l, g in order]
        NAMES_DVE += [f"pt{g}" for g in range(4)]
        for n in range(16):
            NAMES_DVE += [f"u{n}", f"s{n}"] + NEXT_DVE.get(n, [])
        NAMES_ACT = ["e1", "ei", "e0", "smp"] + [f"tr{a}{h}" for a, h in tr]
        for g in range(4):
            NAMES_ACT += [f"z{g}", f"q{g}"]
        for n in range(16):
            NAMES_ACT += [f"sw{n}"]
            if n % 2:
                NAMES_ACT += [f"y{n // 2}"]
            NAMES_ACT += NEXT_ACT.get(n, [])
        NAMES_ACT += ["fin"]
        NAMES_POOL = []
        for g in range(4):
            NAMES_POOL += [f"ti{g}", f"tm{g}", f"tt{g}"]
        NAMES_POOL += ["rr", "t1", "cm", "rk"]
        pe_ = Steps(A.sem("pe_steps"), NAMES_PE)
        dv_ = Steps(A.sem("dve_steps"), NAMES_DVE)
        ac_ = Steps(A.sem("act_steps"), NAMES_ACT)
        po_ = Steps(A.sem("pool_steps"), NAMES_POOL)
        NCH = KC

        def unit(g, u):
            return 2 * g + u % 2, u // 2

        def uid(t, h):
            return 4 * (t // 2) + 2 * h + t % 2

        with nc.Block() as block:

            @block.sync
            def _(sp):
                for dst, src in ((ident, "k_ident"), (bones, "k_bones"), (maskg, "k_maskg"), (mask1, "k_mask1"),
                                 (mask1t, "k_mask1t"), (mlev, "k_mlev")):
                    sp.dma_start(dst[:], T[src]).then_inc(s_k, 16)
                sp.dma_start(seg[:], T["k_seg"].broadcast_to([P, NT])).then_inc(s_k, 16)
                for s in (s_bo, s_y, s_so, s_ss):
                    sp.sem_inc(s, 16)

                def rows(c):
                    return ds(c * P, P)

                def load(c):
                    for i in range(5):
                        sp.dma_start(raw[:, i, :], T["proj_d"][i, rows(c), :]).then_inc(s_raw, 16)
                    sp.dma_start(par[:], T["wkv_par"][ds(c, 1)].rearrange("o p n -> (o p) n")).then_inc(s_raw, 16)

                def store(c, then=None):
                    dv_.wait(sp, "bo", c, apart=s_nil)
                    sp.dma_start(T["bonus_d"][rows(c), :], RK[:]).then_inc(s_bo, 16)
                    ac_.wait(sp, "smp", c, apart=s_nil)
                    sp.dma_start(T["sv_d"][:, :, ds(c * P, P)].rearrange("a s n -> s a n"), SS[:]).then_inc(s_ss, 16)
                    if then:
                        pe_.wait(sp, "tr31", c, apart=s_nil)
                        ac_.wait(sp, "e0", c, apart=s_nil)
                        then(c + 1)
                    ac_.wait(sp, "y7", c, apart=s_nil)
                    sp.dma_start(T["y_d"][ds(c * P, P), 0:NP], Y[:]).then_inc(s_y, 16)
                    ac_.wait(sp, "fin", c, apart=s_nil)
                    sp.dma_start(T["wkv_prompt"][ds(c * 2, 2)].rearrange("h i j -> i h j"),
                                 SO[:].rearrange("i (h j) -> i h j", h=2)).then_inc(s_so, 16)

                load(0)
                with sp.Fori(0, NCH - 1) as c:
                    store(c, load)
                store(NCH - 1, lambda c: load(0))
                sp.wait_ge(s_raw, 96 * (NCH + 1))
                for s in (s_bo, s_y, s_so, s_ss):
                    sp.wait_ge(s, 16 * NCH + 16)

            @block.scalar
            def _(act):
                def step(name, *a, **k):
                    ac_.step(name, act.activation(*a, **k))

                def norm(s):
                    def do(c):
                        pe_.wait(act, f"n2{'abc'[s]}", c)
                        step(f"n2{'abc'[s]}", RN[:, s * SL:(s + 1) * SL], ps[:, 7 - s % 2, 0:SL], ACT.Sqrt)
                    return do

                def sgw(c):
                    act.wait_ge(s_raw, c * 96 + 192)
                    step("sgw", W, W, ACT.Sigmoid, bias=par[:, 0:1])

                nxt = {"sgw": sgw, "alr": lambda c: step("alr", L, L, ACT.Sigmoid, bias=par[:, 1:2]),
                       "sq": lambda c: step("sq", SQ[:], K, ACT.Square, scale=par[:, 2:3]),
                       "n2a": norm(0), "n2b": norm(1), "n2c": norm(2)}
                act.wait_ge(s_k, 16 * 7)
                ac_.ahead(act, nxt)
                with act.Fori(0, NCH) as c:
                    dv_.wait_before(act, "s15", c)
                    step("e1", E1[:], C[:], ACT.Exp, scale=-EXP_HALF)
                    step("ei", EI[:], C[:], ACT.Exp, scale=EXP_HALF)
                    po_.wait_before(act, "cm", c)
                    step("e0", E0[:], E0[:], ACT.Exp, scale=-EXP_HALF)
                    pe_.wait(act, "smp", c)
                    act.wait_ge(s_ss, c * 16 + 16)
                    step("smp", SS[:].rearrange("s a n -> s (a n)"), ps[0:NS, 6:8, :].rearrange("s b n -> s (b n)")[:, 0:6 * P], ACT.Copy)
                    for n, (a, h) in enumerate(tr):
                        pe_.wait(act, f"tr{a}{h}", c)
                        step(f"tr{a}{h}", tok[:, a, 4 * h:4 * h + 4, :].rearrange("p t n -> p (t n)"), ps[:, n % 2, :], ACT.Copy)
                    for g in range(4):
                        pe_.wait(act, f"z{g}", c)
                        step(f"z{g}", X0[:, g].rearrange("p u n -> p (u n)"), ps[:, 6, 0:256], ACT.Copy)
                        pe_.wait(act, f"q{g}", c)
                        step(f"q{g}", Q[:, 4 * g:4 * g + 4].rearrange("p u n -> p (u n)"), ps[:, 7, 0:256], ACT.Copy)
                    for n in range(16):
                        if n:
                            dv_.wait(act, f"s{n - 1}", c)
                        else:
                            dv_.wait(act, "zero", c)
                        step(f"sw{n}", SW[:, n % 2], ST[:, n % 4], ACT.Copy, scale=E1[:, n * CH + CH - 1:n * CH + CH])
                        if n % 2:
                            t = n // 2
                            pe_.wait(act, f"y{t}", c)
                            if n == 1:
                                act.wait_ge(s_y, c * 16 + 16)
                            step(f"y{t}", Y[:, t * P:(t + 1) * P], ps[:, t % 2, 0:P], ACT.Copy)
                        for x in NEXT_ACT.get(n, []):
                            nxt[x](c)
                    pe_.wait(act, "fin", c)
                    act.wait_ge(s_so, c * 16 + 16)
                    step("fin", SO[:], ps[0:HD, 6, 0:P], ACT.Copy)

            @block.gpsimd
            def _(pool):
                def rr(c):
                    wait_at(pool, s_raw, c * 96 + 192, s_nil)
                    wait_at(pool, s_bo, c * 16 + 32, s_nil)
                    po_.step("rr", pool.tensor_scalar(RK[:], R, par[:, 4:5], None, ALU.mult))

                def t1(c):
                    ac_.wait(pool, "alr", c, apart=s_nil)
                    po_.step("t1", pool.tensor_scalar(KH[:], L, -1.0, par[:, 3:4], ALU.add, ALU.mult))

                def cm(c):
                    dv_.wait(pool, "scan", c, apart=s_nil)
                    po_.step("cm", pool.tensor_tensor(E0[:], C[:], W, ALU.subtract))

                def rk(c):
                    dv_.wait(pool, "kh", c, apart=s_nil)
                    po_.step("rk", pool.tensor_tensor(RK[:], RK[:], KH[:], ALU.mult))

                nxt = {"rr": rr, "t1": t1, "cm": cm, "rk": rk}
                pool.wait_ge(s_k, 16 * 7)
                po_.ahead(pool, nxt)
                with pool.Fori(0, NCH) as c:
                    for g in range(4):
                        bc = lambda m: m[:].rearrange("p (o n) -> p o n", o=1).broadcast_to([P, 4, P])
                        Tg, Ttg = TB[:, g, 0], TB[:, g, 1]
                        dv_.wait(pool, f"ga{g}", c, apart=s_nil)
                        po_.step(f"ti{g}", pool.tensor_tensor(Tg, Tg, bc(ident), ALU.add))
                        po_.step(f"tm{g}", pool.tensor_tensor(Ttg, GB[:, 4 * g:4 * g + 4, 0, :], bc(mask1t), ALU.mult))
                        po_.wait(pool, f"tm{g}", c, apart=s_nil)
                        po_.step(f"tt{g}", pool.tensor_tensor(Ttg, Ttg, bc(ident), ALU.add))
                    for x in ("rr", "t1", "cm", "rk"):
                        nxt[x](c)

            @block.vector
            def _(dve):
                def tt(name, out, a, b, op=ALU.mult):
                    dv_.step(name, dve.tensor_tensor(out, a, b, op))

                def kkr(c):
                    dve.wait_ge(s_raw, c * 96 + 192)
                    dv_.step("kkr", dve.tensor_scalar(KK[:], K, par[:, 2:3], None, ALU.mult))

                def rmax(c):
                    ac_.wait(dve, "n2c", c)
                    dv_.step("rmax", dve.tensor_scalar(RN[:], RN[:], 1e-12, None, ALU.max))

                def rinv(i):
                    def do(c):
                        x = RN[:, i * (NT // RI):(i + 1) * (NT // RI)]
                        dv_.wait(dve, "rmax", c)
                        dv_.step(f"rinv{i}", dve.reciprocal(x, x))
                    return do

                def kk(c):
                    dv_.wait(dve, f"rinv{RI - 1}", c)
                    tt("kk", KK[:], KK[:], RN[:])

                def scan(c):
                    ac_.wait(dve, "sgw", c)
                    dv_.step("scan", dve.tensor_tensor_scan(C[:], seg[:], W, 0.0, ALU.mult, ALU.add))

                def kh(c):
                    po_.wait(dve, "t1", c)
                    dv_.step("kh", dve.scalar_tensor_tensor(out=KH[:], in0=KH[:], scalar=1.0, in1=K, op0=ALU.add, op1=ALU.mult))

                def bn(c):
                    dv_.wait(dve, "kk", c)
                    dv_.step("bn", dve.scalar_tensor_tensor(out=BN[:], in0=KK[:], scalar=-1.0, in1=L, op0=ALU.mult, op1=ALU.mult))

                assert NT % RI == 0
                nxt = {"kkr": kkr, "scan": scan, "kh": kh, "rmax": rmax, "kk": kk, "bn": bn}
                for i in range(RI):
                    nxt[f"rinv{i}"] = rinv(i)
                dve.wait_ge(s_k, 16 * 7)
                dv_.ahead(dve, nxt)
                with dve.Fori(0, NCH) as c:
                    pe_.wait_before(dve, "fin", c)
                    dv_.step("zero", dve.memset(ST[:, 0], 0.0))
                    ac_.wait(dve, "e1", c)
                    tt("rt", AR[:, 1], R, E1[:])
                    ac_.wait(dve, "ei", c)
                    dv_.wait_before(dve, "bn", c)
                    tt("bh", BH[:], BN[:], EI[:])
                    tt("khh", KHH[:], KH[:], EI[:])
                    ac_.wait(dve, "e0", c)
                    tt("at", AR[:, 0], KK[:], E0[:])
                    pe_.wait(dve, "bonus", c)
                    dv_.step("bo", dve.tensor_tensor(RK[:].rearrange("p (s n) -> p s n", s=3), ps[:, 3:6, 0:SL],
                                                     V.rearrange("p (s n) -> p s n", s=3), ALU.mult))
                    mg = maskg[:].rearrange("p (o a) n -> p o a n", o=1).broadcast_to([P, 4, 2, P])
                    for g in range(4):
                        u = slice(4 * g, 4 * g + 4)
                        for nm, G, b in (("gb", GB, 2), ("gk", GK, 4)):
                            pe_.wait(dve, f"{nm}{g}", c)
                            tt(f"{nm}{g}", G[:, u], ps[:, b:b + 2, :].rearrange("p b (v a n) -> p (b v) a n", a=2, n=P), mg)
                        pe_.wait(dve, f"ga{g}", c)
                        tt(f"ga{g}", TB[:, g, 0].rearrange("p (h v) n -> p h v n", h=2), ps[:, 6:8, 0:256].rearrange("p h (v n) -> p h v n", n=P),
                           mask1[:].rearrange("p (a b n) -> p a b n", a=1, b=1).broadcast_to([P, 2, 2, P]))
                    for k, l, g in order:
                        pe_.wait(dve, f"{k}{l}{g}", c)
                        if k == "X":
                            tt(f"X{l}{g}", XB[:, g], ps[:, g % 2, :].rearrange("p (u n) -> p u n", u=4),
                               mlev[:, l:l + 1, :].broadcast_to([P, 4, P]))
                        else:
                            b = 2 + 2 * (g % 2)
                            a0 = 0 if l < LEVELS - 1 else 1
                            tt(f"T{l}{g}", TB[:, g, a0:2].rearrange("p a u n -> p a (u n)"), ps[:, b + a0:b + 2, :],
                               TB[:, g, a0:2].rearrange("p a u n -> p a (u n)"), ALU.add)
                    for g in range(4):
                        pe_.wait(dve, f"pt{g}", c)
                        dv_.step(f"pt{g}", dve.tensor_copy(PT[:, 2 * g:2 * g + 2].rearrange("p t n -> p (t n)"), ps[:, g % 2, 0:256]))
                    for n in range(16):
                        t, q = divmod(n, 2)
                        rows = slice(q * CH, q * CH + CH)
                        pe_.wait(dve, f"u{n}", c)
                        if n == 0:
                            ac_.wait(dve, "q3", c)
                        if n >= 4:
                            pe_.wait(dve, f"y{t - 2}", c)
                        tt(f"u{n}", UB[rows, t % 2], ps[rows, 2:4, 0:HD],
                           Q[rows, uid(t, 0):uid(t, 1) + 1:2, :], ALU.add)
                        pe_.wait(dve, f"s{n}", c)
                        ac_.wait(dve, f"sw{n}", c)
                        dv_.step(f"s{n}", dve.scalar_tensor_tensor(
                            out=ST[:, (n + 1) % 4], in0=ps[:, 4 + q, 0:HD], scalar=E1[:, n * CH + CH - 1:n * CH + CH],
                            in1=SW[:, n % 2], op0=ALU.mult, op1=ALU.add))
                        for x in NEXT_DVE.get(n, []):
                            nxt[x](c)

            @block.tensor
            def _(pe):
                def norm(s):
                    def do(c):
                        ac_.wait(pe, "n2a" if s == 2 else "sq", c)
                        pe_.step(f"n2{'abc'[s]}", pe.matmul(ps[:, 7 - s % 2, 0:SL], bones[:], SQ[:, s * SL:(s + 1) * SL],
                                                           start=True, stop=True))
                    return do

                nxt = {"n2a": norm(0), "n2b": norm(1), "n2c": norm(2)}
                pe.wait_ge(s_k, 16 * 7)
                pe_.ahead(pe, nxt)
                with pe.Fori(0, NCH) as c:
                    ac_.wait_before(pe, "y7", c)
                    dv_.wait_before(pe, "s15", c)
                    po_.wait_before(pe, "rk", c)
                    for s in range(3):
                        ins = pe.matmul(ps[:, 3 + s, 0:SL], bones[:], RK[:, s * SL:(s + 1) * SL], start=True, stop=True)
                    pe_.step("bonus", ins)
                    ac_.wait_before(pe, "fin", c)
                    dv_.wait(pe, "khh", c)
                    for i, x in enumerate((R, E1[:], KH[:], V, KK[:], BN[:])):
                        ins = pe.transpose(ps[0:NS, 6 + i // 4, (i % 4) * P:(i % 4 + 1) * P], x[:, NP:NT], ident[:])
                    pe_.step("smp", ins)
                    for n, (a, h) in enumerate(tr):
                        x = (AR[:, 0, :], V, BH[:], KHH[:])[a]
                        if n == 0:
                            dv_.wait(pe, "at", c)
                        if n >= 2:
                            ac_.wait(pe, "tr%d%d" % tr[n - 2], c)
                        for t in range(4):
                            ins = pe.transpose(ps[:, n % 2, t * P:(t + 1) * P], x[:, (4 * h + t) * P:(4 * h + t + 1) * P], ident[:])
                        pe_.step(f"tr{a}{h}", ins)
                    for g in range(4):
                        for nm, x, b in (("gb", BH, 2), ("gk", KHH, 4)):
                            if g:
                                dv_.wait(pe, f"{nm}{g - 1}", c)
                            else:
                                dv_.wait(pe, "bo", c)
                            for u in range(4):
                                t, h = unit(g, u)
                                r, cols = slice(h * HD, h * HD + HD), slice(t * P, t * P + P)
                                ins = pe.matmul(ps[:, b + u // 2, (u % 2) * 256:(u % 2) * 256 + 256], x[r, cols], AR[r, :, cols],
                                                start=True, stop=True)
                            pe_.step(f"{nm}{g}", ins)
                        if g:
                            dv_.wait(pe, f"ga{g - 1}", c)
                        else:
                            ac_.wait(pe, "smp", c)
                        for u in range(4):
                            t, h = unit(g, u)
                            r, cols = slice(h * HD, h * HD + HD), slice(t * P, t * P + P)
                            ins = pe.matmul(ps[:, 6 + h, (u % 2) * P:(u % 2 + 1) * P], AR[r, 0, cols], BH[r, cols], start=True, stop=True)
                        pe_.step(f"ga{g}", ins)
                    ac_.wait(pe, "tr31", c)
                    for k, l, g in order:
                        if k == "X":
                            if l == 0:
                                po_.wait(pe, f"tt{g}", c)
                            else:
                                dv_.wait(pe, f"T{l - 1}{g}", c)
                            if g >= 2:
                                dv_.wait(pe, f"X{l}{g - 2}", c)
                            for u in range(4):
                                ins = pe.matmul(ps[:, g % 2, u * P:(u + 1) * P], GB[:, 4 * g + u, 0, :], TB[:, g, 0, u, :],
                                                start=True, stop=True)
                        else:
                            dv_.wait(pe, f"X{l}{g}", c)
                            if g >= 2:
                                dv_.wait(pe, f"T{l}{g - 2}", c)
                            elif l == 0:
                                dv_.wait(pe, "gk3", c)
                            b = 2 + 2 * (g % 2)
                            for u in range(4):
                                cols = slice(u * P, (u + 1) * P)
                                if l < LEVELS - 1:
                                    pe.matmul(ps[:, b, cols], TB[:, g, 1, u, :], XB[:, g, u, :], start=True, stop=True)
                                ins = pe.matmul(ps[:, b + 1, cols], XB[:, g, u, :], TB[:, g, 1, u, :], start=True, stop=True)
                        pe_.step(f"{k}{l}{g}", ins)
                    for g in range(4):
                        if g:
                            ac_.wait(pe, f"z{g - 1}", c)
                        else:
                            dv_.wait(pe, "ga3", c)
                        for u in range(4):
                            t, h = unit(g, u)
                            ins = pe.matmul(ps[:, 6, u * HD:(u + 1) * HD], GK[:, 4 * g + u, 0, :], tok[:, 1, t, h * HD:h * HD + HD],
                                            start=True, stop=True)
                        pe_.step(f"z{g}", ins)
                        dv_.wait(pe, f"T{LEVELS - 1}{g}", c)
                        if g >= 2:
                            dv_.wait(pe, f"pt{g - 2}", c)
                        for u in range(4):
                            t, h = unit(g, u)
                            ins = pe.matmul(ps[h * HD:h * HD + HD, g % 2, (u % 2) * P:(u % 2 + 1) * P],
                                            tok[:, 0, t, h * HD:h * HD + HD], TB[:, g, 1, u, :], start=True, stop=True)
                        pe_.step(f"pt{g}", ins)
                        ac_.wait(pe, f"z{g}", c)
                        if g:
                            ac_.wait(pe, f"q{g - 1}", c)
                        for u in range(4):
                            ins = pe.matmul(ps[:, 7, u * HD:(u + 1) * HD], TB[:, g, 1, u, :], X0[:, g, u, :], start=True, stop=True)
                        pe_.step(f"q{g}", ins)
                    for n in range(16):
                        t, q = divmod(n, 2)
                        rows = slice(q * CH, q * CH + CH)
                        dv_.wait(pe, f"s{n - 1}" if n else "pt3", c, apart=s_nil)
                        for h in range(2):
                            hr = slice(h * HD, h * HD + HD)
                            ins = pe.matmul(ps[rows, 2 + h, 0:HD], PT[hr, t, rows], ST[hr, n % 4, :],
                                            start=True, stop=True)
                        pe_.step(f"u{n}", ins)
                        for h in range(2):
                            hr = slice(h * HD, h * HD + HD)
                            pe.matmul(ps[hr, 4 + q, 0:HD], tok[rows, 3, t, hr], tok[rows, 1, t, hr], start=True, stop=False)
                        dv_.wait(pe, f"u{n}", c, apart=s_nil)
                        for h in range(2):
                            hr = slice(h * HD, h * HD + HD)
                            ins = pe.matmul(ps[hr, 4 + q, 0:HD], tok[rows, 2, t, hr], UB[rows, t % 2, h, :], start=False, stop=True)
                        pe_.step(f"s{n}", ins)
                        if q:
                            if t >= 2:
                                ac_.wait(pe, f"y{t - 2}", c)
                            for h in range(2):
                                hr, u = slice(h * HD, h * HD + HD), uid(t, h)
                                o = ps[hr, t % 2, 0:P]
                                pe.matmul(o, UB[:, t % 2, h, :], GB[:, u, 1, :], start=True, stop=False, skip_group_check=True)
                                pe.matmul(o, tok[:, 1, t, hr], GK[:, u, 1, :], start=False, stop=False, skip_group_check=True)
                                for qq in range(2):
                                    m = 2 * t + qq
                                    ins = pe.matmul(ps[hr, t % 2, qq * CH:(qq + 1) * CH], ST[hr, m % 4, :],
                                                    AR[hr, 1, t * P + qq * CH:t * P + (qq + 1) * CH],
                                                    start=False, stop=True, skip_group_check=True)
                            pe_.step(f"y{t}", ins)
                        for x in NEXT_PE.get(n, []):
                            nxt[x](c)
                    ac_.wait(pe, "n2b", c, apart=s_nil)
                    dv_.wait(pe, "s15", c, apart=s_nil)
                    pe_.step("fin", pe.transpose(ps[0:HD, 6, 0:P], ST[:, 0, :], ident[:]))


def wkv_consts():
    i = np.arange(P)
    t, s = i[:, None], i[None, :]
    same = (t // CH) == (s // CH)
    one = np.float32
    out = {"k_ident": np.eye(P, dtype=one)}
    out["k_bones"] = ((t // HD) == (s // HD)).astype(one)
    out["k_maskg"] = np.stack([(same & (t < s)).astype(one), (same & (t <= s)).astype(one)], 1)
    lev = [((t // (2 * m)) == (s // (2 * m))) & ((t // m) % 2 == 1) & ((s // m) % 2 == 0) for m in (1, 2, 4, 8, 16, 32)]
    out["k_mask1"] = lev[0].astype(one)
    out["k_mask1t"] = np.ascontiguousarray(lev[0].T).astype(one)
    out["k_mlev"] = np.stack(lev[1:], 1).astype(one)
    n = np.arange(NT)
    out["k_seg"] = ((n % CH != 0) & (n < NP)).astype(one)[None]
    return out


NTP = 9 * P
TT = NTP // P
ZC = NTP + P
NE, NG, EG = 32, 4, 8
BIG = 1e30


def phase_sample(nc, T):
    with Pool_(nc, "smp") as A:
        ident = A.sb("ident", [P, P])
        v = A.sb("v", [P, 6, HD])
        S = A.sb("S", [P, HD, HD])
        T1 = A.sb("T1", [P, HD, HD])
        T2 = A.sb("T2", [P, HD, HD])
        T3 = A.sb("T3", [P, HD, HD])
        sa = A.sb("sa", [P, HD])
        y = A.sb("y", [P, HD])
        ys = A.sb("ys", [NS, D])
        ysT = A.sb("ysT", [P, KC, NS])
        ps = A.ps("ps", [P, KC, NS])
        s_ld = A.sem("loaded")
        s_v = A.sem("dve_steps")
        s_p = A.sem("pool_steps")
        s_y = A.sem("y_stored")
        s_S = A.sem("state_stored")
        s_yl = A.sem("y_token_rows")
        s_t = A.sem("y_transposed")
        s_c = A.sem("yT_ready")
        s_o = A.sem("yT_stored")
        vec = lambda i: v[:, i]
        key = lambda x: x.rearrange("p (o j) -> p o j", o=1).broadcast_to([P, HD, HD])
        val = lambda x: x.rearrange("p (i o) -> p i o", o=1).broadcast_to([P, HD, HD])
        with nc.Block() as block:

            @block.sync
            def _(sp):
                sp.dma_start(S[:], T["state_wkv"]).then_inc(s_ld, 16)
                sp.dma_start(v[:], T["sv_d"].rearrange("a s (h d) -> (s h) a d", d=HD)).then_inc(s_ld, 16)
                sp.dma_start(ident[:], T["k_ident"]).then_inc(s_ld, 16)
                sp.wait_ge(s_v, 5)
                sp.dma_start(T["wkv_sample"], T2[:]).then_inc(s_S, 16)
                sp.wait_ge(s_v, 7)
                sp.dma_start(T["ys_d"].rearrange("s (h d) -> (s h) d", d=HD), y[:]).then_inc(s_y, 16)
                sp.wait_ge(s_y, 16)
                sp.dma_start(ys[:], T["ys_d"]).then_inc(s_yl, 16)
                sp.wait_ge(s_c, 1)
                sp.dma_start(T["y_d"].rearrange("(c p) n -> p c n", p=P)[:, :, NP:NT], ysT[:]).then_inc(s_o, 16)
                sp.wait_ge(s_o, 16)
                sp.wait_ge(s_S, 16)

            @block.vector
            def _(dve):
                link = Chain(dve, s_v)
                dve.wait_ge(s_ld, 48)
                link(dve.tensor_tensor(T1[:], S[:], key(vec(4)), ALU.mult))
                link(dve.tensor_reduce(sa[:], T1[:], AX, ALU.add))
                link(dve.tensor_tensor(T1[:], val(sa[:]), key(vec(5)), ALU.mult))
                dve.wait_ge(s_p, 2)
                link(dve.tensor_tensor(T1[:], T1[:], T3[:], ALU.add))
                link(dve.tensor_tensor(T2[:], T2[:], T1[:], ALU.add))
                link(dve.tensor_tensor(T1[:], T2[:], key(vec(0)), ALU.mult))
                link(dve.tensor_reduce(y[:], T1[:], AX, ALU.add))
                dve.wait_ge(s_t, 1)
                dve.tensor_copy(ysT[:], ps[:]).then_inc(s_c, 1)

            @block.gpsimd
            def _(pool):
                pool.wait_ge(s_ld, 48)
                pool.tensor_tensor(T2[:], S[:], key(vec(1)), ALU.mult).then_inc(s_p, 1)
                pool.tensor_tensor(T3[:], val(vec(3)), key(vec(2)), ALU.mult).then_inc(s_p, 1)

            @block.tensor
            def _(pe):
                pe.wait_ge(s_ld, 48)
                pe.wait_ge(s_yl, 16)
                for k in range(KC):
                    ins = pe.transpose(ps[:, k, :], ys[:, k * P:(k + 1) * P], ident[0:NS, 0:NS])
                ins.then_inc(s_t, 1)


def phase_gn(nc, T):
    U = 4
    with Pool_(nc, "gn") as A:
        bones = A.sb("bones", [P, P])
        par = A.sb("par", [P, 2, KC])
        y = A.sb("y", [P, U, 3, NT])
        sq = A.sb("sq", [P, U, NT])
        rs = A.sb("rs", [P, NT])
        z = A.sb("z", [P, U, ZC])
        ps = [A.ps(f"ps{i}", [P, 3, 512]) for i in range(2)]
        s_nil = A.sem("waits_apart")
        s_k = A.sem("constants_loaded")
        s_ld = [A.sem(f"rows_loaded{i}") for i in range(U)]
        s_st = [A.sem(f"z_stored{i}") for i in range(U)]
        s_z = A.sem("pads_zeroed")
        three = lambda x: x.rearrange("p (s n) -> p s n", s=3)
        slots = lambda f: [x for i in range(U) for x in f(i)]
        dv_ = Steps(A.sem("dve_steps"), slots(lambda i: [f"yc{(i + 1) % U}", f"eps{i}", f"rs{i}", f"yn{i}", f"aff{i}"]))
        pe_ = Steps(A.sem("pe_steps"), slots(lambda i: [f"mean{(i + 1) % U}", f"var{i}"]))
        ac_ = Steps(A.sem("act_steps"), slots(lambda i: [f"sq{(i + 1) % U}", f"var{i}"]))
        po_ = Steps(A.sem("pool_steps"), slots(lambda i: [f"bo{i}", f"z{i}"]))
        NIT = KC // U
        with nc.Block() as block:

            @block.sync
            def _(sp):
                def load(k, i):
                    rows = ds(k * P, P) if not isinstance(k, int) else slice(k * P, k * P + P)
                    sp.dma_start(y[:, i, 0, :], T["y_d"][rows, :]).then_inc(s_ld[i], 16)
                    sp.dma_start(y[:, i, 1, :], T["bonus_d"][rows, :]).then_inc(s_ld[i], 16)
                    sp.dma_start(y[:, i, 2, :], T["proj_d"][5, rows, :]).then_inc(s_ld[i], 16)

                def store(c, i):
                    po_.wait(sp, f"z{i}", c, apart=s_nil)
                    sp.dma_start(T["z_d"][ds(c * (U * P) + i * P, P), :], z[:, i]).then_inc(s_st[i], 16)

                sp.dma_start(bones[:], T["k_bones64"]).then_inc(s_k, 16)
                for i in range(U):
                    load(i, i)
                sp.dma_start(par[:], T["gn_par"]).then_inc(s_k, 16)
                for s in s_st:
                    sp.sem_inc(s, 16)
                with sp.Fori(0, NIT - 1) as c:
                    for i in range(U):
                        store(c, i)
                        load(c * U + (U + i), i)
                store(NIT - 1, 0)
                load(0, 0)
                for i in range(1, U):
                    store(NIT - 1, i)
                for s in s_st:
                    sp.wait_ge(s, 16 * NIT + 16)

            @block.scalar
            def _(act):
                def square(i):
                    def do(c):
                        dv_.wait(act, f"yc{i}", c)
                        (pe_.wait if i == 0 else pe_.wait_before)(act, f"var{i}", c)
                        ac_.step(f"sq{i}", act.activation(sq[:, i], y[:, i, 0, :], ACT.Square))
                    return do

                ac_.ahead(act, {"sq0": square(0)})
                with act.Fori(0, NIT) as c:
                    for i in range(U):
                        square((i + 1) % U)(c)
                        dv_.wait(act, f"eps{i}", c)
                        ac_.step(f"var{i}", act.activation(rs[:], rs[:], ACT.Sqrt))

            @block.gpsimd
            def _(pool):
                po_.open(pool)
                pool.memset(z[:, :, NT:ZC], 0.0).then_inc(s_z, 1)
                pool.wait_ge(s_z, 1)
                with pool.Fori(0, NIT) as c:
                    for i in range(U):
                        Y = y[:, i, 0, :]
                        dv_.wait(pool, f"aff{i}", c, apart=s_nil)
                        po_.step(f"bo{i}", pool.tensor_tensor(Y, Y, y[:, i, 1, :], ALU.add))
                        po_.wait(pool, f"bo{i}", c, apart=s_nil)
                        wait_at(pool, s_st[i], c * 16 + 16, s_nil)
                        po_.step(f"z{i}", pool.tensor_tensor(z[:, i, 0:NT], Y, y[:, i, 2, :], ALU.mult))

            @block.vector
            def _(dve):
                def centre(i):
                    def do(c):
                        Y = y[:, i, 0, :]
                        pe_.wait(dve, f"mean{i}", c)
                        dv_.step(f"yc{i}", dve.tensor_tensor(three(Y), three(Y), ps[0][:, :, 0:SL], ALU.subtract))
                    return do

                dve.wait_ge(s_k, 32)
                dv_.ahead(dve, {"yc0": centre(0)})
                with dve.Fori(0, NIT) as c:
                    for i in range(U):
                        Y = y[:, i, 0, :]
                        k = c * U + i
                        centre((i + 1) % U)(c)
                        pe_.wait(dve, f"var{i}", c)
                        dv_.step(f"eps{i}", dve.tensor_scalar(three(rs[:]), ps[1][:, :, 0:SL], GN_EPS, None, ALU.add))
                        ac_.wait(dve, f"var{i}", c)
                        dv_.step(f"rs{i}", dve.reciprocal(rs[:], rs[:]))
                        dv_.wait(dve, f"rs{i}", c)
                        dv_.step(f"yn{i}", dve.tensor_tensor(Y, Y, rs[:], ALU.mult))
                        dv_.wait(dve, f"yn{i}", c)
                        dv_.step(f"aff{i}", dve.tensor_scalar(Y, Y, par[:, 0, ds(k, 1)], par[:, 1, ds(k, 1)], ALU.mult, ALU.add))

            @block.tensor
            def _(pe):
                def mean(i):
                    def do(c):
                        (dv_.wait_before if i == 1 else dv_.wait)(pe, f"yc{(i - 1) % U}", c)
                        pe.wait_ge(s_ld[i], c * 48 + (96 if i == 0 else 48))
                        for s in range(3):
                            ins = pe.matmul(ps[0][:, s, 0:SL], bones[:], y[:, i, 0, s * SL:(s + 1) * SL], start=True, stop=True)
                        pe_.step(f"mean{i}", ins)
                    return do

                pe.wait_ge(s_k, 32)
                pe_.ahead(pe, {"mean0": mean(0)})
                with pe.Fori(0, NIT) as c:
                    for i in range(U):
                        mean((i + 1) % U)(c)
                        (ac_.wait if i else ac_.wait_before)(pe, f"sq{i}", c)
                        (dv_.wait if i else dv_.wait_before)(pe, f"eps{(i - 1) % U}", c)
                        for s in range(3):
                            ins = pe.matmul(ps[1][:, s, 0:SL], bones[:], sq[:, i, s * SL:(s + 1) * SL], start=True, stop=True)
                        pe_.step(f"var{i}", ins)


def phase_post(nc, T, layer):
    tag = f"post{layer}"
    W_O = T["w_o"][layer]
    with Pool_(nc, tag) as A:
        ident = A.sb("ident", [P, P])
        low = A.sb("low", [P, P])
        ones = A.sb("ones", [P, P])
        wo = A.sb("wo", [P, KC, D])
        rw = A.sb("rw", [P, KC, NE])
        rb = A.sb("rb", [P, NE])
        iota = A.sb("iota", [P, NE])
        down = A.sb("down", [P, EG])
        valid = A.sb("valid", [P, TT])
        mod = A.sb("mod", [P, 2, 3, D])
        ln = A.sb("ln", [P, 2, D])
        zt = A.sb("zt", [P, 2, KC, P])
        x = A.sb("x", [P, 2, D])
        t1 = A.sb("t1", [P, D])
        x1 = A.sb("x1", [P, 2, D])
        xm = A.sb("xm", [P, 2, D])
        xmT = A.sb("xmT", [P, KC, P])
        st = A.sb("st", [P, 2, 6])
        mv = A.sb("mv", [P, 2])
        rs = A.sb("rs", [P, 1])
        lg = A.sb("lg", [P, TT, NE])
        aff = A.sb("aff", [P, TT, NE])
        sel = A.sb("sel", [P, TT, NE])
        eq = A.sb("eq", [P, TT, NE])
        m1 = A.sb("m1", [P, 2, TT * NG])
        r1 = A.sb("r1", [P, TT * NG])
        oh = A.sb("oh", [P, TT, 2, NE])
        gsum = A.sb("gsum", [P, TT, NG])
        geq = A.sb("geq", [P, TT, NG])
        gm = A.sb("gm", [P, TT])
        gr = A.sb("gr", [P, TT])
        ta = A.sb("ta", [P, TT, 2, NE])
        ga = A.sb("ga", [P, TT, 2])
        gt2 = A.sb("gt2", [P, TT])
        M = A.sb("M", [P, TT, NE])
        Mp = A.sb("Mp", [P, TT + 1, NE])
        EK = A.sb("EK", [P, TT * 2])
        RK = A.sb("RK", [P, TT * 2])
        GT = A.sb("GT", [P, TT * 2])
        cnt = A.sb("cnt", [P, NE])
        cmp_ = A.sb("cmp", [P, 8, TT * 2 + NE])
        nov = A.sb("nov", [P, NE])
        incl = A.sb("incl", [P, NE])
        q = A.sb("q", [P, TT * 2])
        base = A.sb("base", [P, TT * 2])
        q0 = A.sb("q0", [P, TT * 2])
        blk = A.sb("blk", [P, TT * 2])
        rem = A.sb("rem", [P, TT * 2])
        slotf = A.sb("slotf", [P, TT * 2])
        tixf = A.sb("tixf", [P, TT * 2])
        sloti = A.sb("sloti", [P, TT * 2], I32)
        tixi = A.sb("tixi", [P, TT * 2], I32)
        be = A.sb("be", [1, 16, NE])
        bef = A.sb("bef", [1, 2 + 48])
        pr = A.sb("pr", [1, 8])
        bei = A.sb("bei", [1, 2 + 48], I32)
        tokid = A.sb("tokid", [P, TT], I32)
        dummy = A.sb("dummy", [P, 2])
        zero48 = A.sb("zero48", [P, 48], I32)
        ps_mm = A.ps("ps_mm", [P, 2, 2, 512])
        ps_tr = A.ps("ps_tr", [P, 2, 512])
        ps_lg = A.ps("ps_lg", [P, NE])
        ps_rk = A.ps("ps_rk", [P, TT, NE])
        s_nil = A.sem("waits_apart")
        s_k = A.sem("constants_loaded")
        s_wo = [A.sem(f"w_o_loaded{b}") for b in range(2)]
        s_mz = A.sem("mod_zeroed")
        s_zt = [A.sem(f"z_tile_loaded{j}") for j in range(2)]
        s_x = [A.sem(f"x_loaded{j}") for j in range(2)]
        s_x1 = [A.sem(f"x1_stored{j}") for j in range(2)]
        s_xm = [A.sem(f"xm_stored{j}") for j in range(2)]
        s_init = A.sem("table_cleared")
        s_sc = A.sem("tokens_scattered")
        s_res = A.sem("routing_stored")
        both = lambda *names: [f"{x}{j}" for j in range(2) for x in names]
        dv_ = Steps(A.sem("dve_steps"), both("gmul", "res", "st0", "st1", "ag", "eps", "rs", "xn", "xg", "x1"))
        pe_ = Steps(A.sem("pe_steps"), both("mm", "tr", "lg"))
        ac_ = Steps(A.sem("act_steps"), both("sd", "xmT", "lg"))
        po_ = Steps(A.sem("pool_steps"), both("xs", "xm"))
        s_aff = A.sem("affinities_ready")
        s_M = A.sem("assignments_ready")
        s_rk = A.sem("ranks_summed")
        s_fin = A.sem("final_steps")
        s_cnt = A.sem("routing_chain")
        s_mm0 = A.sem("first_product")
        HALF = TT // 2
        NK = 16 * 17
        with nc.Block() as block:

            def tiles(eng, body):
                with eng.Fori(0, HALF) as i:
                    for j in range(2):
                        body(i, j, i * 2 + j)
                body(HALF, 0, TT - 1)

            rows = lambda t: ds(t * P, P) if not isinstance(t, int) else slice(t * P, t * P + P)

            @block.sync
            def _(sp):
                zv = T["z_d"].rearrange("(k p) n -> p k n", p=P)
                wov = W_O.rearrange("(k p) n -> p k n", p=P)
                sp.dma_start(zt[:, 0], zv[:, :, 0:P]).then_inc(s_zt[0], 16)
                for b in range(2):
                    sp.dma_start(wo[:, :, b * 512:(b + 1) * 512], wov[:, :, b * 512:(b + 1) * 512]).then_inc(s_wo[b], 16)
                sp.dma_start(zt[:, 1], zv[:, :, P:2 * P]).then_inc(s_zt[1], 16)
                for dst, src in ((ident, T["k_ident"]), (low, T["k_low"]), (ones, T["k_ones"]), (iota, T["k_iota"]),
                                 (valid, T["k_valid"]), (tokid, T["k_tokid"]), (dummy, T["k_dummy"]),
                                 (rw, T["router_w"].rearrange("(k p) e -> p k e", p=P)),
                                 (rb, T["router_b"].broadcast_to([P, NE]))):
                    sp.dma_start(dst[:], src).then_inc(s_k, 16)
                for i in range(2):
                    sp.dma_start(ln[:, i], T["ln_gb"][layer * 2, i:i + 1, :].broadcast_to([P, D])).then_inc(s_k, 16)
                sp.wait_ge(s_mz, 1)
                a0, a1 = T["ada_d"][2 * layer], T["ada_d"][2 * layer + 1]
                for j, (a, lo) in enumerate(((a0, 2 * D), (a1, 0), (a1, D))):
                    sp.dma_start(mod[:, 0, j], a[NS:NC, lo:lo + D].broadcast_to([P, D])).then_inc(s_k, 16)
                    sp.dma_start(mod[0:NS, 1, j], a[0:NS, lo:lo + D]).then_inc(s_k, 16)

                def body(i, j, t):
                    dv_.wait_before(sp, f"res{j}", i, apart=s_nil)
                    sp.dma_start(x[:, j], T["x_in"][layer][rows(t), :]).then_inc(s_x[j], 16)
                    if isinstance(t, int):
                        return
                    if j:
                        pe_.wait(sp, "mm0", i, apart=s_nil)
                    else:
                        sp.wait_ge(s_mm0, 1)
                        pe_.wait_before(sp, "mm1", i, apart=s_nil)
                    sp.dma_start(zt[:, j], zv[:, :, ds((t + 2) * P, P)]).then_inc(s_zt[j], 16)

                tiles(sp, body)
                sp.wait_ge(s_fin, 2)
                sp.dma_start(T["blk_d"][layer], bei[:]).then_inc(s_res, 16)
                sp.dma_start(T["slot_d"][layer], sloti[:]).then_inc(s_res, 16)
                sp.dma_start(T["gate_d"][layer], GT[:]).then_inc(s_res, 16)
                sp.wait_ge(s_res, 48)

            @block.gpsimd
            def _(pool):
                po_.open(pool)
                pool.memset(mod[:, 1], 0.0).then_inc(s_mz, 1)
                pool.memset(zero48[:], 0).then_inc(s_mz, 1)
                pool.wait_ge(s_mz, 2)
                pool.dma_start(T["table_d"][layer][0:48 * P, :].rearrange("(r b) o -> r (b o)", b=48), zero48[:]).then_inc(s_init, 16)
                pool.wait_ge(s_k, NK)

                def body(i, j, t):
                    kind = 1 if isinstance(t, int) else 0
                    dv_.wait(pool, f"x1{j}", i, apart=s_nil)
                    wait_at(pool, s_xm[j], i * 16 + 16, s_nil)
                    pe_.wait_before(pool, f"tr{j}", i, apart=s_nil)
                    po_.step(f"xs{j}", pool.tensor_tensor(xm[:, j], x1[:, j], mod[:, kind, 2], ALU.mult))
                    po_.wait(pool, f"xs{j}", i, apart=s_nil)
                    po_.step(f"xm{j}", pool.tensor_tensor(xm[:, j], xm[:, j], mod[:, kind, 1], ALU.add))

                tiles(pool, body)
                pool.wait_ge(s_fin, 2)
                pool.wait_ge(s_init, 16)
                for i in range(TT * 2):
                    pool.indirect_dma_start(T["table_d"][layer], bass.IndirectOffsetOnAxis(ap=tixi[:, i:i + 1], axis=0),
                                            tokid[:, i // 2:i // 2 + 1], None).then_inc(s_sc, 16)
                pool.wait_ge(s_sc, 16 * TT * 2)

            @block.scalar
            def _(act):
                ac_.open(act)
                for s in s_x1 + s_xm:
                    act.sem_inc(s, 16)

                def body(i, j, t):
                    dv_.wait(act, f"eps{j}", i)
                    ac_.step(f"sd{j}", act.activation(rs[:], rs[:], ACT.Sqrt))
                    dv_.wait(act, f"x1{j}", i, apart=s_nil)
                    act.dma_start(T["x1_d"][rows(t), :], x1[:, j]).then_inc(s_x1[j], 16)
                    po_.wait(act, f"xm{j}", i, apart=s_nil)
                    act.dma_start(T["xm_d"][rows(t), :], xm[:, j]).then_inc(s_xm[j], 16)
                    pe_.wait(act, f"tr{j}", i)
                    ac_.step(f"xmT{j}", act.activation(xmT[:].rearrange("p (b k) n -> p b (k n)", b=2), ps_tr[:], ACT.Copy))
                    pe_.wait(act, f"lg{j}", i)
                    dst = lg[:, ds(t, 1), :].rearrange("p o e -> p (o e)") if not isinstance(t, int) else lg[:, t]
                    ac_.step(f"lg{j}", act.activation(dst, ps_lg[:], ACT.Copy))

                tiles(act, body)
                ac_.wait(act, "lg0", HALF)
                act.activation(aff[:], lg[:], ACT.Sigmoid).then_inc(s_aff, 1)
                for s in s_x1 + s_xm:
                    act.wait_ge(s, 16 * (HALF + 1 + (s in (s_x1[0], s_xm[0]))))

            @block.vector
            def _(dve):
                dv_.open(dve)
                link = Chain(dve, s_cnt)
                link(dve.memset(Mp[:, 0], 0.0))
                dve.wait_ge(s_k, NK)
                link(dve.tensor_scalar(down[:], iota[:, 0:EG], -1.0, float(EG), ALU.mult, ALU.add))

                def body(i, j, t):
                    kind = 1 if isinstance(t, int) else 0

                    def op(name, ins, then=False):
                        dv_.step(f"{name}{j}", ins)
                        if then:
                            dv_.wait(dve, f"{name}{j}", i, apart=s_nil if then == "apart" else None)

                    if j:
                        pe_.wait(dve, "mm0", i)
                    else:
                        dve.wait_ge(s_mm0, 1)
                        pe_.wait_before(dve, "mm1", i)
                    op("gmul", dve.tensor_tensor(t1[:].rearrange("p (b n) -> p b n", b=2), ps_mm[:, j],
                                                 mod[:, kind, 0].rearrange("p (b n) -> p b n", b=2), ALU.mult), True)
                    dve.wait_ge(s_x[j], i * 16 + 16)
                    op("res", dve.scalar_tensor_tensor(out=t1[:], in0=x[:, j], scalar=ALPHA, in1=t1[:], op0=ALU.mult, op1=ALU.add), True)
                    op("st0", dve.bn_stats(st[:, 0], t1[:, 0:512]))
                    op("st1", dve.bn_stats(st[:, 1], t1[:, 512:D]), "apart")
                    op("ag", dve.bn_aggr(mv[:], st[:]), True)
                    op("eps", dve.tensor_scalar(rs[:], mv[:, 1:2], LN_EPS, None, ALU.add))
                    ac_.wait(dve, f"sd{j}", i)
                    op("rs", dve.reciprocal(rs[:], rs[:]), True)
                    op("xn", dve.tensor_scalar(t1[:], t1[:], mv[:, 0:1], rs[:], ALU.subtract, ALU.mult), True)
                    po_.wait_before(dve, f"xs{j}", i)
                    wait_at(dve, s_x1[j], i * 16 + 16)
                    op("xg", dve.tensor_tensor(x1[:, j], t1[:], ln[:, 0], ALU.mult), True)
                    op("x1", dve.tensor_tensor(x1[:, j], x1[:, j], ln[:, 1], ALU.add))

                tiles(dve, body)

                dve.wait_ge(s_aff, 1)
                link(dve.tensor_tensor(sel[:], aff[:], rb[:].rearrange("p (o e) -> p o e", o=1).broadcast_to([P, TT, NE]), ALU.add))
                groups = lambda a: a.rearrange("p t (g j) -> p (t g) j", g=NG)
                wide = lambda a, n: a.rearrange("p (m o) -> p m o", o=1).broadcast_to([P, a.shape[1], n])
                dn = lambda m, n: down[:, EG - n:].rearrange("p (o j) -> p o j", o=1).broadcast_to([P, m, n])
                for k in range(2):
                    s3, e3, o3 = groups(sel[:]), groups(eq[:]), oh[:, :, k, :].rearrange("p t (g j) -> p t g j", g=NG)
                    e4 = eq[:].rearrange("p t (g j) -> p t g j", g=NG)
                    link(dve.tensor_reduce(m1[:, k], s3, AX, ALU.max))
                    link(dve.tensor_tensor(e3, s3, wide(m1[:, k], EG), ALU.is_equal))
                    link(dve.tensor_tensor(e3, e3, dn(TT * NG, EG), ALU.mult))
                    link(dve.tensor_reduce(r1[:], e3, AX, ALU.max))
                    link(dve.tensor_tensor(e3, dn(TT * NG, EG), wide(r1[:], EG), ALU.is_equal))
                    link(dve.tensor_copy(o3, e4))
                    if k == 0:
                        link(dve.scalar_tensor_tensor(out=s3, in0=e3, scalar=-BIG, in1=s3, op0=ALU.mult, op1=ALU.add))
                link(dve.tensor_tensor(gsum[:].rearrange("p t g -> p (t g)"), m1[:, 0], m1[:, 1], ALU.add))
                link(dve.tensor_reduce(gm[:], gsum[:], AX, ALU.max))
                link(dve.tensor_tensor(geq[:], gsum[:], wide(gm[:], NG), ALU.is_equal))
                link(dve.tensor_tensor(geq[:], geq[:], dn(TT, NG), ALU.mult))
                link(dve.tensor_reduce(gr[:], geq[:], AX, ALU.max))
                link(dve.tensor_tensor(geq[:], dn(TT, NG), wide(gr[:], NG), ALU.is_equal))
                g5 = geq[:].rearrange("p t (g o) -> p t g o", o=1).broadcast_to([P, TT, NG, EG])
                for k in range(2):
                    o4 = oh[:, :, k, :].rearrange("p t (g j) -> p t g j", g=NG)
                    link(dve.tensor_tensor(o4, o4, g5, ALU.mult))
                flat = lambda a: a.rearrange("p t k e -> p (t k) e")
                io = iota[:].rearrange("p (o e) -> p o e", o=1).broadcast_to([P, TT * 2, NE])
                af = aff[:].rearrange("p t (o e) -> p t o e", o=1).broadcast_to([P, TT, 2, NE])
                link(dve.tensor_tensor(flat(ta[:]), flat(oh[:]), io, ALU.mult))
                link(dve.tensor_reduce(EK[:], flat(ta[:]), AX, ALU.add))
                link(dve.tensor_tensor(ta[:], oh[:], af, ALU.mult))
                link(dve.tensor_reduce(ga[:].rearrange("p t k -> p (t k)"), flat(ta[:]), AX, ALU.add))
                link(dve.tensor_reduce(gt2[:], ga[:], AX, ALU.add))
                link(dve.reciprocal(gt2[:], gt2[:]))
                link(dve.tensor_tensor(GT[:].rearrange("p (t k) -> p t k", k=2), ga[:], wide(gt2[:], 2), ALU.mult))
                link(dve.tensor_tensor(oh[:].rearrange("p t k e -> p t (k e)"), oh[:].rearrange("p t k e -> p t (k e)"),
                                       wide(valid[:], 2 * NE), ALU.mult))
                link(dve.tensor_tensor(M[:], oh[:, :, 0], oh[:, :, 1], ALU.add))
                for t in range(TT - 1):
                    link(dve.tensor_tensor(Mp[:, t + 1], Mp[:, t], M[:, t], ALU.add))
                dve.tensor_tensor(Mp[:, TT], Mp[:, TT - 1], M[:, TT - 1], ALU.add).then_inc(s_M, 1)
                dve.wait_ge(s_rk, 1)
                rkb = ps_rk[:].rearrange("p t (o e) -> p t o e", o=1).broadcast_to([P, TT, 2, NE])
                link(dve.tensor_tensor(ta[:], oh[:], rkb, ALU.mult))
                link(dve.tensor_reduce(RK[:], flat(ta[:]), AX, ALU.add))
                link(dve.tensor_copy(cnt[:], ps_lg[:]))
                for jj in range(8):
                    link(dve.tensor_scalar(cmp_[:, jj, 0:TT * 2], RK[:], 128.0 * (jj + 1), None, ALU.is_ge))
                for jj in range(8):
                    link(dve.tensor_scalar(cmp_[:, jj, TT * 2:], cnt[:], 128.0 * (jj + 1), None, ALU.is_gt))
                link(dve.tensor_reduce(q[:], cmp_[:, :, 0:TT * 2].rearrange("p j n -> p n j"), AX, ALU.add))
                link(dve.tensor_reduce(nov[:], cmp_[:, :, TT * 2:].rearrange("p j n -> p n j"), AX, ALU.add))
                link(dve.tensor_tensor_scan(incl[:], ones[:, 0:NE], nov[:], 0.0, ALU.mult, ALU.add))
                link(dve.tensor_tensor(nov[:], incl[:], nov[:], ALU.subtract))
                link(dve.tensor_tensor(flat(ta[:]), flat(oh[:]), nov[:].rearrange("p (o e) -> p o e", o=1).broadcast_to([P, TT * 2, NE]),
                                       ALU.mult))
                link(dve.tensor_reduce(base[:], flat(ta[:]), AX, ALU.add))
                link(dve.tensor_scalar(q0[:], q[:], 0.0, None, ALU.is_equal))
                link(dve.scalar_tensor_tensor(out=base[:], in0=base[:], scalar=float(NE - 1), in1=q[:], op0=ALU.add, op1=ALU.add))
                link(dve.tensor_tensor(blk[:], EK[:], base[:], ALU.subtract))
                link(dve.tensor_tensor(blk[:], blk[:], q0[:], ALU.mult))
                link(dve.tensor_tensor(blk[:], blk[:], base[:], ALU.add))
                link(dve.scalar_tensor_tensor(out=rem[:], in0=q[:], scalar=-128.0, in1=RK[:], op0=ALU.mult, op1=ALU.add))
                link(dve.scalar_tensor_tensor(out=slotf[:], in0=blk[:], scalar=128.0, in1=rem[:], op0=ALU.mult, op1=ALU.add))
                link(dve.tensor_scalar(slotf[:], slotf[:], 128.0, None, ALU.add))
                vb = valid[:].rearrange("p (t o) -> p t o", o=1).broadcast_to([P, TT, 2])
                tk = lambda a: a[:].rearrange("p (t k) -> p t k", k=2)
                link(dve.tensor_tensor(tk(slotf), tk(slotf), vb, ALU.mult))
                link(dve.scalar_tensor_tensor(out=tixf[:], in0=rem[:], scalar=48.0, in1=blk[:], op0=ALU.mult, op1=ALU.add))
                db = dummy[:].rearrange("p (o k) -> p o k", o=1).broadcast_to([P, TT, 2])
                link(dve.tensor_tensor(tk(tixf), tk(tixf), db, ALU.subtract))
                link(dve.tensor_tensor(tk(tixf), tk(tixf), vb, ALU.mult))
                link(dve.tensor_tensor(tk(tixf), tk(tixf), db, ALU.add))
                link(dve.tensor_copy(sloti[:], slotf[:]))
                dve.tensor_copy(tixi[:], tixf[:]).then_inc(s_fin, 1)
                link(dve.tensor_tensor(be[:], incl[0:1, :].rearrange("p (o e) -> p o e", o=1).broadcast_to([1, 16, NE]),
                                       iota[0:1, 0:16].rearrange("p (b o) -> p b o", o=1).broadcast_to([1, 16, NE]), ALU.is_le))
                link(dve.tensor_reduce(bef[:, 1 + NE:49], be[:], AX, ALU.add))
                link(dve.tensor_scalar(bef[:, 1 + NE:49], bef[:, 1 + NE:49], float(NE - 1), None, ALU.min))
                link(dve.tensor_copy(bef[:, 1:1 + NE], iota[0:1, :]))
                link(dve.memset(bef[:, 49:50], 0.0))
                link(dve.tensor_scalar(pr[:], iota[0:1, 0:8], 2.0, incl[0:1, NE - 1:NE], ALU.mult, ALU.is_lt))
                link(dve.tensor_reduce(bef[:, 0:1], pr[:], AX, ALU.add))
                link(dve.tensor_scalar(bef[:, 0:1], bef[:, 0:1], NE / 2, None, ALU.add))
                dve.tensor_copy(bei[:], bef[:]).then_inc(s_fin, 1)

            @block.tensor
            def _(pe):
                pe_.open(pe)

                def product(j, first=False):
                    for b in range(2):
                        if first:
                            pe.wait_ge(s_wo[b], 16)
                        for k in range(KC):
                            ins = pe.matmul(ps_mm[:, j, b], zt[:, j, k, :], wo[:, k, b * 512:(b + 1) * 512],
                                            start=(k == 0), stop=(k == KC - 1))
                    return ins

                pe.wait_ge(s_zt[0], 16)
                product(0, True).then_inc(s_mm0, 1)
                pe.wait_ge(s_k, NK)

                def body(i, j, t):
                    if not isinstance(t, int):
                        (dv_.wait if j else dv_.wait_before)(pe, f"gmul{1 - j}", i, apart=s_nil)
                        pe.wait_ge(s_zt[1 - j], i * 16 + 16 + 16 * j)
                        pe_.step(f"mm{j}", product(1 - j))
                    else:
                        pe_.skip(pe, "mm0", i)
                    po_.wait(pe, f"xm{j}", i, apart=s_nil)
                    (ac_.wait if j else ac_.wait_before)(pe, f"xmT{1 - j}", i, apart=s_nil)
                    for k in range(KC):
                        ins = pe.transpose(ps_tr[:, k // 4, (k % 4) * P:(k % 4 + 1) * P], xm[:, j, k * P:(k + 1) * P], ident[:])
                    pe_.step(f"tr{j}", ins)
                    ac_.wait(pe, f"xmT{j}", i, apart=s_nil)
                    (ac_.wait if j else ac_.wait_before)(pe, f"lg{1 - j}", i, apart=s_nil)
                    for k in range(KC):
                        ins = pe.matmul(ps_lg[:], xmT[:, k, :], rw[:, k, :], start=(k == 0), stop=(k == KC - 1))
                    pe_.step(f"lg{j}", ins)

                tiles(pe, body)
                pe.wait_ge(s_M, 1)
                for w, m, first in ((low, M[:], True), (ones, Mp[:, 0:TT], False)):
                    pe.matmul(ps_rk[:].rearrange("p t e -> p (t e)"), w[:], m.rearrange("p t e -> p (t e)"), start=first, stop=not first)
                pe.matmul(ps_lg[:], ones[:], Mp[:, TT], start=True, stop=True).then_inc(s_rk, 1)


def post_consts():
    one = np.float32
    i = np.arange(P)
    out = {"k_low": (i[:, None] < i[None, :]).astype(one), "k_ones": np.ones((P, P), one)}
    out["k_bones64"] = ((i[:, None] // HD) == (i[None, :] // HD)).astype(one) / HD
    out["k_iota"] = np.broadcast_to(np.arange(NE, dtype=one), (P, NE)).copy()
    tok = np.arange(NTP).reshape(TT, P).T
    out["k_valid"] = np.ascontiguousarray(tok < NT).astype(one)
    out["k_tokid"] = np.ascontiguousarray(tok).astype(np.int32)
    out["k_dummy"] = np.stack([48 * P + i, 49 * P + i], 1).astype(one)
    return out


NBLK = 48
DE = 512
KE = DE // P


def phase_moe(nc, T, layer):
    W_IN, W_OUT = T["moe_w_in"][layer], T["moe_w_out"][layer]
    with Pool_(nc, f"moe{layer}") as A:
        ident = A.sb("ident", [P, P])
        bei = A.sb("bei", [1, 2 + NBLK], I32)
        idx = A.sb("idx", [P, NBLK + 2], I32)
        col = A.sb("col", [P, 2], I32)
        X = A.sb("X", [P, 2, D])
        xT = A.sb("xT", [P, 2, KC, P])
        wi = A.sb("wi", [P, 2, KC, 2 * DE])
        wo = A.sb("wo", [P, 2, KE, D])
        sg = A.sb("sg", [P, DE])
        h = A.sb("h", [P, DE])
        hT = A.sb("hT", [P, KE, P])
        y = A.sb("y", [P, 2, D])
        ps_x = A.ps("ps_x", [P, 2, 512])
        ps_h = A.ps("ps_h", [P, 2, 512])
        ps_a = A.ps("ps_a", [P, 512])
        ps_y = A.ps("ps_y", [P, 2, 512])
        s_nil = A.sem("waits_apart")
        s_k = A.sem("constants_loaded")
        s_ix = A.sem("table_padded")
        s_wi = [A.sem(f"w_in_loaded{j}") for j in range(2)]
        s_wo = [A.sem(f"w_out_loaded{j}") for j in range(2)]
        s_x = [A.sem(f"rows_gathered{j}") for j in range(2)]
        s_y = [A.sem(f"y_stored{j}") for j in range(2)]
        s_x0 = A.sem("first_xT")
        s_z = A.sem("block_before_first_zeroed")
        s_yl = A.sem("last_product")
        s_ye = A.sem("last_y_ready")
        pe_ = Steps(A.sem("pe_steps"), [f"{n}{j}" for j in range(2) for n in ("gate", "up", "xT", "y0", "y1", "hT")])
        ac_ = Steps(A.sem("act_steps"), [f"{n}{j}" for j in range(2) for n in ("silu", "y0", "hT")])
        dv_ = Steps(A.sem("dve_steps"), [f"{n}{j}" for j in range(2) for n in ("h", "xT", "y1")])
        po_ = Steps(A.sem("pool_steps"), ["col0", "col1"])

        def pairs(eng):
            eng.wait_ge(s_k, 48)
            return eng.value_load(bei[0:1, 0:1], min_val=NE // 2, max_val=NBLK // 2)

        with nc.Block() as block:

            @block.sync
            def _(sp):
                sp.dma_start(bei[:], T["blk_d"][layer]).then_inc(s_k, 16)
                sp.dma_start(idx[:, 0:NBLK], T["table_d"][layer][0:NBLK * P, :].rearrange("(r b) o -> r (b o)", b=NBLK)).then_inc(s_k, 16)
                sp.dma_start(ident[:], T["k_ident"]).then_inc(s_k, 16)
                for j in range(2):
                    sp.dma_start(wi[:, j], W_IN[j].rearrange("(k p) n -> p k n", p=P)).then_inc(s_wi[j], 16)
                    if j == 0:
                        sp.dma_start(wo[:, j], W_OUT[j].rearrange("(k p) n -> p k n", p=P)).then_inc(s_wo[j], 16)
                n = pairs(sp)
                expert = lambda at: sp.value_load(bei[0:1, ds(at + 1, 1)], min_val=0, max_val=NE - 1)

                def w_out(e, i, j):
                    pe_.wait(sp, f"y1{1 - j}", i, apart=s_nil)
                    sp.dma_start(wo[:, j], W_OUT[ds(e, 1)].rearrange("o (k p) n -> p (o k) n", p=P)).then_inc(s_wo[j], 16)

                with sp.Fori(0, n - 1) as i:
                    for j in range(2):
                        e1, e2 = expert(i * 2 + (1 + j)), expert(i * 2 + (2 + j))
                        pe_.wait(sp, f"up{j}", i, apart=s_nil)
                        sp.dma_start(wi[:, j], W_IN[ds(e2, 1)].rearrange("o (k p) n -> p (o k) n", p=P)).then_inc(s_wi[j], 16)
                        w_out(e1, i, 1 - j)
                w_out(expert(n * 2 - 1), n - 1, 1)

            @block.gpsimd
            def _(pool):
                pool.memset(idx[:, NBLK:], 0).then_inc(s_ix, 1)
                pool.wait_ge(s_ix, 1)
                po_.open(pool)
                n = pairs(pool)

                def gather(j):
                    pool.indirect_dma_start(X[:, j], None, T["xm_d"], bass.IndirectOffsetOnAxis(ap=col[:, j:j + 1], axis=0)
                                            ).then_inc(s_x[j], 16)

                for j in range(2):
                    pool.tensor_copy(col[:, j:j + 1], idx[:, j:j + 1]).then_inc(s_ix, 1)
                    pool.wait_ge(s_ix, 2 + j)
                    gather(j)
                pool.wait_ge(s_x0, 1)
                with pool.Fori(0, n) as i:
                    for j in range(2):
                        pe_.wait(pool, f"xT{1 - j}", i, apart=s_nil) if j else pe_.wait_before(pool, "xT1", i, apart=s_nil)
                        pool.wait_ge(s_x[j], i * 16 + 16)
                        po_.step(f"col{j}", pool.tensor_copy(col[:, j:j + 1], idx[:, ds(i * 2 + (2 + j), 1)]))
                        po_.wait(pool, f"col{j}", i, apart=s_nil)
                        gather(j)
                for j in range(2):
                    wait_at(pool, s_x[j], n * 16 + 16, s_nil)

            @block.tensor
            def _(pe):
                pe_.open(pe)
                n = pairs(pe)

                def transposes(j):
                    for k in range(KC):
                        ins = pe.transpose(ps_x[:, k // 4, (k % 4) * P:(k % 4 + 1) * P], X[:, j, k * P:(k + 1) * P], ident[:])
                    return ins

                pe.wait_ge(s_x[0], 16)
                transposes(0).then_inc(s_x0, 1)
                with pe.Fori(0, n) as i:
                    for j in range(2):
                        if j:
                            dv_.wait(pe, "xT0", i, apart=s_nil)
                        else:
                            dv_.wait_before(pe, "xT1", i, apart=s_nil)
                            pe.wait_ge(s_x0, 2)
                        pe.wait_ge(s_wi[j], i * 16 + 16)
                        for half, name in enumerate(("gate", "up")):
                            (ac_.wait if j else ac_.wait_before)(pe, f"silu{1 - j}", i, apart=s_nil)
                            if half:
                                (dv_.wait if j else dv_.wait_before)(pe, f"h{1 - j}", i, apart=s_nil)
                            for k in range(KC):
                                ins = pe.matmul(ps_h[:, half], xT[:, j, k, :], wi[:, j, k, half * DE:(half + 1) * DE],
                                                start=(k == 0), stop=(k == KC - 1))
                            pe_.step(f"{name}{j}", ins)
                        pe.wait_ge(s_x[1 - j], i * 16 + 16 + 16 * j)
                        pe_.step(f"xT{j}", transposes(1 - j))
                        if j:
                            ac_.wait(pe, "hT0", i, apart=s_nil)
                        else:
                            pe.wait_ge(s_z, 1)
                            ac_.wait_before(pe, "hT1", i, apart=s_nil)
                        pe.wait_ge(s_wo[1 - j], i * 16 + 16)
                        for half in range(2):
                            if half:
                                (dv_.wait if j else dv_.wait_before)(pe, f"y1{1 - j}", i, apart=s_nil)
                            else:
                                (ac_.wait if j else ac_.wait_before)(pe, f"y0{1 - j}", i, apart=s_nil)
                            for k in range(KE):
                                ins = pe.matmul(ps_y[:, half], hT[:, k, :], wo[:, 1 - j, k, half * 512:(half + 1) * 512],
                                                start=(k == 0), stop=(k == KE - 1))
                            pe_.step(f"y{half}{j}", ins)
                        dv_.wait(pe, f"h{j}", i, apart=s_nil)
                        for k in range(KE):
                            ins = pe.transpose(ps_a[:, k * P:(k + 1) * P], h[:, k * P:(k + 1) * P], ident[:])
                        pe_.step(f"hT{j}", ins)
                ac_.wait(pe, "hT1", n - 1, apart=s_nil)
                dv_.wait(pe, "y11", n - 1, apart=s_nil)
                wait_at(pe, s_wo[1], n * 16 + 16, s_nil)
                for half in range(2):
                    for k in range(KE):
                        ins = pe.matmul(ps_y[:, half], hT[:, k, :], wo[:, 1, k, half * 512:(half + 1) * 512],
                                        start=(k == 0), stop=(k == KE - 1))
                    ins.then_inc(s_yl, 1)

            @block.scalar
            def _(act):
                ac_.open(act)
                for s in s_y:
                    act.sem_inc(s, 16)
                n = pairs(act)
                with act.Fori(0, n) as i:
                    for j in range(2):
                        pe_.wait(act, f"gate{j}", i)
                        (dv_.wait if j else dv_.wait_before)(act, f"h{1 - j}", i)
                        ac_.step(f"silu{j}", act.activation(sg[:], ps_h[:, 0], ACT.Silu))
                        pe_.wait(act, f"y0{j}", i)
                        act.wait_ge(s_y[j], i * 16 + 16)
                        ac_.step(f"y0{j}", act.activation(y[:, j, 0:512], ps_y[:, 0], ACT.Copy))
                        ac_.wait(act, f"y0{j}", i)
                        dv_.wait(act, f"y1{j}", i, apart=s_nil)
                        act.dma_start(T["ysl_d"][ds(i * (2 * P) + j * P, P), :], y[:, j]).then_inc(s_y[j], 16)
                        pe_.wait(act, f"hT{j}", i)
                        ac_.step(f"hT{j}", act.activation(hT[:].rearrange("p k n -> p (k n)"), ps_a[:], ACT.Copy))
                act.wait_ge(s_yl, 1)
                wait_at(act, s_y[0], n * 16 + 16, s_nil)
                act.activation(y[:, 0, 0:512], ps_y[:, 0], ACT.Copy).then_inc(s_ye, 1)
                act.wait_ge(s_ye, 2)
                act.dma_start(T["ysl_d"][ds(n * (2 * P), P), :], y[:, 0]).then_inc(s_y[0], 16)
                wait_at(act, s_y[0], n * 16 + 32, s_nil)
                wait_at(act, s_y[1], n * 16 + 16, s_nil)

            @block.vector
            def _(dve):
                dv_.open(dve)
                dve.memset(hT[:], 0.0).then_inc(s_z, 1)
                dve.memset(wo[:, 1], 0.0).then_inc(s_wo[1], 16)
                n = pairs(dve)
                xTv = lambda j: xT[:, j].rearrange("p (b k) n -> p b (k n)", b=2)
                dve.wait_ge(s_x0, 1)
                dve.tensor_copy(xTv(0), ps_x[:]).then_inc(s_x0, 1)
                with dve.Fori(0, n) as i:
                    for j in range(2):
                        ac_.wait(dve, f"silu{j}", i)
                        pe_.wait(dve, f"up{j}", i)
                        (pe_.wait if j else pe_.wait_before)(dve, f"hT{1 - j}", i)
                        dv_.step(f"h{j}", dve.tensor_tensor(h[:], sg[:], ps_h[:, 1], ALU.mult))
                        pe_.wait(dve, f"xT{j}", i)
                        dv_.step(f"xT{j}", dve.tensor_copy(xTv(1 - j), ps_x[:]))
                        pe_.wait(dve, f"y1{j}", i)
                        dve.wait_ge(s_y[j], i * 16 + 16)
                        dv_.step(f"y1{j}", dve.tensor_copy(y[:, j, 512:D], ps_y[:, 1]))
                dve.wait_ge(s_yl, 2)
                wait_at(dve, s_y[0], n * 16 + 16, s_nil)
                dve.tensor_copy(y[:, 0, 512:D], ps_y[:, 1]).then_inc(s_ye, 1)


def phase_combine(nc, T, layer):
    out = T["x_in"][1] if layer == 0 else None
    with Pool_(nc, f"comb{layer}") as A:
        slot = A.sb("slot", [P, 2 * TT + 2], I32)
        col = A.sb("col", [P, 2, 2], I32)
        gate = A.sb("gate", [P, 2 * TT])
        mod = A.sb("mod", [P, 2, D])
        ln = A.sb("ln", [P, 2, D])
        x = A.sb("x", [P, 2, D])
        Y = A.sb("Y", [P, 2, 2, D])
        o = A.sb("o", [P, 2, D])
        st = A.sb("st", [P, 2, 6])
        mv = A.sb("mv", [P, 2])
        rs = A.sb("rs", [P, 1])
        s_nil = A.sem("waits_apart")
        s_k = A.sem("constants_loaded")
        s_z = A.sem("mod_zeroed")
        s_x = [A.sem(f"x_loaded{j}") for j in range(2)]
        s_g = [A.sem(f"rows_gathered{j}") for j in range(2)]
        s_o = [A.sem(f"x_stored{j}") for j in range(2)]
        s_c0 = A.sem("first_columns")
        N = [f"{n}{j}" for j in range(2) for n in ("g1", "gm", "res", "st0", "st1", "ag", "eps", "rs", "xn")]
        dv_ = Steps(A.sem("dve_steps"), N)
        ac_ = Steps(A.sem("act_steps"), ["g00", "sd0", "g01", "sd1"])
        po_ = Steps(A.sem("pool_steps"), [f"{n}{j}" for j in range(2) for n in ("ca", "cb", "xg", "xb")])
        HALF = TT // 2
        assert TT % 2
        with nc.Block() as block:

            def tiles(eng, body):
                with eng.Fori(0, HALF) as i:
                    for j in range(2):
                        body(i, j, i * 2 + j)
                body(HALF, 0, TT - 1)

            rows = lambda t: ds(t * P, P) if not isinstance(t, int) else slice(t * P, t * P + P)
            cols = lambda t, k: ds(t * 2 + k, 1) if not isinstance(t, int) else slice(t * 2 + k, t * 2 + k + 1)

            @block.sync
            def _(sp):
                sp.dma_start(slot[:, 0:2 * TT], T["slot_d"][layer]).then_inc(s_k, 16)
                sp.dma_start(gate[:], T["gate_d"][layer]).then_inc(s_k, 16)
                for i in range(2):
                    sp.dma_start(ln[:, i], T["ln_gb"][layer * 2 + 1, i:i + 1, :].broadcast_to([P, D])).then_inc(s_k, 16)
                a = T["ada_d"][2 * layer + 1]
                sp.wait_ge(s_z, 1)
                sp.dma_start(mod[:, 0], a[NS:NC, 2 * D:3 * D].broadcast_to([P, D])).then_inc(s_k, 16)
                sp.dma_start(mod[0:NS, 1], a[0:NS, 2 * D:3 * D]).then_inc(s_k, 16)

                for s in s_o:
                    sp.sem_inc(s, 16)
                sp.dma_start(x[:, 0], T["x1_d"][0:P, :]).then_inc(s_x[0], 16)

                def body(i, j, t):
                    if not isinstance(t, int):
                        (dv_.wait if j else dv_.wait_before)(sp, f"res{1 - j}", i, apart=s_nil)
                        sp.dma_start(x[:, 1 - j], T["x1_d"][rows(t + 1), :]).then_inc(s_x[1 - j], 16)
                    po_.wait(sp, f"xb{j}", i, apart=s_nil)
                    if isinstance(t, int) and layer == 1:
                        sp.dma_start(T["y_sample"], o[0:NS, j]).then_inc(s_o[j], 16)
                    else:
                        sp.dma_start((out if layer == 0 else T["y_prompt"])[rows(t), :], o[:, j]).then_inc(s_o[j], 16)

                tiles(sp, body)
                sp.wait_ge(s_o[0], 16 * (HALF + 2))
                sp.wait_ge(s_o[1], 16 * (HALF + 1))

            @block.gpsimd
            def _(pool):
                po_.open(pool)
                pool.memset(mod[:, 1], 0.0).then_inc(s_z, 1)
                pool.memset(slot[:, 2 * TT:], 0).then_inc(s_z, 1)
                pool.wait_ge(s_z, 2)
                pool.wait_ge(s_k, 96)

                def gather(t, j, copies):
                    copies(0, pool.tensor_copy(col[:, j, 0:1], slot[:, cols(t, 0)]))
                    copies(1, pool.tensor_copy(col[:, j, 1:2], slot[:, cols(t, 1)]))
                    for k in range(2):
                        pool.indirect_dma_start(Y[:, j, k], None, T["ysl_d"], bass.IndirectOffsetOnAxis(ap=col[:, j, k:k + 1], axis=0)
                                                ).then_inc(s_g[j], 16)

                def first(t):
                    def do(k, ins):
                        ins.then_inc(s_c0, 1)
                        if k:
                            pool.wait_ge(s_c0, 2 * t + 2)
                    return do

                for t in range(2):
                    gather(t, t, first(t))

                def body(i, j, t):
                    dv_.wait(pool, f"xn{j}", i, apart=s_nil)
                    if isinstance(t, int):
                        po_.skip(pool, "ca0", i)
                        po_.skip(pool, "cb0", i)
                    else:
                        def copies(k, ins):
                            po_.step(f"c{'ab'[k]}{j}", ins)
                            if k:
                                po_.wait(pool, f"cb{j}", i, apart=s_nil)

                        gather(t + 2, j, copies)
                    po_.step(f"xg{j}", pool.tensor_tensor(o[:, j], o[:, j], ln[:, 0], ALU.mult))
                    po_.wait(pool, f"xg{j}", i, apart=s_nil)
                    po_.step(f"xb{j}", pool.tensor_tensor(o[:, j], o[:, j], ln[:, 1], ALU.add))

                tiles(pool, body)
                pool.wait_ge(s_g[0], 32 * (HALF + 1))
                pool.wait_ge(s_g[1], 32 * (HALF + 1))

            @block.scalar
            def _(act):
                ac_.open(act)
                act.wait_ge(s_k, 96)

                def body(i, j, t):
                    wait_at(act, s_g[j], i * 32 + 32, s_nil)
                    ac_.step(f"g0{j}", act.activation(Y[:, j, 0], Y[:, j, 0], ACT.Copy, scale=gate[:, cols(t, 0)]))
                    dv_.wait(act, f"eps{j}", i)
                    ac_.step(f"sd{j}", act.activation(rs[:], rs[:], ACT.Sqrt))

                tiles(act, body)

            @block.vector
            def _(dve):
                dv_.open(dve)
                dve.wait_ge(s_k, 96)

                def body(i, j, t):
                    kind = 1 if isinstance(t, int) else 0

                    def op(name, ins, then=True):
                        dv_.step(f"{name}{j}", ins)
                        if then:
                            dv_.wait(dve, f"{name}{j}", i, apart=s_nil if then == "apart" else None)

                    a, b = Y[:, j, 0], Y[:, j, 1]
                    dve.wait_ge(s_g[j], i * 32 + 32)
                    ac_.wait(dve, f"g0{j}", i)
                    op("g1", dve.scalar_tensor_tensor(out=a, in0=b, scalar=gate[:, cols(t, 1)], in1=a, op0=ALU.mult, op1=ALU.add))
                    op("gm", dve.tensor_tensor(a, a, mod[:, kind], ALU.mult))
                    dve.wait_ge(s_x[j], i * 16 + 16)
                    op("res", dve.scalar_tensor_tensor(out=a, in0=x[:, j], scalar=ALPHA, in1=a, op0=ALU.mult, op1=ALU.add))
                    op("st0", dve.bn_stats(st[:, 0], a[:, 0:512]), False)
                    op("st1", dve.bn_stats(st[:, 1], a[:, 512:D]), "apart")
                    op("ag", dve.bn_aggr(mv[:], st[:]))
                    op("eps", dve.tensor_scalar(rs[:], mv[:, 1:2], LN_EPS, None, ALU.add), False)
                    ac_.wait(dve, f"sd{j}", i)
                    op("rs", dve.reciprocal(rs[:], rs[:]))
                    dve.wait_ge(s_o[j], i * 16 + 16)
                    op("xn", dve.tensor_scalar(o[:, j], a, mv[:, 0:1], rs[:], ALU.subtract, ALU.mult), False)

                tiles(dve, body)


NG3 = 3
DIL = (1, 4, 16)
KVH, REP = 4, 4
ROT = 16
PASS = HD - ROT
PAST = 256
NEG = -1e30
QR = NG3 * H * ROT
QP = NG3 * H * PASS
NR, NPS = QR // P, QP // P
SCALE = HD ** -0.5


def phase_qkv(nc, T):
    with Pool_(nc, "qkv") as A:
        ident = A.sb("ident", [P, P])
        rotp = A.sb("rotp", [P, P])
        ada = A.sb("ada", [NC, 4, D])
        mod = A.sb("mod", [P, 4, KC, NC])
        x = A.sb("x", [P, TT, D])
        kc = x[0:HD].rearrange("p t n -> p (t n)")[:, 0:2 * KVH * NP].rearrange("p (a h n) -> p a h n", a=2, h=KVH)
        hh = A.sb("hh", [P, 2, KC, NT])
        cos = A.sb("cos", [P, NT])
        sin = A.sb("sin", [P, NT])
        ctok = A.sb("ctok", [P, TT, 2, 8])
        wkv = A.sb("wkv", [P, KC, 512])
        wr = A.sb("wr", [P, 4, KC, P])
        kv = A.sb("kv", [P, 2, 512])
        tmp = A.sb("tmp", [P, 4, KVH, 8])
        kn = A.sb("kn", [HD, 2, KVH, P])
        raw = A.sb("raw", [P, NT])
        t1 = A.sb("t1", [P, NT])
        t2 = A.sb("t2", [P, NT])
        ev = A.sb("ev", [P, 2, NT])
        qsT = A.sb("qsT", [P, NR + NPS, NS])
        qs = A.sb("qs", [NS, (NR + NPS) * P])
        ps = [A.ps(f"ps{i}", [P, 3, 512]) for i in range(2)]
        pm = A.ps("pm", [P, 2, 512])
        s_nil = A.sem("waits_apart")
        s_ld = A.sem("constants_loaded")
        s_x = A.sem("x_loaded")
        s_mt = A.sem("mod_transposed")
        s_m = A.sem("mod_ready")
        s_z = A.sem("dve_chain")
        s_xt = A.sem("x_transposed")
        s_h = A.sem("h_ready")
        s_kvp = A.sem("kv_product")
        s_kve = A.sem("kv_evacuated")
        s_kvr = A.sem("kv_rotated")
        s_kt = A.sem("k_transposed")
        s_kn = A.sem("k_copied")
        s_kvs = [A.sem(f"kv_stored{i}") for i in range(2)]
        s_kns = [A.sem(f"k_natural_stored{i}") for i in range(2)]
        s_kcs = A.sem("k_classes_stored")
        s_wr = [A.sem(f"w_loaded{i}") for i in range(4)]
        s_q = A.sem("q_product")
        s_raw = A.sem("q_raw")
        s_rp = A.sem("q_swapped")
        s_rm = A.sem("q_rotated")
        s_e = A.sem("q_ready")
        s_evs = [A.sem(f"q_stored{i}") for i in range(2)]
        s_qt = A.sem("sample_q_transposed")
        s_qs = A.sem("sample_q_ready")
        s_qd = A.sem("sample_q_stored")
        NCH = NR + NPS
        wv = T["w_q"].rearrange("(k p) (c n) -> p k c n", p=P, n=P)

        def group(n):
            return n // (NR // NG3) if n < NR else (n - NR) // (NPS // NG3)

        def classes(v, g, half=None):
            d = DIL[g]
            v = v[:, 0:NP].rearrange("p (c n) -> p n c", c=d)
            return v if half is None else v[:, half * 512 // d:(half + 1) * 512 // d, :]

        tokens = lambda v, g: v.rearrange("p (n c) -> p n c", c=DIL[g])
        with nc.Block() as block:

            @block.sync
            def _(sp):
                for dst, src in ((ident[:], T["k_ident"]), (rotp[:], T["k_rotp"]), (ada[:, 0:2], T["ada_d"][2, :, 0:2 * D].rearrange("c (a n) -> c a n", a=2)),
                                 (ada[:, 2:4], T["kva_d"].rearrange("c (a n) -> c a n", a=2)), (cos[:], T["k_cos"]),
                                 (sin[:], T["k_sin"]), (ctok[:], T["k_ctok"])):
                    sp.dma_start(dst, src).then_inc(s_ld, 16)
                sp.dma_start(x[:], T["x_in"][1].rearrange("(t p) n -> p t n", p=P)).then_inc(s_x, 16)
                sp.dma_start(wkv[:], T["w_kv"].rearrange("(k p) n -> p k n", p=P)).then_inc(s_ld, 16)
                for j in range(4):
                    sp.dma_start(wr[:, j], wv[:, :, j, :]).then_inc(s_wr[j], 16)
                for t in range(TT):
                    r = slice(t * P, t * P + P)
                    j = t % 2
                    sp.wait_ge(s_kvr, t + 1)
                    if t < TILES:
                        sp.dma_start(T["k_prompt"][r, :], kv[:, j, 0:256]).then_inc(s_kvs[j], 16)
                        sp.dma_start(T["v_prompt"][r, :], kv[:, j, 256:512]).then_inc(s_kvs[j], 16)
                        for g, d in enumerate(DIL):
                            dst = T["v_d"][g].rearrange("(c n) f -> n c f", c=d)[t * P // d:(t + 1) * P // d]
                            sp.dma_start(dst, kv[:, j, 256:512]).then_inc(s_kvs[j], 16)
                        sp.wait_ge(s_kn, t + 1)
                        sp.dma_start(T["k_d"][0, :, :, r].rearrange("h d n -> d h n"), kn[:, j]).then_inc(s_kns[j], 16)
                    else:
                        sp.dma_start(T["k_sample"], kv[0:NS, j, 0:256]).then_inc(s_kvs[j], 16)
                        sp.dma_start(T["v_sample"], kv[0:NS, j, 256:512]).then_inc(s_kvs[j], 16)
                for g in (1, 2):
                    sp.dma_start(T["k_d"][g].rearrange("h d n -> d h n"), kc[:, g - 1]).then_inc(s_kcs, 16)
                for n in range(4, NCH):
                    sp.wait_ge(s_q, n - 3)
                    sp.dma_start(wr[:, n % 4], wv[:, :, n, :]).then_inc(s_wr[n % 4], 16)

            @block.gpsimd
            def _(pool):
                for n in range(NCH):
                    pool.wait_ge(s_e, n + 1)
                    dst = T["qr_d"][n * P:(n + 1) * P, :] if n < NR else T["qp_d"][(n - NR) * P:(n - NR + 1) * P, :]
                    pool.dma_start(dst, ev[:, n % 2, 0:NP]).then_inc(s_evs[n % 2], 16)
                pool.wait_ge(s_qs, NCH // 4)
                pool.dma_start(T["qs_d"], qs[:]).then_inc(s_qd, 16)
                pool.wait_ge(s_qd, 16)
                pool.wait_ge(s_kcs, 32)
                pool.wait_ge(s_kvs[0], 16 * (5 * 4 + 2))
                pool.wait_ge(s_kvs[1], 16 * 5 * 4)
                for j in range(2):
                    pool.wait_ge(s_evs[j], 16 * NCH // 2)
                    pool.wait_ge(s_kns[j], 16 * TILES // 2)

            @block.vector
            def _(dve):
                link = Chain(dve, s_z)
                for a in range(2):
                    dve.wait_ge(s_mt, a + 1)
                    dve.tensor_copy(mod[:, 2 * a:2 * a + 2].rearrange("p a k c -> p (a k) c"),
                                    pm[:, a, 0:2 * KC * 16].rearrange("p (a c) -> p a c", c=16)[:, :, 0:NC]).then_inc(s_m, 1)
                dve.wait_ge(s_m, 2)
                for u in range(2 * KC):
                    k, half = divmod(u, 2)
                    dve.wait_ge(s_xt, u + 1)
                    for a in range(2):
                        ins = dve.tensor_scalar(hh[:, a, k, half * 512:half * 512 + 512], ps[u % 2][:, 0, :],
                                                mod[:, 2 * a + 1, k, NS:NC], mod[:, 2 * a, k, NS:NC], ALU.mult, ALU.add)
                    ins.then_inc(s_h, 1)
                dve.wait_ge(s_xt, 2 * KC + 1)
                v = pm[:, 0, 0:KC * NS].rearrange("p (k s) -> p k s", s=NS)
                for a in range(2):
                    hs = hh[:, a, :, NP:NT]
                    link(dve.tensor_tensor(hs, v, mod[:, 2 * a + 1, :, 0:NS], ALU.mult))
                    ins = dve.tensor_tensor(hs, hs, mod[:, 2 * a, :, 0:NS], ALU.add)
                ins.then_inc(s_h, 1)
                for t in range(TT):
                    r = P if t < TILES else NS
                    j = t % 2
                    dve.wait_ge(s_kve, t + 1)
                    kh = kv[0:r, j, 0:256].rearrange("p (h d) -> p h d", h=KVH)
                    a, b = kh[:, :, 0:8], kh[:, :, 8:16]
                    c = ctok[0:r, t, 0:1, :].broadcast_to([r, KVH, 8])
                    s = ctok[0:r, t, 1:2, :].broadcast_to([r, KVH, 8])
                    for i, (o, m) in enumerate(((a, c), (b, s), (b, c), (a, s))):
                        ins = dve.tensor_tensor(tmp[0:r, i], o, m, ALU.mult)
                    link(ins)
                    dve.tensor_tensor(a, tmp[0:r, 0], tmp[0:r, 1], ALU.subtract)
                    dve.tensor_tensor(b, tmp[0:r, 2], tmp[0:r, 3], ALU.add).then_inc(s_kvr, 1)
                    if t < TILES:
                        dve.wait_ge(s_kt, t + 1)
                        src = ps[j][0:HD, 1, :].rearrange("p (h n) -> p h n", h=KVH)
                        if t >= 2:
                            dve.wait_ge(s_kns[j], 16 * (t // 2))
                        dve.tensor_copy(kn[:, j], src)
                        for g in (1, 2):
                            d = DIL[g]
                            for hd in range(KVH):
                                ins = dve.tensor_copy(
                                    kc[:, g - 1, hd].rearrange("p (c n) -> p n c", c=d)[:, t * P // d:(t + 1) * P // d, :],
                                    src[:, hd].rearrange("p (n c) -> p n c", c=d))
                        ins.then_inc(s_kn, 1)
                for n in range(NR):
                    dve.wait_ge(s_raw, n + 1)
                    dve.tensor_tensor(t1[:], raw[:], cos[:], ALU.mult)
                    dve.wait_ge(s_rp, n + 1)
                    link(dve.tensor_tensor(t2[:, 0:NP].rearrange("p (s n) -> p s n", s=2), pm[:],
                                           sin[:, 0:NP].rearrange("p (s n) -> p s n", s=2), ALU.mult))
                    link(dve.tensor_tensor(t2[:, NP:NT], ps[n % 2][:, 2, 64:64 + NS], sin[:, NP:NT], ALU.mult))
                    if n >= 2:
                        dve.wait_ge(s_evs[n % 2], 16 * (n // 2))
                    g = group(n)
                    dve.tensor_tensor(classes(ev[:, n % 2], g), tokens(t1[:, 0:NP], g), tokens(t2[:, 0:NP], g), ALU.add)
                    dve.tensor_tensor(qsT[:, n], t1[:, NP:NT], t2[:, NP:NT], ALU.add).then_inc(s_e, 1)

            @block.tensor
            def _(pe):
                pe.wait_ge(s_ld, 16 * 8)
                for b in range(2):
                    for a in range(2):
                        for k in range(KC):
                            o = (a * KC + k) * 16
                            ins = pe.transpose(pm[:, b, o:o + NC], ada[:, 2 * b + a, k * P:(k + 1) * P], ident[0:NC, 0:NC])
                    ins.then_inc(s_mt, 1)
                pe.wait_ge(s_x, 16)
                for u in range(2 * KC):
                    k, half = divmod(u, 2)
                    if u >= 2:
                        pe.wait_ge(s_h, u - 1)
                    for t in range(4):
                        ins = pe.transpose(ps[u % 2][:, 0, t * P:(t + 1) * P], x[:, 4 * half + t, k * P:(k + 1) * P], ident[:])
                    ins.then_inc(s_xt, 1)
                pe.wait_ge(s_m, 1)
                for k in range(KC):
                    ins = pe.transpose(pm[:, 0, k * NS:(k + 1) * NS], x[0:NS, TILES, k * P:(k + 1) * P], ident[0:NS, 0:NS])
                ins.then_inc(s_xt, 1)
                pe.wait_ge(s_h, 2 * KC + 1)

                def k_transposes(t):
                    pe.wait_ge(s_kvr, t + 1)
                    if t >= 2:
                        pe.wait_ge(s_kn, t - 1)
                    for hd in range(KVH):
                        ins = pe.transpose(ps[t % 2][0:HD, 1, hd * P:(hd + 1) * P], kv[:, t % 2, hd * HD:(hd + 1) * HD], ident[:])
                    ins.then_inc(s_kt, 1)

                for t in range(TT):
                    r = P if t < TILES else NS
                    if t >= 2:
                        pe.wait_ge(s_kve, t - 1)
                    for k in range(KC):
                        ins = pe.matmul(pm[0:r, t % 2, :], hh[:, 1, k, t * P:t * P + r], wkv[:, k, :], start=(k == 0), stop=(k == KC - 1))
                    ins.then_inc(s_kvp, 1)
                    if t:
                        k_transposes(t - 1)
                pe.wait_ge(s_kn, TILES)
                pe.wait_ge(s_kve, TT)

                def product(n):
                    pe.wait_ge(s_wr[n % 4], 16 * (n // 4 + 1))
                    for k in range(KC):
                        for s, w in enumerate((512, 512, NS)):
                            ins = pe.matmul(ps[n % 2][:, s, 0:w], wr[:, n % 4, k, :], hh[:, 0, k, s * 512:s * 512 + w],
                                            start=(k == 0), stop=(k == KC - 1))
                    ins.then_inc(s_q, 1)

                def swap(n):
                    pe.wait_ge(s_raw, n + 1)
                    for dst, lo, w in ((pm[:, 0], 0, 512), (pm[:, 1], 512, 512), (ps[n % 2][:, 2, 64:64 + NS], NP, NS)):
                        ins = pe.matmul(dst, rotp[:], raw[:, lo:lo + w], start=True, stop=True)
                    ins.then_inc(s_rp, 1)

                for n in range(NCH):
                    if n >= 2:
                        pe.wait_ge(s_e, n - 1)
                    product(n)
                    if 1 <= n <= NR:
                        if n >= 2:
                            pe.wait_ge(s_e, n - 1)
                        swap(n - 1)
                for b in range(NCH // 4):
                    if b == 0:
                        pe.wait_ge(s_e, NCH)
                    if b >= 2:
                        pe.wait_ge(s_qs, b - 1)
                    for i in range(4):
                        ins = pe.transpose(pm[0:NS, b % 2, i * P:(i + 1) * P], qsT[:, 4 * b + i, :], ident[:])
                    ins.then_inc(s_qt, 1)

            @block.scalar
            def _(act):
                for t in range(TT):
                    r = P if t < TILES else NS
                    act.wait_ge(s_kvp, t + 1)
                    if t >= 2:
                        act.wait_ge(s_kvs[t % 2], 16 * 5 * (t // 2))
                        act.wait_ge(s_kt, t - 1)
                    act.activation(kv[0:r, t % 2, :], pm[0:r, t % 2, :], ACT.Copy).then_inc(s_kve, 1)
                for n in range(NR):
                    act.wait_ge(s_q, n + 1)
                    if n:
                        act.wait_ge(s_e, n)
                    act.activation(raw[:, 0:NP].rearrange("p (s n) -> p s n", s=2), ps[n % 2][:, 0:2, :], ACT.Copy)
                    act.activation(raw[:, NP:NT], ps[n % 2][:, 2, 0:NS], ACT.Copy).then_inc(s_raw, 1)
                for n in range(NR, NCH):
                    g = group(n)
                    act.wait_ge(s_q, n + 1)
                    if n == NR:
                        act.wait_ge(s_e, NR)
                    act.wait_ge(s_evs[n % 2], 16 * (n // 2))
                    act.activation(qsT[:, n], ps[n % 2][:, 2, 0:NS], ACT.Copy)
                    for half in range(2):
                        ins = act.activation(classes(ev[:, n % 2], g, half), tokens(ps[n % 2][:, half, :], g), ACT.Copy)
                    ins.then_inc(s_e, 1)
                for b in range(NCH // 4):
                    act.wait_ge(s_qt, b + 1)
                    act.activation(qs[:, b * 512:(b + 1) * 512], pm[0:NS, b % 2, :], ACT.Copy).then_inc(s_qs, 1)


def attend_units():
    out = []
    for g, d in enumerate(DIL):
        n = NP // d // P
        for b in range(TILES):
            before = n > 1 and b % n > 0
            out.append((g, b, 1 + before, 0 if before else (1 if n else 2)))
    return out


def phase_attend(nc, T):
    units = attend_units()
    U = len(units)
    with Pool_(nc, "att") as A:
        ident = A.sb("ident", [P, P])
        mk = A.sb("mk", [P, 3, 2 * P])
        q = A.sb("q", [HD, NG3, REP, NP])
        k = A.sb("k", [HD, NG3, NP])
        v = A.sb("v", [P, NG3, TILES, HD])
        S = A.sb("S", [P, 2, REP, 2 * P])
        PT = A.sb("PT", [P, 2, 2, REP * P])
        nm = A.sb("nm", [P, 2, REP])
        ml = A.sb("ml", [P, U, 2, REP])
        rl = A.sb("rl", [P, 2, REP])
        o = A.sb("o", [P, 4, REP * HD])
        ps_s = [A.ps(f"ps_s{j}", [P, REP, 2 * P]) for j in range(2)]
        ps_t = A.ps("ps_t", [P, 2, 512])
        ps_o = A.ps("ps_o", [P, 2, 512])
        s_nil = A.sem("waits_apart")
        s_k = A.sem("constants_loaded")
        s_qk = [A.sem(f"q_k_loaded{g}") for g in range(NG3)]
        s_v = [A.sem(f"v_loaded{g}") for g in range(NG3)]
        s_st = [A.sem(f"unit_stored{x}") for x in range(4)]
        s_ml = A.sem("sums_stored")
        slots = lambda first, *names: first + [x for u in range(U) for n in names
                                               for x in ([f"{n}{u}"] if n[0] in "tpro" else [f"{n}{u + 2}"] if u + 2 < U else [])]
        pe_ = Steps(A.sem("pe_steps"), slots(["s0", "s1"], "t", "s", "o"))
        dv_ = Steps(A.sem("dve_steps"), slots(["mask0", "max0", "neg0", "mask1", "max1", "neg1"], "pt", "rl", "mask", "max", "neg"))
        ac_ = Steps(A.sem("act_steps"), slots(["exp0", "exp1"], "o", "exp"))
        last = {g: max(u for u in range(U) if units[u][0] == g) for g in range(NG3)}

        def wait_back(eng, steps, name, u, back, h, apart=None):
            if u >= back:
                steps.wait(eng, f"{name}{u - back}", h, apart)
            else:
                steps.wait_before(eng, f"{name}{u - back + U}", h, apart)

        with nc.Block() as block:

            @block.sync
            def _(sp):
                sp.dma_start(mk[:], T["k_masks"].rearrange("m p n -> p m n")).then_inc(s_k, 16)
                sp.dma_start(ident[:], T["k_ident"]).then_inc(s_k, 16)
                for s in s_st:
                    sp.sem_inc(s, 16)
                sp.sem_inc(s_ml, 16)

                with sp.Fori(0, KVH) as h:
                    for u, (g, b, _, _) in enumerate(units):
                        ac_.wait(sp, f"o{u}", h, apart=s_nil)
                        sp.dma_start(T["o_d"][g * NP + b * P:g * NP + (b + 1) * P, ds(h * (REP * HD), REP * HD)], o[:, u % 4]).then_inc(s_st[u % 4], 16)
                    sp.dma_start(T["ml_d"].rearrange("(u p) x -> p u x", p=P)[:, :, ds(h * (2 * REP), 2 * REP)],
                                 ml[:].rearrange("p u a r -> p u (a r)")).then_inc(s_ml, 16)
                for s in s_st:
                    sp.wait_ge(s, 16 * (U // 4 * KVH + 1))
                sp.wait_ge(s_ml, 16 * (KVH + 1))

            @block.gpsimd
            def _(pool):
                def load(h, g):
                    if not isinstance(h, int):
                        pe_.wait_before(pool, f"s{last[g]}", h, apart=s_nil)
                    for d, t, at in ((ROT, "qr_d", 0), (PASS, "qp_d", ROT)):
                        pool.dma_start(q[at:at + d, g], T[t].rearrange("(g x) n -> g x n", g=NG3)[g][ds(h * (REP * d), REP * d), :]
                                       .rearrange("(r d) n -> d r n", r=REP)).then_inc(s_qk[g], 16)
                    pool.dma_start(k[:, g], T["k_d"][g].rearrange("h d n -> (h d) n")[ds(h * HD, HD), :]).then_inc(s_qk[g], 16)
                    if not isinstance(h, int):
                        pe_.wait_before(pool, f"o{last[g]}", h, apart=s_nil)
                    pool.dma_start(v[:, g], T["v_d"][g].rearrange("(b p) f -> p b f", p=P)[:, :, ds(h * HD, HD)]).then_inc(s_v[g], 16)

                for g in range(NG3):
                    load(0, g)
                with pool.Fori(1, KVH) as h:
                    for g in range(NG3):
                        load(h, g)
                for g in range(NG3):
                    pool.wait_ge(s_qk[g], 48 * KVH)
                    pool.wait_ge(s_v[g], 16 * KVH)

            @block.vector
            def _(dve):
                dv_.open(dve)
                dve.wait_ge(s_k, 32)
                with dve.Fori(0, KVH) as h:
                    def soft(u):
                        _, _, nk, m = units[u]
                        j, W = u % 2, nk * P
                        x = S[:, j, :, 0:W]
                        pe_.wait(dve, f"s{u}", h)
                        wait_back(dve, pe_, "t", u, 2, h)
                        dv_.step(f"mask{u}", dve.scalar_tensor_tensor(
                            out=x, in0=ps_s[j][:, :, 0:W], scalar=SCALE,
                            in1=mk[:, m:m + 1, 2 * P - W:2 * P].broadcast_to([P, REP, W]), op0=ALU.mult, op1=ALU.add))
                        dv_.wait(dve, f"mask{u}", h)
                        if u == 0:
                            dve.wait_ge(s_ml, h * 16 + 16)
                        dv_.step(f"max{u}", dve.tensor_reduce(ml[:, u, 0], x, AX, ALU.max))
                        dv_.wait(dve, f"max{u}", h)
                        wait_back(dve, ac_, "exp", u, 2, h)
                        dv_.step(f"neg{u}", dve.tensor_scalar(nm[:, j], ml[:, u, 0], -1.0, None, ALU.mult))

                    soft(0)
                    soft(1)
                    for u in range(U):
                        nk = units[u][2]
                        pe_.wait(dve, f"t{u}", h)
                        dv_.step(f"pt{u}", dve.tensor_copy(PT[:, u % 2, 0:nk], ps_t[:, 0:nk]))
                        ac_.wait(dve, f"exp{u}", h)
                        wait_back(dve, ac_, "o", u, 2, h)
                        dv_.step(f"rl{u}", dve.reciprocal(rl[:, u % 2], ml[:, u, 1]))
                        if u + 2 < U:
                            soft(u + 2)

            @block.scalar
            def _(act):
                ac_.open(act)
                with act.Fori(0, KVH) as h:
                    def exp(u):
                        j, W = u % 2, units[u][2] * P
                        dv_.wait(act, f"neg{u}", h)
                        for r in range(REP):
                            x = S[:, j, r, 0:W]
                            ins = act.activation(x, x, ACT.Exp, bias=nm[:, j, r:r + 1], accum_out=ml[:, u, 1, r:r + 1])
                        ac_.step(f"exp{u}", ins)

                    exp(0)
                    exp(1)
                    for u in range(U):
                        dv_.wait(act, f"rl{u}", h)
                        act.wait_ge(s_st[u % 4], h * (16 * U // 4) + 16 * (u // 4) + 16)
                        pe_.wait(act, f"o{u}", h)
                        for r in range(REP):
                            c = slice(r * HD, (r + 1) * HD)
                            ins = act.activation(o[:, u % 4, c], ps_o[:, u % 2, c], ACT.Copy, scale=rl[:, u % 2, r:r + 1])
                        ac_.step(f"o{u}", ins)
                        if u + 2 < U:
                            exp(u + 2)

            @block.tensor
            def _(pe):
                pe_.open(pe)
                pe.wait_ge(s_k, 32)
                with pe.Fori(0, KVH) as h:
                    def scores(u):
                        g, b, nk, _ = units[u]
                        pe.wait_ge(s_qk[g], h * 48 + 48)
                        wait_back(pe, dv_, "mask", u, 2, h, apart=s_nil)
                        for r in range(REP):
                            ins = pe.matmul(ps_s[u % 2][:, r, 0:nk * P], q[:, g, r, b * P:(b + 1) * P], k[:, g, (b + 1 - nk) * P:(b + 1) * P],
                                            start=True, stop=True)
                        pe_.step(f"s{u}", ins)

                    scores(0)
                    scores(1)
                    for u in range(U):
                        g, b, nk, _ = units[u]
                        ac_.wait(pe, f"exp{u}", h, apart=s_nil)
                        wait_back(pe, dv_, "pt", u, 1, h, apart=s_nil)
                        for x in range(nk):
                            for r in range(REP):
                                ins = pe.transpose(ps_t[:, x, r * P:(r + 1) * P], S[:, u % 2, r, x * P:(x + 1) * P], ident[:])
                        pe_.step(f"t{u}", ins)
                        if u + 2 < U:
                            scores(u + 2)
                        dv_.wait(pe, f"pt{u}", h, apart=s_nil)
                        pe.wait_ge(s_v[g], h * 16 + 16)
                        wait_back(pe, ac_, "o", u, 2, h, apart=s_nil)
                        for r in range(REP):
                            for x in range(nk):
                                ins = pe.matmul(ps_o[:, u % 2, r * HD:(r + 1) * HD], PT[:, u % 2, x, r * P:(r + 1) * P],
                                                v[:, g, b + 1 - nk + x, :], start=(x == 0), stop=(x == nk - 1))
                        pe_.step(f"o{u}", ins)


def attn_consts():
    one = np.float32
    out = {}
    rp = np.zeros((P, P), one)
    for i in range(P):
        b, r = divmod(i, ROT)
        if r < 8:
            rp[b * ROT + r + 8, i] = -1.0
        else:
            rp[b * ROT + r - 8, i] = 1.0
    out["k_rotp"] = rp
    half = ROT // 2
    inv = (one(500000.0) ** (-np.arange(half, dtype=one) * one(2.0) / one(ROT))).astype(one)
    pos = np.concatenate([np.arange(NP), np.full(NS, PAST)]).astype(one)
    ang = (pos[:, None] * inv[None, :]).astype(one)
    c, s = np.cos(ang).astype(one), np.sin(ang).astype(one)
    out["k_cos"] = np.ascontiguousarray(np.tile(c.T, (P // half, 1)))
    out["k_sin"] = np.ascontiguousarray(np.tile(s.T, (P // half, 1)))
    ct = np.zeros((NTP, 2, half), one)
    ct[:NT, 0], ct[:NT, 1] = c, s
    out["k_ctok"] = np.ascontiguousarray(ct.reshape(TT, P, 2, half).transpose(1, 0, 2, 3))
    i = np.arange(P)
    m = np.full((3, P, 2 * P), NEG, one)
    m[0, :, 0:P][i[None, :] >= i[:, None]] = 0.0
    causal = i[None, :] <= i[:, None]
    m[0, :, P:][causal] = 0.0
    m[1, :, P:][causal] = 0.0
    m[2, :, P:][causal & (i[None, :] // 64 == i[:, None] // 64)] = 0.0
    out["k_masks"] = m
    return out


def phase_attend_sum(nc, T, fetch):
    with Pool_(nc, "asum") as A:
        ident = A.sb("ident", [P, P])
        O = A.sb("O", [P, 2, NG3, D])
        ml = A.sb("ml", [P, 2, NG3, KVH, 2, REP])
        L = A.sb("L", [P, 2, NG3, H])
        mx = A.sb("mx", [P, 2, H])
        zT = A.sb("zT", [P, 2, KC * P])
        ps = [A.ps(f"ps{j}", [P, 2, 512]) for j in range(2)]
        s_nil = A.sem("waits_apart")
        s_k = A.sem("constants_loaded")
        s_ld = [A.sem(f"tile_loaded{j}") for j in range(2)]
        s_st = [A.sem(f"z_stored{j}") for j in range(2)]
        both = lambda *names: [f"{x}{j}" for j in range(2) for x in names]
        dv_ = Steps(A.sem("dve_steps"), both("lse", "mx", "sub", "sum", "rcp", "w", "m0", "m2", "a1", "a2"))
        ac_ = Steps(A.sem("act_steps"), both("ln", "exp", "zT"))
        po_ = Steps(A.sem("pool_steps"), both("m1"))
        pe_ = Steps(A.sem("pe_steps"), both("t"))
        bc = lambda x, n=HD: x.rearrange("p (h o) -> p h o", o=1).broadcast_to([P, x.shape[1], n])
        heads = lambda x: x.rearrange("p (h d) -> p h d", h=H)
        over = lambda x: x.rearrange("p (o h) -> p o h", o=1).broadcast_to([P, NG3, H])
        with nc.Block() as block:

            @block.sync
            def _(sp):
                sp.dma_start(ident[:], T["k_ident"]).then_inc(s_k, 16)
                with sp.Fori(0, TILES // 2) as i:
                    for j in range(2):
                        pe_.wait_before(sp, f"t{j}", i, apart=s_nil)
                        for g, d in enumerate(DIL):
                            n = P // d
                            for src, dst in ((T["o_d"], O[:, j, g, :]), (T["ml_d"], ml[:, j, g].rearrange("p h a r -> p (h a r)"))):
                                src = src[g * NP:(g + 1) * NP, :].rearrange("(c n) f -> n c f", c=d)
                                sp.dma_start(dst, src[ds(i * (2 * n) + j * n, n)]).then_inc(s_ld[j], 16)
                fetch(sp)

            @block.gpsimd
            def _(pool):
                po_.open(pool)
                with pool.Fori(0, TILES // 2) as i:
                    for j in range(2):
                        pool.wait_ge(s_ld[j], i * 96 + 96)
                        dv_.wait(pool, f"w{j}", i, apart=s_nil)
                        o = heads(O[:, j, 1])
                        po_.step(f"m1{j}", pool.tensor_tensor(o, o, bc(L[:, j, 1]), ALU.mult))

            @block.scalar
            def _(act):
                ac_.open(act)
                for s in s_st:
                    act.sem_inc(s, 16)
                with act.Fori(0, TILES // 2) as i:
                    for j in range(2):
                        act.wait_ge(s_ld[j], i * 96 + 96)
                        (dv_.wait_before)(act, f"m2{j}", i)
                        po_.wait_before(act, f"m1{j}", i)
                        ac_.step(f"ln{j}", act.activation(L[:, j].rearrange("p g (h r) -> p g h r", h=KVH), ml[:, j, :, :, 1, :], ACT.Ln))
                        dv_.wait(act, f"sub{j}", i)
                        ac_.step(f"exp{j}", act.activation(L[:, j], L[:, j], ACT.Exp))
                        pe_.wait(act, f"t{j}", i)
                        act.wait_ge(s_st[j], i * 16 + 16)
                        ac_.step(f"zT{j}", act.activation(zT[:, j].rearrange("p (b n) -> p b n", b=2), ps[j][:], ACT.Copy))
                        ac_.wait(act, f"zT{j}", i, apart=s_nil)
                        act.dma_start(T["z_d"].rearrange("(k p) n -> p k n", p=P)[:, :, ds(i * (2 * P) + j * P, P)],
                                      zT[:, j].rearrange("p (k n) -> p k n", k=KC)).then_inc(s_st[j], 16)
                for j in range(2):
                    act.wait_ge(s_st[j], 16 * TILES // 2 + 16)

            @block.vector
            def _(dve):
                dv_.open(dve)
                with dve.Fori(0, TILES // 2) as i:
                    for j in range(2):
                        def op(name, ins, then=True):
                            dv_.step(f"{name}{j}", ins)
                            if then:
                                dv_.wait(dve, f"{name}{j}", i)

                        Lj = L[:, j]
                        L4 = Lj.rearrange("p g (h r) -> p g h r", h=KVH)
                        ac_.wait(dve, f"ln{j}", i)
                        dve.wait_ge(s_ld[j], i * 96 + 96)
                        op("lse", dve.tensor_tensor(L4, L4, ml[:, j, :, :, 0, :], ALU.add))
                        op("mx", dve.tensor_reduce(mx[:, j], Lj.rearrange("p g h -> p h g"), AX, ALU.max))
                        op("sub", dve.tensor_tensor(Lj, Lj, over(mx[:, j]), ALU.subtract))
                        ac_.wait(dve, f"exp{j}", i)
                        op("sum", dve.tensor_reduce(mx[:, j], Lj.rearrange("p g h -> p h g"), AX, ALU.add))
                        op("rcp", dve.reciprocal(mx[:, j], mx[:, j]))
                        op("w", dve.tensor_tensor(Lj, Lj, over(mx[:, j]), ALU.mult))
                        for g in (0, 2):
                            o = heads(O[:, j, g])
                            op(f"m{g}", dve.tensor_tensor(o, o, bc(L[:, j, g]), ALU.mult), g == 2)
                        op("a1", dve.tensor_tensor(O[:, j, 0], O[:, j, 0], O[:, j, 2], ALU.add))
                        po_.wait(dve, f"m1{j}", i)
                        op("a2", dve.tensor_tensor(O[:, j, 0], O[:, j, 0], O[:, j, 1], ALU.add), False)

            @block.tensor
            def _(pe):
                pe_.open(pe)
                pe.wait_ge(s_k, 16)
                with pe.Fori(0, TILES // 2) as i:
                    for j in range(2):
                        dv_.wait(pe, f"a2{j}", i, apart=s_nil)
                        ac_.wait_before(pe, f"zT{j}", i, apart=s_nil)
                        for k in range(KC):
                            ins = pe.transpose(ps[j][:, k // 4, (k % 4) * P:(k % 4 + 1) * P], O[:, j, 0, k * P:(k + 1) * P], ident[:])
                        pe_.step(f"t{j}", ins)


def phase_attend_ends(nc, T):
    NK = [PAST // d + 1 if PAST // d < 128 else 129 for d in DIL]
    OFF = [sum(NK[:g]) for g in range(NG3)]
    ALL = sum(NK)
    GR = [slice(OFF[g], OFF[g] + NK[g]) for g in range(NG3)]
    with Pool_(nc, "satt") as A:
        ident = A.sb("ident", [P, P])
        q = A.sb("q", [P, NG3, HD])
        K = A.sb("K", [P, ALL, HD])
        V = A.sb("V", [P, ALL, HD])
        s = A.sb("s", [P, ALL])
        m = A.sb("m", [P, NG3])
        nm = A.sb("nm", [P, NG3])
        l = A.sb("l", [P, NG3])
        ls = A.sb("ls", [P, NG3])
        mx = A.sb("mx", [P, 4])
        w = A.sb("w", [P, NG3])
        rl = A.sb("rl", [P, NG3])
        z = A.sb("z", [P, HD])
        zr = A.sb("zr", [NS, D])
        zT = A.sb("zT", [P, KC, NS])
        ps = A.ps("ps", [P, KC, NS])
        s_q = A.sem("q_loaded")
        s_K = A.sem("keys_loaded")
        s_V = A.sem("values_loaded")
        s_d = A.sem("dve_steps")
        s_nm = A.sem("stage_ended")
        s_a = A.sem("act_steps")
        s_z = A.sem("z_stored")
        s_zl = A.sem("z_rows")
        s_t = A.sem("z_transposed")
        s_c = A.sem("zT_ready")
        s_o = A.sem("zT_stored")

        def rows(eng, dst, cache, new, sem):
            for g, d in enumerate(DIL):
                n = NK[g] - 1
                src = T[cache].rearrange("x (k s) d -> x k s d", s=d)[:, PAST // d - n:, 0, :]
                for r in range(REP):
                    eng.dma_start(dst[r::REP, OFF[g]:OFF[g] + n], src).then_inc(sem, 16)
                    eng.dma_start(dst[r::REP, OFF[g] + n],
                                  T[new].rearrange("b (h d) -> (b h) d", h=KVH)).then_inc(sem, 16)

        def fetch(sp):
            sp.dma_start(ident[:], T["k_ident"]).then_inc(s_q, 16)
            for b in range(NS):
                for at, d, base in ((0, ROT, 0), (ROT, PASS, QR)):
                    sp.dma_start(q[b * H:(b + 1) * H, :, at:at + d],
                                 T["qs_d"][b, base:base + NG3 * H * d].rearrange("(g h d) -> h g d", g=NG3, h=H)).then_inc(s_q, 16)
            rows(sp, K, "cache_k", "k_sample", s_K)
            rows(sp, V, "cache_v", "v_sample", s_V)

        phase_attend_sum(nc, T, fetch)
        with nc.Block() as block:

            @block.sync
            def _(sp):
                sp.wait_ge(s_nm, 3)
                sp.dma_start(T["zs_d"].rearrange("b (h d) -> (b h) d", h=H), z[:]).then_inc(s_z, 16)
                sp.wait_ge(s_z, 16)
                sp.dma_start(zr[:], T["zs_d"]).then_inc(s_zl, 16)
                sp.wait_ge(s_c, 1)
                sp.dma_start(T["z_d"].rearrange("(c p) n -> p c n", p=P)[:, :, NP:NT], zT[:]).then_inc(s_o, 16)
                sp.wait_ge(s_o, 16)

            @block.scalar
            def _(act):
                act.wait_ge(s_nm, 1)
                for g in range(NG3):
                    act.activation(s[:, GR[g]], s[:, GR[g]], ACT.Exp, bias=nm[:, g:g + 1], accum_out=l[:, g:g + 1]).then_inc(s_a, 1)
                act.wait_ge(s_a, 3)
                act.activation(ls[:], l[:], ACT.Ln).then_inc(s_a, 1)
                act.wait_ge(s_nm, 2)
                act.activation(w[:], ls[:], ACT.Exp).then_inc(s_a, 1)

            @block.vector
            def _(dve):
                link = Chain(dve, s_d)
                dve.wait_ge(s_q, 16 * (1 + 2 * NS))
                dve.wait_ge(s_K, 16 * 2 * REP * NG3)
                for g in range(NG3):
                    link(dve.tensor_tensor(K[:, GR[g]], K[:, GR[g]], q[:, g:g + 1].broadcast_to([P, NK[g], HD]), ALU.mult))
                link(dve.tensor_reduce(s[:], K[:], AX, ALU.add))
                link(dve.tensor_scalar(s[:], s[:], SCALE, None, ALU.mult))
                for g in range(NG3):
                    ins = dve.tensor_reduce(m[:, g:g + 1], s[:, GR[g]], AX, ALU.max)
                    link(ins)
                dve.tensor_scalar(nm[:], m[:], -1.0, None, ALU.mult).then_inc(s_nm, 1)
                dve.wait_ge(s_a, 4)
                link(dve.tensor_tensor(ls[:], ls[:], m[:], ALU.add))
                link(dve.tensor_reduce(mx[:, 0:1], ls[:], AX, ALU.max))
                dve.tensor_scalar(ls[:], ls[:], mx[:, 0:1], None, ALU.subtract).then_inc(s_nm, 1)
                link(dve.reciprocal(rl[:], l[:]))
                dve.wait_ge(s_a, 5)
                link(dve.tensor_reduce(mx[:, 1:2], w[:], AX, ALU.add))
                link(dve.reciprocal(mx[:, 2:3], mx[:, 1:2]))
                link(dve.tensor_scalar(w[:], w[:], mx[:, 2:3], None, ALU.mult))
                link(dve.tensor_tensor(w[:], w[:], rl[:], ALU.mult))
                for g in range(NG3):
                    link(dve.tensor_scalar(s[:, GR[g]], s[:, GR[g]], w[:, g:g + 1], None, ALU.mult))
                dve.wait_ge(s_V, 16 * 2 * REP * NG3)
                link(dve.tensor_tensor(V[:], V[:], s[:].rearrange("p (k o) -> p k o", o=1).broadcast_to([P, ALL, HD]), ALU.mult))
                dve.tensor_reduce(z[:], V[:].rearrange("p k d -> p d k"), AX, ALU.add).then_inc(s_nm, 1)
                dve.wait_ge(s_t, 1)
                dve.tensor_copy(zT[:], ps[:]).then_inc(s_c, 1)

            @block.tensor
            def _(pe):
                pe.wait_ge(s_q, 16 * (1 + 2 * NS))
                pe.wait_ge(s_zl, 16)
                for k in range(KC):
                    ins = pe.transpose(ps[:, k, :], zr[:, k * P:(k + 1) * P], ident[0:NS, 0:NS])
                ins.then_inc(s_t, 1)


SCRATCH = {
    "ada_d": (4, NC, 3 * D), "kva_d": (NC, 2 * D), "x0_d": (NTP, D), "x2_d": (NTP, D),
    "proj_d": (6, D, NT), "bonus_d": (D, NT), "sv_d": (6, NS, D), "y_d": (D, NT), "ys_d": (NS, D),
    "z_d": (D, ZC), "x1_d": (NTP, D), "xm_d": (NTP, D), "ysl_d": ((NBLK + 1) * P, D),
    "qr_d": (QR, NP), "qp_d": (QP, NP), "qs_d": (NS, QR + QP), "k_d": (NG3, KVH, HD, NP), "v_d": (NG3, NP, KVH * HD),
    "o_d": (NG3 * NP, D), "ml_d": (NG3 * NP, 2 * H), "zs_d": (NS, D),
}
OUTPUTS = [
    ("y_prompt", (NP, D), (1, NP, D)), ("y_sample", (NS, D), (NS, 1, D)),
    ("wkv_prompt", (H, HD, HD), (1, 1, H, HD, HD)), ("shift_prompt", (D,), (1, 1, D)),
    ("k_prompt", (NP, KVH * HD), (1, NP, KVH, HD)), ("v_prompt", (NP, KVH * HD), (1, NP, KVH, HD)),
    ("wkv_sample", (NS * H, HD, HD), (1, NS, H, HD, HD)), ("shift_sample", (NS, D), (1, NS, D)),
    ("k_sample", (NS, KVH * HD), (NS, 1, KVH, HD)), ("v_sample", (NS, KVH * HD), (NS, 1, KVH, HD)),
]


def yoco_step(nc, T):
    for name, shape in SCRATCH.items():
        T[name] = nc.dram_tensor("t_" + name, shape, F32, kind="Internal").ap()
    for name, shape, dt in (("table_d", ((NBLK + 2) * P, 1), I32), ("slot_d", (P, 2 * TT), I32),
                            ("gate_d", (P, 2 * TT), F32), ("blk_d", (1, 2 + NBLK), I32)):
        T[name] = [nc.dram_tensor(f"t_{name}{i}", shape, dt, kind="Internal").ap() for i in range(2)]
    T["x_in"] = [T["x0_d"], T["x2_d"]]
    T["w_o"] = [T["rwkv_w_o"], T["w_o_attn"]]
    phase_ada(nc, T)
    phase_mix(nc, T)
    phase_wkv(nc, T)
    phase_sample(nc, T)
    phase_gn(nc, T)
    phase_post(nc, T, 0)
    phase_moe(nc, T, 0)
    phase_combine(nc, T, 0)
    phase_qkv(nc, T)
    phase_attend(nc, T)
    phase_attend_ends(nc, T)
    phase_post(nc, T, 1)
    phase_moe(nc, T, 1)
    phase_combine(nc, T, 1)


def laid_out(inp):
    f = lambda name: np.asarray(inp[name])
    chunks = lambda a: a.reshape(KC, P)
    vec = lambda name: chunks(f(name).reshape(D))
    out = {"x_prompt": f("x_prompt")[0], "x_sample": f("x_sample")[:, 0], "state_wkv": f("state_wkv").reshape(NS * H, HD, HD),
           "state_shift": f("state_shift")[0], "c_prompt": f("c_prompt"), "c_sample": f("c_sample")}
    for name in ("cache_k", "cache_v"):
        out[name] = f(name).transpose(0, 2, 1, 3).reshape(NS * KVH, PAST, HD)
    for name in ("ada_w", "ada_b", "rwkv_w_rkv", "w_kv", "kv_ada_w", "router_w", "moe_w_in", "moe_w_out"):
        out[name] = f(name)
    out["kv_ada_b"] = f("kv_ada_b")[None]
    out["router_b"] = f("router_b")[None]
    for name in ("rwkv_w1", "rwkv_w2", "rwkv_a1", "rwkv_a2", "rwkv_g1", "rwkv_g2", "rwkv_w_o", "w_o_attn"):
        out[name] = f(name)[0]
    out["ln_gb"] = np.stack([f("ln_g").reshape(4, D), f("ln_b").reshape(4, D)], 1)
    out["mu_c"] = f("rwkv_mu").reshape(6, KC, P).transpose(2, 0, 1)
    out["wkv_par"] = np.stack([vec("rwkv_" + n) for n in ("w0", "a0", "k_k", "k_a", "r_k")], 2)
    out["gn_par"] = np.stack([vec("rwkv_lnx_g"), vec("rwkv_lnx_b")], 0).transpose(2, 0, 1)
    wq = f("w_q").reshape(D, NG3 * H, HD)
    out["w_q"] = np.concatenate([wq[:, :, :ROT].reshape(D, QR), wq[:, :, ROT:].reshape(D, QP)], 1)
    return out


def kernel(**inputs):
    import concourse.bacc as _bacc
    from concourse.bass_utils import run_bass_kernel_spmd as _run

    nc = _bacc.Bacc("TRN2", target_bir_lowering=False, num_devices=1)
    arrays, T = {}, {}
    for name, a in {**laid_out(inputs), **wkv_consts(), **post_consts(), **attn_consts()}.items():
        a = np.ascontiguousarray(a)
        arrays[f"in_{name}_dram"] = a
        T[name] = nc.dram_tensor(f"in_{name}_dram", a.shape, mybir.dt.from_np(a.dtype), kind="ExternalInput").ap()
    for i, (name, shape, _) in enumerate(OUTPUTS):
        T[name] = nc.dram_tensor(f"out_{i}_dram", shape, F32, kind="ExternalOutput").ap()
    yoco_step(nc, T)
    nc.compile()
    r = _run(nc, [arrays], core_ids=[0])
    return tuple(r.results[0][f"out_{i}_dram"].reshape(shape) for i, (_, _, shape) in enumerate(OUTPUTS))
```
